# Optimizing a Trainium2 kernel written in Bass

```python
import math
import jax, jax.numpy as jnp
from jax import lax
import numpy as np

D_MODEL = 1024
BATCH = 1
SEQ = 512
DEPTH = 2
DEC_BATCH = 8
DEC_SEQ = 8
PAST_LEN = 1024
PAGE_SIZE = 128

LRU_WIDTH = 256
LRU_BLOCKS = 4
LRU_BW = LRU_WIDTH // LRU_BLOCKS
CONV_WIDTH = 4
LRU_C = 8.0
MLA_HEADS = 8
Q_RANK = 256
KV_RANK = 128
QK_NOPE = 64
QK_ROPE = 32
V_HEAD = 64
ROPE_THETA = 10000.0
Q_BLOCK = 128
GLA_HEADS = 4
GLA_DK = 32
GLA_DV = 64
GLA_GATE_RANK = 16
GLA_TAU = 16.0
GLA_CHUNK = 16
MLA_WIDTH = MLA_HEADS * V_HEAD
GLA_WIDTH = GLA_HEADS * GLA_DV
MIX_WIDTH = LRU_WIDTH + MLA_WIDTH + GLA_WIDTH
IN_SIZES = (LRU_WIDTH, LRU_WIDTH, Q_RANK, KV_RANK, QK_ROPE,
            GLA_HEADS * GLA_DK, GLA_HEADS * GLA_DK, GLA_WIDTH, GLA_GATE_RANK, GLA_WIDTH)
IN_COLS = sum(IN_SIZES)
N_GROUPS = 4
EXPERTS_PER_GROUP = 8
N_EXPERTS = N_GROUPS * EXPERTS_PER_GROUP
TOP_K = 2
D_EXPERT = 256
EPS = 1e-6

kernel_name = 'hymba_rglru_mla_gla_hmoe_step'

F32 = jnp.float32

def rmsnorm(x, g):
    xf = x.astype(F32)
    y = xf * lax.rsqrt(jnp.mean(xf * xf, axis=-1, keepdims=True) + EPS)
    return (y * g.astype(F32)).astype(x.dtype)

def rope(x, pos):
    half = x.shape[-1] // 2
    inv = ROPE_THETA ** (-jnp.arange(half, dtype=F32) / half)
    ang = pos[:, None] * inv
    shape = (1, pos.shape[0]) + (1,) * (x.ndim - 3) + (half,)
    cos = jnp.cos(ang).reshape(shape)
    sin = jnp.sin(ang).reshape(shape)
    x1, x2 = x[..., :half], x[..., half:]
    return jnp.concatenate([x1 * cos - x2 * sin, x1 * sin + x2 * cos], axis=-1).astype(x.dtype)

def causal_conv(x, buf, w, b):
    S = x.shape[1]
    xp = jnp.concatenate([buf.astype(x.dtype), x], axis=1)
    y = b
    for k in range(CONV_WIDTH):
        y = y + w[k] * xp[:, k:k + S]
    return y, xp[:, -(CONV_WIDTH - 1):]

def rg_lru(x, h0, wa, ba, wi, bi, lam):
    B, S, C = x.shape
    xf = x.astype(F32)
    xb = xf.reshape(B, S, LRU_BLOCKS, LRU_BW)
    r = jax.nn.sigmoid(jnp.einsum('bsnc,ncd->bsnd', xb, wa.astype(F32)).reshape(B, S, C) + ba)
    i = jax.nn.sigmoid(jnp.einsum('bsnc,ncd->bsnd', xb, wi.astype(F32)).reshape(B, S, C) + bi)
    log_a = -LRU_C * r * jax.nn.softplus(-lam.astype(F32))
    a = jnp.exp(log_a)
    u = jnp.sqrt(-jnp.expm1(2.0 * log_a)) * (i * xf)

    def combine(left, right):
        a1, b1 = left
        a2, b2 = right
        return a1 * a2, a2 * b1 + b2

    a_cum, b_cum = lax.associative_scan(combine, (a, u), axis=1)
    h = a_cum * h0.astype(F32)[:, None] + b_cum
    return h, h[:, -1]

def mla_attend(q_abs, q_pe, ckv, kpe, offset):
    B, Sq, H, R = q_abs.shape
    Sk = ckv.shape[1]
    blk = math.gcd(Q_BLOCK, Sq)
    nb = Sq // blk
    scale = (QK_NOPE + QK_ROPE) ** -0.5
    k_pos = jnp.arange(Sk)

    def one_block(args):
        qa, qp, qpos = args
        s = (jnp.einsum('bqhr,bkr->bhqk', qa, ckv) + jnp.einsum('bqhr,bkr->bhqk', qp, kpe)).astype(F32) * scale
        s = jnp.where(k_pos[None, :] <= qpos[:, None], s, -jnp.inf)
        p = jax.nn.softmax(s, axis=-1).astype(ckv.dtype)
        return jnp.einsum('bhqk,bkr->bqhr', p, ckv)

    qa_b = q_abs.reshape(B, nb, blk, H, R).transpose(1, 0, 2, 3, 4)
    qp_b = q_pe.reshape(B, nb, blk, H, QK_ROPE).transpose(1, 0, 2, 3, 4)
    qpos_b = (offset + jnp.arange(Sq)).reshape(nb, blk)
    o = lax.map(one_block, (qa_b, qp_b, qpos_b))
    return o.transpose(1, 0, 2, 3, 4).reshape(B, Sq, H, R)

def gla_scan(q, k, v, log_alpha, s0):
    B, S, H, _ = q.shape
    C = math.gcd(GLA_CHUNK, S)
    N = S // C

    def to_chunks(t):
        return t.astype(F32).reshape(B, N, C, H, t.shape[-1]).transpose(1, 0, 3, 2, 4)

    qc, kc, vc, gc = to_chunks(q), to_chunks(k), to_chunks(v), to_chunks(log_alpha)
    causal = jnp.tril(jnp.ones((C, C), dtype=bool))[:, :, None]

    def step(st, inp):
        qi, ki, vi, gi = inp
        cum = jnp.cumsum(gi, axis=2)
        o_inter = jnp.einsum('bhtd,bhde->bhte', qi * jnp.exp(cum), st)
        diff = cum[:, :, :, None, :] - cum[:, :, None, :, :]
        decay = jnp.exp(jnp.where(causal, diff, -jnp.inf))
        att = jnp.einsum('bhtd,bhsd,bhtsd->bhts', qi, ki, decay)
        o = o_inter + jnp.einsum('bhts,bhse->bhte', att, vi)
        last = cum[:, :, -1:, :]
        k_dec = ki * jnp.exp(last - cum)
        st_new = jnp.exp(last[:, :, 0, :])[..., None] * st + jnp.einsum('bhsd,bhse->bhde', k_dec, vi)
        return st_new, o

    s_fin, o = lax.scan(step, s0.astype(F32), (qc, kc, vc, gc))
    return o.transpose(1, 0, 3, 2, 4).reshape(B, S, H, GLA_DV), s_fin

def token_mixers(hn, past_ckv, past_kpe, conv_buf, lru_h0, gla_s0, lw):
    B, S, _ = hn.shape
    offset = 0 if past_ckv is None else past_ckv.shape[1]
    pos = offset + jnp.arange(S, dtype=F32)
    z = hn @ lw['w_in']
    x_lru, y_lru, c_q, c_kv, k_pe, g_q, g_k, g_v, g_a, g_o = jnp.split(
        z, list(np.cumsum(IN_SIZES)[:-1]), axis=-1)

    xc, conv_new = causal_conv(x_lru, conv_buf, lw['conv_w'], lw['conv_b'])
    h, lru_new = rg_lru(xc, lru_h0, lw['lru_wa'], lw['lru_ba'], lw['lru_wi'], lw['lru_bi'], lw['lru_lambda'])
    out_a = h * jax.nn.gelu(y_lru.astype(F32))

    q = (rmsnorm(c_q, lw['q_norm_g']) @ lw['w_uq']).reshape(B, S, MLA_HEADS, QK_NOPE + QK_ROPE)
    q_nope, q_pe = q[..., :QK_NOPE], rope(q[..., QK_NOPE:], pos)
    q_abs = jnp.einsum('bshn,rhn->bshr', q_nope, lw['w_uk'])
    ckv_new = rmsnorm(c_kv, lw['kv_norm_g'])
    kpe_new = rope(k_pe, pos)
    if past_ckv is None:
        ckv_all, kpe_all = ckv_new, kpe_new
    else:
        ckv_all = jnp.concatenate([past_ckv.astype(ckv_new.dtype), ckv_new], axis=1)
        kpe_all = jnp.concatenate([past_kpe.astype(kpe_new.dtype), kpe_new], axis=1)
    o_lat = mla_attend(q_abs, q_pe, ckv_all, kpe_all, offset)
    out_b = jnp.einsum('bshr,rhv->bshv', o_lat, lw['w_uv']).reshape(B, S, MLA_WIDTH)

    gq = g_q.reshape(B, S, GLA_HEADS, GLA_DK) * (GLA_DK ** -0.5)
    gk = g_k.reshape(B, S, GLA_HEADS, GLA_DK)
    gv = g_v.reshape(B, S, GLA_HEADS, GLA_DV)
    log_alpha = (jax.nn.log_sigmoid((g_a @ lw['gla_wa2'] + lw['gla_ba']).astype(F32)) / GLA_TAU
                 ).reshape(B, S, GLA_HEADS, GLA_DK)
    o_c, gla_new = gla_scan(gq, gk, gv, log_alpha, gla_s0)
    out_c = (rmsnorm(o_c, lw['gla_norm_g']) * jax.nn.silu(g_o.reshape(B, S, GLA_HEADS, GLA_DV).astype(F32))
             ).reshape(B, S, GLA_WIDTH)

    n_a, n_b, n_c = jnp.split(lw['out_norm_g'], [LRU_WIDTH, LRU_WIDTH + MLA_WIDTH])
    merged = jnp.concatenate([rmsnorm(out_a, n_a), rmsnorm(out_b, n_b), rmsnorm(out_c, n_c)],
                             axis=-1).astype(hn.dtype)
    return merged @ lw['w_out'], ckv_new, kpe_new, conv_new, lru_new, gla_new

def hier_moe(h, lw):
    B, S, D = h.shape
    T = B * S
    t = h.reshape(T, D)
    rows = jnp.arange(T)
    g_logits = (t @ lw['router_wg']).astype(F32) + lw['router_bg']
    g_prob = jax.nn.softmax(g_logits, axis=-1)
    g_sel = jnp.argmax(g_logits, axis=-1)
    e_logits = ((t @ lw['router_we']).astype(F32) + lw['router_be']).reshape(T, N_GROUPS, EXPERTS_PER_GROUP)
    e_in = e_logits[rows, g_sel]
    top_v, top_i = lax.top_k(e_in, TOP_K)
    w_sel = jax.nn.softmax(top_v, axis=-1) * g_prob[rows, g_sel][:, None]
    idx = g_sel[:, None] * EXPERTS_PER_GROUP + top_i
    gates = jnp.einsum('tk,tke->te', w_sel, jax.nn.one_hot(idx, N_EXPERTS, dtype=F32))
    hg = jnp.einsum('td,edf->tef', t, lw['w_gate'])
    hu = jnp.einsum('td,edf->tef', t, lw['w_up'])
    a = jax.nn.silu(hg) * hu * gates[:, :, None].astype(hg.dtype)
    y = jnp.einsum('tef,efd->td', a, lw['w_down'])
    return y.reshape(B, S, D).astype(h.dtype)

def decoder(x, cache_ckv, cache_kpe, page_table, conv0, lru0, gla0, final_norm_g, w):
    new_ckv, new_kpe, new_conv, new_lru, new_gla = [], [], [], [], []
    for l in range(DEPTH):
        lw = {name: arr[l] for name, arr in w.items()}
        if page_table is None:
            past_ckv = past_kpe = None
        else:
            nb = page_table.shape[0]
            past_ckv = cache_ckv[l][page_table].reshape(nb, -1, KV_RANK)
            past_kpe = cache_kpe[l][page_table].reshape(nb, -1, QK_ROPE)
        mix, ckv, kpe, conv, lru, gla = token_mixers(rmsnorm(x, lw['norm1_g']), past_ckv, past_kpe,
                                                     conv0[l], lru0[l], gla0[l], lw)
        x = x + mix.astype(x.dtype)
        x = x + hier_moe(rmsnorm(x, lw['norm2_g']), lw)
        new_ckv.append(ckv)
        new_kpe.append(kpe)
        new_conv.append(conv)
        new_lru.append(lru)
        new_gla.append(gla)
    return (rmsnorm(x, final_norm_g), jnp.stack(new_ckv), jnp.stack(new_kpe), jnp.stack(new_conv),
            jnp.stack(new_lru), jnp.stack(new_gla))

def setup_inputs(seed: int = 0) -> dict:
    key = jax.random.key(seed)
    ks = iter(jax.random.split(key, 64))

    def nrm(shape, scale):
        return jax.random.normal(next(ks), shape, F32) * scale

    def gain(shape):
        return 1.0 + nrm(shape, 0.02)

    n_pages = PAST_LEN // PAGE_SIZE
    n_used = DEC_BATCH * n_pages
    n_phys = n_used + n_used // 4
    page_table = jax.random.permutation(next(ks), n_phys)[:n_used].reshape(DEC_BATCH, n_pages).astype(jnp.int32)
    u = jax.random.uniform(next(ks), (DEPTH, LRU_WIDTH), F32, minval=0.9, maxval=0.999)
    s = u ** (1.0 / LRU_C)
    lru_lambda = jnp.log(s) - jnp.log1p(-s)
    return {
        'x_prompt': nrm((BATCH, SEQ, D_MODEL), 1.0),
        'x_sample': nrm((DEC_BATCH, DEC_SEQ, D_MODEL), 1.0),
        'cache_ckv': nrm((DEPTH, n_phys, PAGE_SIZE, KV_RANK), 1.0),
        'cache_kpe': nrm((DEPTH, n_phys, PAGE_SIZE, QK_ROPE), 1.0),
        'page_table': page_table,
        'state_conv': nrm((DEPTH, DEC_BATCH, CONV_WIDTH - 1, LRU_WIDTH), 1.0),
        'state_lru': nrm((DEPTH, DEC_BATCH, LRU_WIDTH), 0.5),
        'state_gla': nrm((DEPTH, DEC_BATCH, GLA_HEADS, GLA_DK, GLA_DV), 0.3),
        'norm1_g': gain((DEPTH, D_MODEL)),
        'w_in': nrm((DEPTH, D_MODEL, IN_COLS), D_MODEL ** -0.5),
        'conv_w': nrm((DEPTH, CONV_WIDTH, LRU_WIDTH), CONV_WIDTH ** -0.5),
        'conv_b': nrm((DEPTH, LRU_WIDTH), 0.05),
        'lru_wa': nrm((DEPTH, LRU_BLOCKS, LRU_BW, LRU_BW), LRU_BW ** -0.5),
        'lru_ba': nrm((DEPTH, LRU_WIDTH), 0.05),
        'lru_wi': nrm((DEPTH, LRU_BLOCKS, LRU_BW, LRU_BW), LRU_BW ** -0.5),
        'lru_bi': nrm((DEPTH, LRU_WIDTH), 0.05),
        'lru_lambda': lru_lambda,
        'q_norm_g': gain((DEPTH, Q_RANK)),
        'w_uq': nrm((DEPTH, Q_RANK, MLA_HEADS * (QK_NOPE + QK_ROPE)), Q_RANK ** -0.5),
        'kv_norm_g': gain((DEPTH, KV_RANK)),
        'w_uk': nrm((DEPTH, KV_RANK, MLA_HEADS, QK_NOPE), KV_RANK ** -0.5),
        'w_uv': nrm((DEPTH, KV_RANK, MLA_HEADS, V_HEAD), KV_RANK ** -0.5),
        'gla_wa2': nrm((DEPTH, GLA_GATE_RANK, GLA_HEADS * GLA_DK), GLA_GATE_RANK ** -0.5),
        'gla_ba': nrm((DEPTH, GLA_HEADS * GLA_DK), 0.1),
        'gla_norm_g': gain((DEPTH, GLA_DV)),
        'out_norm_g': gain((DEPTH, MIX_WIDTH)),
        'w_out': nrm((DEPTH, MIX_WIDTH, D_MODEL), MIX_WIDTH ** -0.5),
        'norm2_g': gain((DEPTH, D_MODEL)),
        'router_wg': nrm((DEPTH, D_MODEL, N_GROUPS), D_MODEL ** -0.5),
        'router_bg': nrm((DEPTH, N_GROUPS), 0.01),
        'router_we': nrm((DEPTH, D_MODEL, N_EXPERTS), D_MODEL ** -0.5),
        'router_be': nrm((DEPTH, N_EXPERTS), 0.01),
        'w_gate': nrm((DEPTH, N_EXPERTS, D_MODEL, D_EXPERT), D_MODEL ** -0.5),
        'w_up': nrm((DEPTH, N_EXPERTS, D_MODEL, D_EXPERT), D_MODEL ** -0.5),
        'w_down': nrm((DEPTH, N_EXPERTS, D_EXPERT, D_MODEL), D_EXPERT ** -0.5),
        'final_norm_g': gain((D_MODEL,)),
    }

def reference(x_prompt, x_sample, cache_ckv, cache_kpe, page_table, state_conv, state_lru, state_gla,
              norm1_g, w_in, conv_w, conv_b, lru_wa, lru_ba, lru_wi, lru_bi, lru_lambda,
              q_norm_g, w_uq, kv_norm_g, w_uk, w_uv, gla_wa2, gla_ba, gla_norm_g, out_norm_g, w_out,
              norm2_g, router_wg, router_bg, router_we, router_be, w_gate, w_up, w_down, final_norm_g):
    w = dict(norm1_g=norm1_g, w_in=w_in, conv_w=conv_w, conv_b=conv_b, lru_wa=lru_wa, lru_ba=lru_ba,
             lru_wi=lru_wi, lru_bi=lru_bi, lru_lambda=lru_lambda, q_norm_g=q_norm_g, w_uq=w_uq,
             kv_norm_g=kv_norm_g, w_uk=w_uk, w_uv=w_uv, gla_wa2=gla_wa2, gla_ba=gla_ba,
             gla_norm_g=gla_norm_g, out_norm_g=out_norm_g, w_out=w_out, norm2_g=norm2_g,
             router_wg=router_wg, router_bg=router_bg, router_we=router_we, router_be=router_be,
             w_gate=w_gate, w_up=w_up, w_down=w_down)
    bp = x_prompt.shape[0]
    conv0 = jnp.zeros((DEPTH, bp, CONV_WIDTH - 1, LRU_WIDTH), x_prompt.dtype)
    lru0 = jnp.zeros((DEPTH, bp, LRU_WIDTH), F32)
    gla0 = jnp.zeros((DEPTH, bp, GLA_HEADS, GLA_DK, GLA_DV), F32)
    y_prompt, ckv_p, kpe_p, conv_p, lru_p, gla_p = decoder(
        x_prompt, None, None, None, conv0, lru0, gla0, final_norm_g, w)
    y_sample, ckv_s, kpe_s, conv_s, lru_s, gla_s = decoder(
        x_sample, cache_ckv, cache_kpe, page_table, state_conv, state_lru, state_gla, final_norm_g, w)
    return (y_prompt, y_sample, ckv_p, kpe_p, ckv_s, kpe_s, conv_p, conv_s, lru_p, lru_s, gla_p, gla_s)


_drawn_inputs = setup_inputs


def setup_inputs(seed=0):
    import zlib

    import numpy as np

    out = dict(_drawn_inputs(seed))
    spreads = {}
    factors = {'lru_ba': 3.431, 'router_bg': 3.437, 'router_be': 2.852, 'final_norm_g': 2.937}
    for name, (base, spread) in spreads.items():
        noise = np.random.default_rng([zlib.crc32(name.encode()), seed]).standard_normal(out[name].shape)
        drawn = base * np.exp(spread * noise) if base else spread * noise
        out[name] = __import__('jax').numpy.asarray(drawn.astype(out[name].dtype))
    for name, factor in factors.items():
        out[name] = (out[name] * factor).astype(out[name].dtype)
    return out
```

```python
from contextlib import ExitStack

import numpy as np

import concourse.bass as bass
from concourse import mybir

F32 = mybir.dt.float32
BF16 = mybir.dt.bfloat16
I32 = mybir.dt.int32
U32 = mybir.dt.uint32
ALU = mybir.AluOpType
ACT = mybir.ActivationFunctionType
AX_X = mybir.AxisListType.X

P = 128
DEPTH, D, SEQ, NB, NQ = 2, 1024, 512, 8, 8
NS = NB * NQ
T = SEQ + NS
TT = 5
KT = D // P
HALF = T // 2
PAGE, NPAGE = 128, 8
HEADS, NOPE, ROPE, VH = 8, 64, 32, 64
GH, GDK, GDV, CH = 4, 32, 64, 16
NCH = SEQ // CH
EXPERTS, GROUPS, EPG, DE = 32, 4, 8, 256
EPS = 1e-6
SCALE = float(NOPE + ROPE) ** -0.5
NEG = -1e30
RING = 4
MAXBLK = EXPERTS + 8
TABLE = MAXBLK + TT + 1
XE = 3 + SEQ
SEXT = NQ + 3
HE = SEQ + NB * (NQ + 1)

_o = np.cumsum([0, 256, 256, 256, 128, 32, 128, 128, 256, 16, 256])
X_LRU, Y_LRU, C_Q, C_KV, K_PE, G_Q, G_K, G_V, G_A, G_O = (int(v) for v in _o[:10])
ZT = 14
Z_X, Z_Y, Z_CQ, Z_CKV, Z_PE, Z_GQ, Z_GK, Z_GV, Z_GO = 0, 2, 4, 6, 7, 8, 9, 10, 12
Z_ORDER = [4, 5, 6, 7, 0, 1, 2, 3, 8, 9, 10, 11, 12, 13]
ATT_STEPS = HEADS * 4 + 3
GN_STEP = CH + 2


def rows_of(t):
    return P if t < TT - 1 else NS


C_ID, C_TRI, C_ONE, C_BLK, C_BM = 0, 128, 256, 384, 512
C_COS, C_SIN, C_IOTA, C_CM, C_QM, C_TOK, C_RST = 768, 1344, 1920, 2048, 2064, 2068, 2073
C_END = 2073 + T
M_CAUSAL, M_SAMPLE, M_ID = 0, 128, 384
M_END = 512
V_CW, V_CB, V_BA, V_BI, V_LAM, V_QN, V_KN, V_GB, V_GN, V_ON, V_SC, V_SL = (
    0, 8, 10, 12, 14, 16, 18, 19, 20, 21, 29, 77)
V_END = 93


def constants():
    c = np.zeros((P, C_END), np.float32)
    i = np.arange(P)
    c[:, C_ID:C_ID + P] = np.eye(P)
    c[:, C_TRI:C_TRI + P] = i[:, None] < i[None, :]
    c[:, C_ONE:C_ONE + P] = 1.0
    c[:, C_BLK:C_BLK + P] = (i[:, None] // GDV) == (i[None, :] // GDV)
    for j in range(2):
        head = 2 * j + i // GDV
        c[:, C_BM + j * P:C_BM + (j + 1) * P] = (i[:, None] // GDK == head[None, :]) * GDK ** -0.5
    pos = np.concatenate([np.arange(SEQ), np.tile(PAGE * NPAGE + np.arange(NQ), NB)]).astype(np.float32)
    half = ROPE // 2
    inv = (np.float32(10000.0) ** (-np.arange(half, dtype=np.float32) / half)).astype(np.float32)
    ang = pos[None, :] * inv[i % half][:, None]
    sign = np.where(i % ROPE < half, -1.0, 1.0)[:, None]
    c[:, C_COS:C_COS + T] = np.cos(ang)
    c[:, C_SIN:C_SIN + T] = np.sin(ang) * sign
    c[:, C_IOTA:C_IOTA + P] = i[None, :]
    c[:, C_CM:C_CM + 8] = i[:, None] // CH == np.arange(8)[None, :]
    c[:, C_CM + 8:C_CM + 16] = i[:, None] // NQ == np.arange(8)[None, :]
    c[:, C_QM:C_QM + GH] = (i[:, None] // GDK == np.arange(GH)[None, :]) * GDK ** -0.5
    c[:, C_TOK:C_TOK + TT] = i[:, None] + P * np.arange(TT)[None, :]
    c[:, C_RST:C_RST + T] = 1.0
    c[:, C_RST:C_RST + SEQ:CH] = 0.0
    c[:, C_RST + SEQ:C_RST + T:NQ] = 0.0
    m = np.zeros((P, M_END), np.float32)
    m[:, M_CAUSAL:M_CAUSAL + P] = np.where(i[None, :] <= i[:, None], 0.0, NEG)
    b2, q = i // 64, i % NQ
    for p in range(4):
        kb, kk = np.arange(NS) // NQ, np.arange(NS) % NQ
        ok = (kb[None, :] == (2 * p + b2)[:, None]) & (kk[None, :] <= q[:, None])
        m[:, M_SAMPLE + p * NS:M_SAMPLE + (p + 1) * NS] = np.where(ok, 0.0, NEG)
    m[:, M_ID:M_ID + P] = np.eye(P)
    return c, m


def attention_order(s):
    ahead, n = 2, HEADS * 4
    if s < n:
        yield ("s", s // 4, s % 4)
    if ahead <= s < n + ahead:
        yield ("pt", (s - ahead) // 4, (s - ahead) % 4)
    if s > ahead and (s - ahead) % 4 == 0:
        yield ("pv", (s - ahead) // 4 - 1)


def psum_plan():
    keys = [("hn", t, g) for t in range(TT) for g in range(2)]
    for m in Z_ORDER:
        keys += [("z", m, h) for h in range(2)]
        if m == Z_X + 1:
            keys += [("qsum", 0), ("qsum", 1), ("kvsum", 0), ("kvsum", 1)]
            keys += [("gate", 0, k) for k in range(3)]
        if m == Z_Y + 1:
            keys += [("q", j, h) for j in range(4) for h in range(2)]
            keys += [(kind, g, h) for g in range(2) for h in range(2) for kind in ("pe", "rot")]
            keys += [("gate", 1, k) for k in range(3)]
            keys += [("alpha", h) for h in range(2)]
            keys += [("qa", hd, h) for hd in range(HEADS) for h in range(2)]
            keys += [("ctok", 0), ("ctok", 1), ("qp",)]
        if m == Z_GV + 1:
            keys += [("vtok", n) for n in range(3)]
    keys += [("ktok", n) for n in range(2)]
    keys += [("delta", t) for t in range(TT)]
    keys += [("inter", g) for g in range(3)]
    for s in range(ATT_STEPS):
        keys += list(attention_order(s))
        if s < CH:
            keys += [("dp", s, 0), ("dp", s, 1)]
            if s < NQ:
                keys += [("ds", s)]
        if s == GN_STEP:
            keys += [("gnorm", j, h) for j in range(2) for h in range(2)]
    for p in range(4):
        keys += [("ss", p, k) for k in range(3)]
        keys += [("sp", p, k) for k in range(3)]
        keys += [("sv", p)]
    keys += [("uv", jj) for jj in range(4)] + [("uvs",)]
    keys += [("osum", k, h) for k in range(3) for h in range(2)]
    keys += [("wo", n, t) for n in range(2) for t in range(TT)]
    keys += [("hm", t, g) for t in range(TT) for g in range(2)]
    keys += [("logits",), ("rank",), ("table",)]
    return keys


def hybrid_step(nc, a, o):
    plan = psum_plan()
    place = {k: (n % 8, n // 8) for n, k in enumerate(plan)}
    assert len(place) == len(plan)
    uses = [sum(1 for b, _ in place.values() if b == k) for k in range(8)]

    with ExitStack() as ctx:
        def sb(name, shape, dt=F32):
            return ctx.enter_context(nc.sbuf_tensor(name, shape, dt))

        def sem(name):
            return ctx.enter_context(nc.semaphore(name))

        cst = sb("cst", [P, C_END])
        mask = sb("mask", [P, M_END], BF16)
        x = sb("x", [P, TT, D])
        vec = sb("vec", [P, V_END])
        sm = sb("sm", [P, 220])
        wlru = sb("wlru", [P, 4 * P])
        wa2 = sb("wa2", [P, P])
        wrt = sb("wrt", [P, KT * 36])
        rbias = sb("rbias", [P, 36])
        ra = sb("ra", [P, 4608])
        rb = sb("rb", [P, 4096])
        re = sb("re", [P, 15616])
        rf = sb("rf", [P, 5280])
        rg = sb("rg", [P, 12288])
        pages = sb("pages", [1, NB * NPAGE], I32)
        blocks = sb("blocks", [1, 128], I32)
        slots = sb("slots", [P, TABLE], U32)
        slot_now = sb("slot_now", [P, 1], U32)
        pos = sb("pos", [P, 2 * TT], U32)

        bank = [ctx.enter_context(nc.psum_tensor(f"bank{b}", [P, 512], F32)) for b in range(8)]

        ident, tri, ones, blk64 = (cst[:, k:k + P] for k in (C_ID, C_TRI, C_ONE, C_BLK))
        cos, sin = cst[:, C_COS:C_COS + T], cst[:, C_SIN:C_SIN + T]
        iota = cst[:, C_IOTA:C_IOTA + P]
        idb = mask[:, M_ID:M_ID + P]

        def cut(region, at, *dims):
            n = int(np.prod(dims))
            v = region[:, at:at + n]
            if len(dims) == 1:
                return v
            names = "abcd"[:len(dims)]
            return v.rearrange(f"p ({' '.join(names)}) -> p {' '.join(names)}",
                               **{k: d for k, d in zip(names, dims)})

        hT = cut(ra, 0, KT, T)
        pT = cut(ra, 0, 2, 4, 512)
        xg = cut(ra, 0, D)
        ysb = cut(ra, 1024, D)
        win = cut(rb, 0, 4, KT, P)
        wout = [cut(rb, 0, KT, 512), cut(ra, 0, KT, 512)]
        xT = cut(rb, 0, KT, P)
        act1 = cut(rb, 1024, DE)
        act2 = cut(rb, 1280, DE)
        actT = cut(rb, 1536, 2, P)
        cq = cut(re, 0, 2, T)
        wq = cut(re, 1152, 2, 1024)
        gw = cut(re, 0, 2, T)
        gdiff = cut(re, 1152, 2, T)
        la = cut(re, 2304, T)
        ckvT = cut(re, 3200, T)
        kpeT = cut(re, 3776, T)
        qn = cut(re, 4352, 4, T)
        gmsk = cut(re, 4352, 2, 512)
        ktok = cut(re, 5376, TT, P)
        gsout = cut(re, 6016, NB, GDV)
        outB = cut(re, 4352, 4, T)
        qpe = cut(re, 6656, 2, T)
        qa = cut(re, 7808, HEADS, SEQ)
        qas = cut(re, 7808 + HEADS * SEQ, NB, 64)
        sq = cut(re, 7808, 3, T)
        rsq = cut(re, 9536, 2, T)
        ctok = cut(re, 12416, TT, P)
        qp = cut(re, 13056, NB, 64)
        ukT = cut(re, 13568, 4, P)
        uv = cut(re, 14080, HEADS * VH)
        prob = cut(re, 14592, 2, 512)
        xs = cut(re, 12416, 2, D)
        gain = cut(re, 14464, D)
        xext = cut(rf, 0, 2, XE + NB * SEXT)
        yl = cut(rf, 1206, 2, T)
        outA = yl
        lru = [cut(rf, 2358 + k * HE, HE) for k in range(5)]
        gtmp = cut(rf, 2358, 2, T)
        router = cut(rf, 0, 5280)
        ygat = cut(rf, 0, 4, D)
        gq, gk, gv = cut(rg, 0, T), cut(rg, 576, T), cut(rg, 1152, 2, T)
        cum = cut(rg, 2304, T)
        qbd = cut(rg, 2880, GH, T)
        kd = cut(rg, 5184, T)
        oacc = cut(rg, 5760, 2, T)
        vtok = cut(rg, 6912, TT, 256)
        st = cut(rg, 8192, NCH + 1 + NB, GDV)
        gout = cut(rg, 11136, 2, T)
        outC = gtmp
        pg = [cut(rg, 6144 * k, 2, NPAGE, 3 * P) for k in range(2)]
        CKV, CKVT, KPET = slice(0, P), slice(P, 2 * P), slice(2 * P, 3 * P)
        sprob = cut(re, 4352, 1088)
        spT = cut(re, 5440, 9, P)
        osq = cut(rg, 0, 8, T)
        ors = cut(rg, 4608, 3, T)
        slot_at = [(rg, 0), (rg, 6144), (re, 0), (re, 6144)]
        wgu = [cut(r, at, KT, 512) for r, at in slot_at]
        wdn = [cut(r, at + 4096, 2, D) for r, at in slot_at]

        h_rows = nc.dram_tensor("h_rows", (T, D), F32).ap()
        y_rows = nc.dram_tensor("y_rows", (TABLE * P, D), F32).ap()

        full = [sem(f"bank{b}_full") for b in range(8)]
        read = [sem(f"bank{b}_read") for b in range(8)]
        names = """const_in mask_in mask_cast x_in vec_in gain_in wq_in uk_in uv_in wlru_in wa2_in gstate_in
            router_in rows_out ctail_out lru_out ckv_out kpe_out gla_out y_out
            xs_ready ssq_ready xs_used z_done q_ready ckv_ready kpe_ready sq_ready norm_used
            pads_ready conv_ready lru_steps gates_used r_ready a_ready pool_lru coef_ready
            la_ready cum_ready kd_ready qbd_ready gmsk_ready gmsk_used diff_ready exp_ready w_ready w_used
            gla_steps gn_ready gate_ready out_a out_c states_ready
            max_ready exp_done prob_ready s_max s_exp s_prob s_used
            merged osq_ready ors_ready wout_used logits_ready route_ready sel_ready
            gathered xg_used xt_act xt_vec gu_done silu_done act_ready at_done actt_ready
            down_done y_act y_vec y_stored combined ygat_in ygat_used pos_ready
            vector_steps scalar_steps pool_steps x_ready final_ready table_ready slot_copied
            lru_saved lnexp tailsaved kperep qpe_ready gelu gexp oacc_ready oacc_steps gsq
            out_b sel_exp sel_exp_done zeros_ready held""".split()
        S = {n: sem(n) for n in names}
        win_in = [sem(f"win{k}_in") for k in range(4)]
        page_in = [sem(f"page{k}_in") for k in range(2)]
        wout_in = [sem(f"wout{k}_in") for k in range(2)]
        wgu_in = [sem(f"wgu{k}_in") for k in range(RING)]
        wdn_in = [sem(f"wdn{k}_in") for k in range(RING)]

        block = ctx.enter_context(nc.Block())

        def begin(pe, L, key):
            b, n = place[key]
            if L * uses[b] + n > 0:
                pe.wait_ge(read[b], L * uses[b] + n)
            return bank[b]

        def done(ins, key):
            ins.then_inc(full[place[key][0]], 1)

        def take(eng, L, key):
            b, n = place[key]
            eng.wait_ge(full[b], L * uses[b] + n + 1)
            return bank[b]

        def give(ins, key):
            ins.then_inc(read[place[key][0]], 1)

        def after(eng, L, key):
            b, n = place[key]
            eng.wait_ge(read[b], L * uses[b] + n + 1)

        def steps(eng, name):
            count = [0]

            def link(ins):
                count[0] += 1
                ins.then_inc(S[name], 1)
                eng.wait_ge(S[name], count[0])
            return link

        halves = [slice(0, HALF), slice(HALF, T)]

        gaT = cut(re, 14592, T)
        ropetmp = cut(re, 14592 + T, HALF)
        eps_col = sm[:, 210:211]
        merged = [outA[:, 0, :], outA[:, 1, :]] + [outB[:, k, :] for k in range(4)] + [outC[:, 0, :], outC[:, 1, :]]
        rows_out = [sem(f"rows_out{k}") for k in range(2)]
        y_out = [sem(f"y_out{k}") for k in range(2)]
        ygat_in = [sem(f"ygat_in{k}") for k in range(4)]
        WUSES = [sum(1 for n in range(ZT) if n % 4 == k) for k in range(4)]
        YUSES = [sum(1 for n in range(2 * TT) if n % 4 == k) for k in range(4)]
        a_out = o
        acc = [0]
        r_log = cut(rf, 0, TT, 36)
        r_g, r_g8, r_e, r_e8, r_part = (cut(rf, 180 + 40 * k, TT, 8) for k in range(5))
        r_gi, r_ei = (cut(rf, 380 + 40 * k, TT, 8).bitcast(U32) for k in range(2))
        r_gid, r_sum, r_two = (cut(rf, 460 + 5 * k, TT) for k in range(3))
        r_eid = cut(rf, 475, TT, 2)
        r_gone = cut(rf, 485, TT, GROUPS)
        r_diff = cut(rf, 505, TT, GROUPS + 1)
        r_any, r_rank, r_hi = (cut(rf, 530 + 160 * k, TT, EXPERTS) for k in range(3))
        r_h2, r_l2 = (cut(rf, 1010 + 10 * k, 2 * TT) for k in range(2))
        r_cnt, r_nb = (cut(rf, 1030 + 32 * k, EXPERTS) for k in range(2))
        r_tab = cut(rf, 1094, 99)
        r_sel, r_prod = (cut(rf, 1200 + 320 * k, TT, 2, EXPERTS) for k in range(2))
        r_lo1 = cut(rf, 1840, 2 * TT, P)
        r_hi1 = cut(rf, 3120, 2 * TT, TABLE)

        def xs_free(eng, n, t):
            if n < 2 * DEPTH and t >= 2:
                take(eng, n // 2, ("hn" if n % 2 == 0 else "hm", t - 2, 1))
            if n % 2 == 1:
                use = n // 2 * (3 if t % 2 == 0 else 2) + t // 2
                if use > 0:
                    eng.wait_ge(rows_out[t % 2], 16 * use)
            if n == 2 * DEPTH and t >= 2:
                eng.wait_ge(y_out[t % 2], 16 * (t // 2))

        def x_done(eng, n, t):
            if n % 2 == 1:
                after(eng, n // 2, ("wo", 0, t))
                after(eng, n // 2, ("wo", 1, t))
            elif n > 0:
                eng.wait_ge(S["combined"], TT * (n // 2 - 1) + t + 1)

        def absorbed_query(eng, copy, L, hd, h):
            bk, key = take(eng, L, ("qa", hd, h)), ("qa", hd, h)
            if h == 0:
                give(copy(qa[:, hd, 0:HALF], bk[:, 0:HALF]), key)
            else:
                copy(qa[:, hd, HALF:SEQ], bk[:, 0:SEQ - HALF])
                give(copy(qas[:, :, NQ * hd:NQ * (hd + 1)],
                          bk[:, SEQ - HALF:HALF].rearrange("p (b q) -> p b q", q=NQ)), key)

        @block.sync
        def _(sp):
            sp.dma_start(x[:, 0:4, :], a["x_prompt"].rearrange("(t p) d -> p t d", p=P)).then_inc(S["x_in"], 16)
            sp.dma_start(x[:NS, 4, :], a["x_sample"]).then_inc(S["x_in"], 16)
            sp.dma_start(cst[:, :], a["cst"]).then_inc(S["const_in"], 16)
            sp.dma_start(rf[:, 0:M_END], a["msk"]).then_inc(S["mask_in"], 16)
            sp.dma_start(pages[:, :], a["page_table"]).then_inc(S["mask_in"], 16)

            def load_gain(n, row):
                if n > 0:
                    sp.wait_ge(S["xs_ready"], TT * n)
                sp.dma_start(gain, row.to_broadcast([P, D])).then_inc(S["gain_in"], 16)

            for L in range(DEPTH):
                if L > 0:
                    sp.wait_ge(S["combined"], TT * (L - 1) + 1)
                load_gain(2 * L, a["norm1_g"][L:L + 1, :])
                sp.dma_start(vec[:, :], a["vecs"][L]).then_inc(S["vec_in"], 16)
                for n, m in enumerate(Z_ORDER):
                    if n >= 4:
                        take(sp, L, ("z", Z_ORDER[n - 4], 1))
                    sp.dma_start(cut(rb, (n % 4) * 1024, 1024), a["win"][L, m]).then_inc(win_in[n % 4], 16)
                    if n == 4:
                        sp.dma_start(cut(re, 13568, 512), a["ukT"][L]).then_inc(S["uk_in"], 16)
                        sp.dma_start(uv, a["w_uv"][L]).then_inc(S["uv_in"], 16)
                    if n == 3:
                        sp.dma_start(cut(re, 1152, 2048), a["wq"][L]).then_inc(S["wq_in"], 16)
                        sp.dma_start(wlru[:, :], a["wlru"][L]).then_inc(S["wlru_in"], 16)
                        sp.dma_start(wa2[64:80, :], a["gla_wa2"][L]).then_inc(S["wa2_in"], 16)
                        sp.dma_start(st[:, NCH + 1:NCH + 1 + NB, :], a["state_gla"][L]).then_inc(S["gstate_in"], 16)
                        sp.dma_start(wrt[:, :], a["wrt"][L]).then_inc(S["router_in"], 16)
                        sp.dma_start(rbias[:, :], a["rbias"][L:L + 1, :].to_broadcast([P, 36])) \
                            .then_inc(S["router_in"], 16)
                take(sp, L, ("z", Z_ORDER[-1], 1))
                wo_rows = a["w_out"][L].rearrange("(k p) n -> p k n", p=P)
                sp.dma_start(wout[0], wo_rows[:, :, 0:512]).then_inc(wout_in[0], 16)
                sp.wait_ge(S["out_c"], L + 1)
                sp.wait_ge(S["gla_out"], 32 * (L + 1))
                for p in range(4):
                    if p > 1:
                        take(sp, L, ("sv", p - 2))
                    for b2 in range(2):
                        for j in range(NPAGE):
                            col = (2 * p + b2) * NPAGE + j
                            page = sp.value_load(pages[0:1, col:col + 1], min_val=0,
                                                 max_val=a["cache"].shape[1] - 1)
                            sp.dma_start(pg[p % 2][:, b2, j, :],
                                         a["cache"][L, bass.ds(page, 1)].rearrange("a p n -> (a p) n")) \
                                .then_inc(page_in[p % 2], 16)
                    if p == 1:
                        take(sp, L, ("pv", HEADS - 1))
                        sp.dma_start(wout[1], wo_rows[:, :, 512:1024]).then_inc(wout_in[1], 16)
                take(sp, L, ("uvs",))
                load_gain(2 * L + 1, a["norm2_g"][L:L + 1, :])

                def load_expert(e, s):
                    for half, w in enumerate((a["w_gate"], a["w_up"])):
                        sp.dma_start(wgu[s][:, :, half * DE:(half + 1) * DE],
                                     w[L, e].rearrange("(k p) f -> p k f", p=P)
                                     if isinstance(e, int) else
                                     w[L, bass.ds(e, 1)].rearrange("a (k p) f -> p (a k) f", p=P)) \
                            .then_inc(wgu_in[s], 16)
                    sp.dma_start(wdn[s], a["w_down"][L, e].rearrange("(k p) d -> p k d", p=P)
                                 if isinstance(e, int) else
                                 a["w_down"][L, bass.ds(e, 1)].rearrange("a (k p) d -> p (a k) d", p=P)) \
                        .then_inc(wdn_in[s], 16)

                sp.wait_ge(S["merged"], 8 * (L + 1))
                load_expert(0, 0)
                take(sp, L, ("wo", 1, TT - 1))
                for s in range(1, RING):
                    load_expert(s, s)
                sp.wait_ge(S["route_ready"], L + 1)
                with sp.Fori(1, EXPERTS // RING) as g:
                    for s in range(RING):
                        over = sp.value_load(blocks[0:1, bass.ds(g * RING + (66 + s - RING + 1), 1)],
                                             min_val=1, max_val=DEPTH * MAXBLK)
                        sp.wait_ge(S["down_done"], over)
                        load_expert(g * RING + s, s)
            load_gain(2 * DEPTH, a["final_norm_g"].rearrange("(a d) -> a d", a=1))
            for t in range(TT):
                r = rows_of(t)
                sp.wait_ge(S["xs_ready"], TT * 2 * DEPTH + t + 1)
                dst = a_out["y_prompt"][t * P:(t + 1) * P, :] if t < 4 else a_out["y_sample"]
                sp.dma_start(dst, xs[:r, t % 2, :]).then_inc(y_out[t % 2], 16)
            sp.wait_ge(y_out[0], 48)
            sp.wait_ge(y_out[1], 32)
            for n in ("ckv_out", "kpe_out", "ctail_out", "lru_out"):
                sp.wait_ge(S[n], 16 * DEPTH)
            sp.wait_ge(S["gla_out"], 32 * DEPTH)

        @block.gpsimd
        def _(pool):
            pool.wait_ge(S["mask_in"], 32)
            nc.gpsimd.tensor_copy(mask[:, :], rf[:, 0:M_END]).then_inc(S["mask_cast"], 1)
            pool.wait_ge(S["mask_cast"], 1)
            nc.gpsimd.memset(rg[:, 11136:11136 + D], 0.0).then_inc(S["zeros_ready"], 1)
            for L in range(DEPTH):
                if L > 0:
                    pool.wait_ge(S["combined"], TT * L)
                pool.wait_ge(S["vec_in"], 16 * (L + 1))
                nc.gpsimd.memset(xext[:, :, 0:3], 0.0)
                for t in range(2):
                    nc.gpsimd.tensor_copy(
                        xext[:, t, XE:].rearrange("p (b c) -> p b c", c=SEXT)[:, :, 0:3],
                        vec[:, V_SC + 24 * t:V_SC + 24 * t + 24].rearrange("p (b k) -> p b k", k=3))
                nc.gpsimd.memset(st[:, 0, :], 0.0)
                for k in (0, 1, 2):
                    last = nc.gpsimd.memset(lru[k][:, SEQ::NQ + 1], 0.0)
                last.then_inc(S["pads_ready"], 1)
                tail = sm[:, 130:184].rearrange("p (t c) -> p t c", t=2)
                if L > 0:
                    pool.wait_ge(S["ctail_out"], 16 * L)
                for t in range(2):
                    after(pool, L, ("z", Z_X + t, 0))
                    after(pool, L, ("z", Z_X + t, 1))
                    nc.gpsimd.tensor_copy(tail[:, t, 0:3], xext[:, t, XE - 3:XE])
                    last = nc.gpsimd.tensor_copy(
                        tail[:, t, 3:27].rearrange("p (b k) -> p b k", k=3),
                        xext[:, t, XE:].rearrange("p (b c) -> p b c", c=SEXT)[:, :, NQ:SEXT])
                last.then_inc(S["tailsaved"], 1)
                pool.wait_ge(S["tailsaved"], L + 1)
                pool.dma_start(a_out["conv"][L].rearrange("p t c -> p (t c)"), sm[:, 130:184]) \
                    .then_inc(S["ctail_out"], 16)
                pool.wait_ge(S["ckv_ready"], 2 * (L + 1))
                pool.dma_start(a_out["ckv"][L], ckvT).then_inc(S["ckv_out"], 16)
                pool.wait_ge(S["kpe_ready"], 2 * (L + 1))
                pool.dma_start(a_out["kpe"][L], kpeT[0:ROPE, :]).then_inc(S["kpe_out"], 16)
                pool.wait_ge(S["lru_saved"], 2 * (L + 1))
                pool.dma_start(a_out["lru"][L].rearrange("p t c -> p (t c)"), sm[:, 110:128]) \
                    .then_inc(S["lru_out"], 16)

                cumP = cum[:, 0:SEQ].rearrange("p (c n) -> p c n", n=CH)
                cumS = cum[:, SEQ:T].rearrange("p (c n) -> p c n", n=NQ)
                pool.wait_ge(S["cum_ready"], L + 1)
                nc.gpsimd.tensor_tensor(gdiff[:, 0, 0:SEQ].rearrange("p (c n) -> p c n", n=CH),
                                        cumP[:, :, CH - 1:CH].to_broadcast([P, NCH, CH]), cumP, ALU.subtract)
                nc.gpsimd.tensor_tensor(gdiff[:, 0, SEQ:T].rearrange("p (c n) -> p c n", n=NQ),
                                        cumS[:, :, NQ - 1:NQ].to_broadcast([P, NB, NQ]), cumS, ALU.subtract) \
                    .then_inc(S["diff_ready"], 1)
                for n in range(4 * TT):
                    t, h = n // 4, n % 4
                    r, cm = rows_of(t), C_CM + (8 if t == TT - 1 else 0)
                    if h == 0 and t % 2 == 0:
                        after(pool, L, ("vtok", t // 2))
                    if n >= 2:
                        was = n - 2
                        if was % 4 == 3:
                            take(pool, L, ("delta", was // 4))
                        else:
                            pool.wait_ge(S["gmsk_used"], 3 * TT * L + 3 * (was // 4) + was % 4 + 1)
                    nc.gpsimd.tensor_tensor(
                        gmsk[:r, n % 2, :].rearrange("p (c e) -> p c e", c=8),
                        vtok[:r, t, h * GDV:(h + 1) * GDV].unsqueeze(1).to_broadcast([r, 8, GDV]),
                        cst[:r, cm:cm + 8].unsqueeze(2).to_broadcast([r, 8, GDV]), ALU.mult) \
                        .then_inc(S["gmsk_ready"], 1)
                for d in range(1, CH):
                    if d >= 3:
                        pool.wait_ge(S["w_ready"], CH * L + d - 1)
                    else:
                        pool.wait_ge(S["kd_ready"], L + 1)
                    n = CH - d
                    last = nc.gpsimd.tensor_tensor(
                        gdiff[:, d % 2, 0:NCH * n].rearrange("p (c n) -> p c n", n=n),
                        cumP[:, :, d:CH], cumP[:, :, 0:n], ALU.subtract)
                    if d < NQ:
                        n = NQ - d
                        last = nc.gpsimd.tensor_tensor(
                            gdiff[:, d % 2, SEQ:SEQ + NB * n].rearrange("p (c n) -> p c n", n=n),
                            cumS[:, :, d:NQ], cumS[:, :, 0:n], ALU.subtract)
                    last.then_inc(S["diff_ready"], 1)
                after(pool, L, ("delta", TT - 1))
                pool.dma_start(a_out["gla_p"][L], st[:, NCH, :]).then_inc(S["gla_out"], 16)
                pool.dma_start(a_out["gla_s"][L], gsout).then_inc(S["gla_out"], 16)

                for t in range(TT):
                    r = rows_of(t)
                    pool.wait_ge(S["xs_ready"], TT * (2 * L + 1) + t + 1)
                    pool.dma_start(h_rows[t * P:t * P + r, :], xs[:r, t % 2, :]).then_inc(rows_out[t % 2], 16)
                pool.wait_ge(rows_out[0], 48 * (L + 1))
                pool.wait_ge(rows_out[1], 32 * (L + 1))

                def hold():
                    nc.gpsimd.tensor_tensor(sm[0:1, 211:212], cst[0:1, 0:1], cst[0:1, 0:1], ALU.mult) \
                        .then_inc(S["held"], 1)

                def gather(block):
                    nc.gpsimd.tensor_copy(slot_now[:, :], slots[:, block]).then_inc(S["slot_copied"], 1)

                def gather_rows(n):
                    pool.wait_ge(S["slot_copied"], n)
                    hold()
                    nc.gpsimd.indirect_dma_start(
                        xg, None, h_rows, bass.IndirectOffsetOnAxis(ap=slot_now[:, 0:1], axis=0)) \
                        .then_inc(S["gathered"], 16)

                pool.wait_ge(S["table_ready"], L + 1)
                gather(slice(0, 1))
                before = pool.value_load(blocks[0:1, 66:67], min_val=0, max_val=DEPTH * MAXBLK)
                if L > 0:
                    pool.wait_ge(S["held"], before + 2 * L)
                gather_rows(before + L + 1)
                with pool.Fori(0, EXPERTS) as e:
                    count = pool.value_load(blocks[0:1, bass.ds(e, 1)], min_val=1, max_val=TT)
                    first = pool.value_load(blocks[0:1, bass.ds(e + 33, 1)], min_val=0, max_val=MAXBLK)
                    ever = pool.value_load(blocks[0:1, bass.ds(e + 66, 1)], min_val=0, max_val=DEPTH * MAXBLK)
                    with pool.Fori(0, count) as c:
                        pool.wait_ge(S["xg_used"], ever + c + L + 1)
                        pool.wait_ge(S["gathered"], (ever + c + L + 1) * 16)
                        pool.wait_ge(S["held"], ever + c + 2 * L + 1)
                        gather(bass.ds(first + c + 1, 1))
                        gather_rows(ever + c + L + 2)
                total = pool.value_load(blocks[0:1, 98:99], min_val=1, max_val=DEPTH * MAXBLK)
                pool.wait_ge(S["gathered"], (total + L + 1) * 16)
                pool.wait_ge(S["held"], total + 2 * L + 1)
                pool.wait_ge(S["y_stored"], (total + 1) * 16)
                hold()
                for n in range(2 * TT):
                    r = rows_of(n // 2)
                    use = (2 * TT * L + n)
                    if n >= 4:
                        pool.wait_ge(S["ygat_used"], 2 * TT * L + n - 3)
                    nc.gpsimd.indirect_dma_start(
                        ygat[:r, n % 4, :], None, y_rows,
                        bass.IndirectOffsetOnAxis(ap=pos[:r, n:n + 1], axis=0)).then_inc(ygat_in[n % 4], 16)

        @block.scalar
        def _(act):
            link = steps(act, "scalar_steps")
            copy, fn = nc.scalar.copy, nc.scalar.activation

            def norm_sums(n):
                junk = cut(rb, 0, D) if n % 2 == 1 else cut(re, 4352, D)
                for t in range(TT):
                    r = rows_of(t)
                    if n == 0 and t == 0:
                        act.wait_ge(S["x_in"], 32)
                    x_done(act, n, t)
                    link(fn(junk[:r, :], x[:r, t, :], ACT.Square, accum_out=sm[:r, t:t + 1]))
                    if t >= TT - 2:
                        k = 0 if t == TT - 2 else t
                        link(fn(sm[:r, 5 + k:6 + t], sm[:r, k:t + 1], ACT.Ln, scale=1.0 / D, bias=eps_col[:r]))
                        fn(sm[:r, 5 + k:6 + t], sm[:r, 5 + k:6 + t], ACT.Exp, scale=-0.5) \
                            .then_inc(S["ssq_ready"], 1)

            def rstds(L, *what):
                for key, dst, n, signal in what:
                    bk = take(act, L, key)
                    give(fn(dst, bk[:, 0:HALF], ACT.Ln, scale=1.0 / n, bias=eps_col), key)
                for key, dst, n, signal in what:
                    after(act, L, key)
                    fn(dst, dst, ACT.Exp, scale=-0.5).then_inc(S[signal], 1)

            xc, R, I, C, H = lru

            def gates(L, t):
                for k, dst in ((0, R), (1, I)):
                    bk = take(act, L, ("gate", t, k))
                    give(fn(dst[:, 0:SEQ], bk[:, :], ACT.Tanh, scale=0.5,
                            bias=sm[:, 22 + 2 * k + t:23 + 2 * k + t]), ("gate", t, k))
                bk = take(act, L, ("gate", t, 2))
                for k, dst in ((0, R), (1, I)):
                    last = fn(dst[:, SEQ:].rearrange("p (b c) -> p b c", c=NQ + 1)[:, :, 1:],
                              bk[:, k * NS:(k + 1) * NS].rearrange("p (b q) -> p b q", q=NQ), ACT.Tanh,
                              scale=0.5, bias=sm[:, 22 + 2 * k + t:23 + 2 * k + t])
                give(last, ("gate", t, 2))

            def decay(L, t):
                act.wait_ge(S["r_ready"], 4 * L + 2 * t + 1)
                link(fn(C, R, ACT.Tanh))
                fn(R, R, ACT.Exp).then_inc(S["a_ready"], 1)

            def input_scale(L, t):
                act.wait_ge(S["r_ready"], 4 * L + 2 * t + 2)
                fn(C, C, ACT.Sqrt).then_inc(S["a_ready"], 1)

            def gelu(L, t):
                act.wait_ge(S["gelu"], 4 * L + 2 * t + 1)
                fn(I[:, 0:T], yl[:, t, :], ACT.Square).then_inc(S["a_ready"], 1)
                act.wait_ge(S["gelu"], 4 * L + 2 * t + 2)
                fn(I[:, 0:T], I[:, 0:T], ACT.Tanh, scale=0.7978845608028654).then_inc(S["a_ready"], 1)

            act.wait_ge(S["zeros_ready"], 1)
            act.dma_start(y_rows[EXPERTS * P:, :].rearrange("(b p) d -> p b d", p=P),
                          rg[:, 11136:11136 + D].unsqueeze(1).to_broadcast([P, TABLE - EXPERTS, D])) \
                .then_inc(S["y_stored"], 16)
            act.wait_ge(S["final_ready"], 1)
            for L in range(DEPTH):
                norm_sums(2 * L)
                for t in range(TT):
                    bk, r = take(act, L, ("hn", t, 0)), rows_of(t)
                    give(copy(hT[:, 0:4, t * P:t * P + r],
                              bk[:, :].rearrange("p (k n) -> p k n", k=4)[:, :, 0:r]), ("hn", t, 0))

                act.wait_ge(S["coef_ready"], 2 * L + 1)
                fn(sm[:, 12:14], sm[:, 10:12], ACT.Exp).then_inc(S["lru_steps"], 1)
                act.wait_ge(S["pads_ready"], L + 1)
                for m in Z_ORDER:
                    for h, cols in enumerate(halves):
                        if m in (Z_CQ, Z_CQ + 1, Z_CKV):
                            bk = take(act, L, ("z", m, h))
                            fn(sq[:, m - Z_CQ, cols], bk[:, 0:HALF], ACT.Square).then_inc(S["sq_ready"], 1)
                        elif m < Z_Y:
                            bk, key = take(act, L, ("z", m, h)), ("z", m, h)
                            if h == 0:
                                give(copy(xext[:, m, 3:3 + HALF], bk[:, 0:HALF]), key)
                            else:
                                copy(xext[:, m, 3 + HALF:XE], bk[:, 0:SEQ - HALF])
                                give(copy(xext[:, m, XE:].rearrange("p (b c) -> p b c", c=SEXT)[:, :, 3:],
                                          bk[:, SEQ - HALF:HALF].rearrange("p (b q) -> p b q", q=NQ)), key)
                        elif m < Z_CQ:
                            bk = take(act, L, ("z", m, h))
                            give(copy(yl[:, m - Z_Y, cols], bk[:, 0:HALF]), ("z", m, h))
                        elif m in (Z_GV, Z_GV + 1):
                            bk = take(act, L, ("z", m, h))
                            give(copy(gv[:, m - Z_GV, cols], bk[:, 0:HALF]), ("z", m, h))
                    if m == Z_X + 1:
                        rstds(L, *[(("qsum", h), rsq[:, 0, cols], 256, "lnexp") for h, cols in enumerate(halves)],
                              *[(("kvsum", h), rsq[:, 1, cols], P, "lnexp") for h, cols in enumerate(halves)])
                        act.wait_ge(S["kpe_ready"], 2 * (L + 1))
                        for g in range(1, 4):
                            last = copy(kpeT[32 * g:32 * g + 32, :], kpeT[0:32, :])
                        last.then_inc(S["kperep"], 1)
                        act.wait_ge(S["coef_ready"], 2 * L + 2)
                        gates(L, 0)
                        decay(L, 0)
                    if m == Z_Y:
                        input_scale(L, 0)
                    if m == Z_Y + 1:
                        gelu(L, 0)
                        for j in range(4):
                            for h, cols in enumerate(halves):
                                bk = take(act, L, ("q", j, h))
                                give(copy(qn[:, j, cols], bk[:, 0:HALF]), ("q", j, h))
                        gates(L, 1)
                        decay(L, 1)
                        for hd in (0, 2):
                            for h in range(2):
                                absorbed_query(act, copy, L, hd, h)
                        input_scale(L, 1)
                        for hd in (4, 6):
                            for h in range(2):
                                absorbed_query(act, copy, L, hd, h)
                        bk = take(act, L, ("ctok", 0))
                        give(copy(ctok[:, 0:4, :], bk[:, :].rearrange("p (t r) -> p t r", t=4)), ("ctok", 0))
                        bk = take(act, L, ("ctok", 1))
                        give(copy(ctok[:NS, 4, :], bk[:NS, 0:P]), ("ctok", 1))
                        gelu(L, 1)
                    if m == Z_GK:
                        act.wait_ge(S["la_ready"], L + 1)
                        link(fn(gdiff[:, 0, :], gdiff[:, 0, :], ACT.Exp, scale=-1.0))
                        fn(gdiff[:, 0, :], gdiff[:, 0, :], ACT.Ln, bias=1.0).then_inc(S["gexp"], 1)
                    if m == Z_GV + 1:
                        for n in range(3):
                            bk = take(act, L, ("vtok", n))
                            if n < 2:
                                give(copy(vtok[:, 2 * n:2 * n + 2, :], bk[:, :].rearrange("p (t c) -> p t c", t=2)),
                                     ("vtok", n))
                            else:
                                give(copy(vtok[:NS, 4, :], bk[:NS, 0:256]), ("vtok", n))
                act.wait_ge(S["cum_ready"], L + 1)
                fn(gw[:, 0, :], cum, ACT.Exp)
                fn(sm[:, 30:62], cum[:, CH - 1:SEQ:CH], ACT.Exp)
                fn(sm[:, 62:70], cum[:, SEQ + NQ - 1:T:NQ], ACT.Exp).then_inc(S["gexp"], 1)
                act.wait_ge(S["diff_ready"], CH * L + 1)
                fn(gdiff[:, 0, :], gdiff[:, 0, :], ACT.Exp).then_inc(S["gexp"], 1)

                def decays(d):
                    act.wait_ge(S["diff_ready"], CH * L + d + 1)
                    n = NCH * (CH - d)
                    last = fn(gdiff[:, d % 2, 0:n], gdiff[:, d % 2, 0:n], ACT.Exp)
                    if d < NQ:
                        n = NB * (NQ - d)
                        last = fn(gdiff[:, d % 2, SEQ:SEQ + n], gdiff[:, d % 2, SEQ:SEQ + n], ACT.Exp)
                    last.then_inc(S["exp_ready"], 1)

                decays(1)
                for s in range(ATT_STEPS):
                    w = s - 2
                    if 2 <= s + 1 < CH and s > 0:
                        decays(s + 1)
                    if s == GN_STEP:
                        act.wait_ge(S["oacc_ready"], L + 1)
                        fn(gtmp, oacc, ACT.Square).then_inc(S["gsq"], 1)
                        fn(gw, gout, ACT.Tanh, scale=0.5).then_inc(S["gexp"], 1)
                    if s == GN_STEP + 1:
                        rstds(L, *[(("gnorm", j, h), gdiff[:, j, cols], GDV, "gn_ready")
                                   for j in range(2) for h, cols in enumerate(halves)])
                    if 0 <= w < 4 * HEADS:
                        hd, i = w // 4, w % 4
                        key = ("pt", hd, i)
                        bk = take(act, L, key)
                        give(copy(pT[:, hd % 2, 0:i + 1, i * P:(i + 1) * P],
                                  bk[:, 0:(i + 1) * P].rearrange("p (k q) -> p k q", q=P)), key)
                    if s < 4 * HEADS:
                        n, key = (s % 4 + 1) * P, ("s", s // 4, s % 4)
                        bk = take(act, L, key)
                        act.wait_ge(S["max_ready"], 4 * HEADS * L + s + 1)
                        give(fn(prob[:, s % 2, 0:n], bk[:, 0:n], ACT.Exp, scale=SCALE,
                                bias=sm[:, 72 + s % 2:73 + s % 2], accum_out=sm[:, 74 + s % 2:75 + s % 2]), key)
                    if s >= 6 and (s - 2) % 4 == 0:
                        hd = (s - 2) // 4 - 1
                        bk = take(act, L, ("pv", hd))
                        give(copy(qa[:, hd, :], bk[:, :]), ("pv", hd))
                act.wait_ge(S["gla_out"], 32 * (L + 1))
                for p in range(4):
                    act.wait_ge(S["s_max"], 4 * L + p + 1)
                    for k, (at, n) in enumerate(((0, 512), (512, 512), (1024, NS))):
                        bk = take(act, L, ("ss", p, k))
                        give(fn(sprob[:, at:at + n], bk[:, 0:n], ACT.Exp, scale=SCALE, bias=sm[:, 84:85],
                                accum_out=sm[:, 85 + k:86 + k]), ("ss", p, k))
                    for k in range(3):
                        bk = take(act, L, ("sp", p, k))
                        if k < 2:
                            give(copy(spT[:, 4 * k:4 * k + 4, :], bk[:, :].rearrange("p (j q) -> p j q", j=4)),
                                 ("sp", p, k))
                        else:
                            give(copy(spT[:NS, 8, :], bk[:NS, 0:P]), ("sp", p, k))
                    bk = take(act, L, ("sv", p))
                    give(copy(qas[:, 2 * p:2 * p + 2, :], bk[:, 0:P].rearrange("p (b c) -> p b c", b=2)), ("sv", p))
                for jj in range(4):
                    bk = take(act, L, ("uv", jj))
                    give(copy(outB[:, jj, 0:SEQ], bk[:, :]), ("uv", jj))

                act.wait_ge(S["out_b"], L + 1)
                after(act, L, ("uv", 3))
                for k in range(8):
                    fn(osq[:, k, :], merged[k], ACT.Square).then_inc(S["osq_ready"], 1)
                rstds(L, *[(("osum", k, h), ors[:, k, cols], n, "ors_ready")
                           for k, n in enumerate((256, 512, 256)) for h, cols in enumerate(halves)])

                norm_sums(2 * L + 1)
                for t in range(TT):
                    bk, r = take(act, L, ("hm", t, 0)), rows_of(t)
                    give(copy(hT[:, 0:4, t * P:t * P + r],
                              bk[:, :].rearrange("p (k n) -> p k n", k=4)[:, :, 0:r]), ("hm", t, 0))
                act.wait_ge(S["sel_exp"], L + 1)
                fn(r_diff, r_diff, ACT.Exp).then_inc(S["sel_exp_done"], 1)

                act.wait_ge(S["route_ready"], L + 1)
                copy(sm[:, 200:201], sm[:, 190:191]).then_inc(S["y_act"], 1)

                def rows_transposed(n):
                    act.wait_ge(S["xg_used"], n)
                    copy(xT[:, 0:4, :], bank[0][:, :].rearrange("p (k n) -> p k n", k=4)).then_inc(S["xt_act"], 1)

                before = act.value_load(blocks[0:1, 66:67], min_val=0, max_val=DEPTH * MAXBLK)
                rows_transposed(before + L + 1)
                with act.Fori(0, EXPERTS) as e:
                    count = act.value_load(blocks[0:1, bass.ds(e, 1)], min_val=1, max_val=TT)
                    first = act.value_load(blocks[0:1, bass.ds(e + 33, 1)], min_val=0, max_val=MAXBLK)
                    ever = act.value_load(blocks[0:1, bass.ds(e + 66, 1)], min_val=0, max_val=DEPTH * MAXBLK)
                    with act.Fori(0, count) as c:
                        act.wait_ge(S["gu_done"], ever + c + 1)
                        fn(act1, bank[2][:, 0:DE], ACT.Silu).then_inc(S["silu_done"], 1)
                        rows_transposed(ever + c + L + 2)
                        act.wait_ge(S["at_done"], ever + c + 1)
                        copy(actT, bank[4][:, 0:DE].rearrange("p (k n) -> p k n", k=2)).then_inc(S["actt_ready"], 1)
                        act.wait_ge(S["down_done"], ever + c + 1)
                        act.wait_ge(S["y_stored"], (ever + c + 1) * 16)
                        copy(ysb[:, 0:512], bank[5][:, :]).then_inc(S["y_act"], 1)
                        act.wait_ge(S["y_act"], ever + c + L + 2)
                        act.wait_ge(S["y_vec"], ever + c + L + 2)
                        act.dma_start(y_rows[bass.ds((first + c) * P, P), :], ysb).then_inc(S["y_stored"], 16)
            norm_sums(2 * DEPTH)

        @block.vector
        def _(dve):
            V = nc.vector
            link = steps(dve, "vector_steps")

            def norm_rows(n):
                dve.wait_ge(S["gain_in"], 16 * (n + 1))
                for t in range(TT):
                    r = rows_of(t)
                    xs_free(dve, n, t)
                    dve.wait_ge(S["ssq_ready"], 2 * n + (1 if t < TT - 1 else 2))
                    V.scalar_tensor_tensor(xs[:r, t % 2, :], x[:r, t, :], sm[:r, 5 + t:6 + t], gain[:r, :],
                                           ALU.mult, ALU.mult).then_inc(S["xs_ready"], 1)

            def rope_add(L, kind_pe, kind_rot, h, cols, dst, signal):
                bk = take(dve, L, kind_pe)
                if kind_pe[1:] != (0, 0):
                    dve.wait_ge(S[signal], 4 * L + 2 * kind_pe[1] + h)
                give(V.tensor_tensor(dst, bk[:, 0:HALF], cos[:, cols], ALU.mult), kind_pe)
                bk = take(dve, L, kind_rot)
                give(V.tensor_tensor(ropetmp, bk[:, 0:HALF], sin[:, cols], ALU.mult), kind_rot)
                after(dve, L, kind_pe)
                after(dve, L, kind_rot)
                V.tensor_tensor(dst, dst, ropetmp, ALU.add).then_inc(S[signal], 1)

            link(V.memset(sm[:, :], 0.0))
            V.memset(eps_col, EPS).then_inc(S["final_ready"], 1)
            dve.wait_ge(S["final_ready"], 1)
            dve.wait_ge(S["const_in"], 16)
            for L in range(DEPTH):
                norm_rows(2 * L)
                for t in range(TT):
                    bk, r = take(dve, L, ("hn", t, 1)), rows_of(t)
                    give(V.tensor_copy(hT[:, 4:8, t * P:t * P + r],
                                       bk[:, :].rearrange("p (k n) -> p k n", k=4)[:, :, 0:r]), ("hn", t, 1))
                dve.wait_ge(S["vec_in"], 16 * (L + 1))
                lam = vec[:, V_LAM:V_LAM + 2]
                z, ex, s1, s2, pl, c1 = (sm[:, 10 + 2 * k:12 + 2 * k] for k in range(6))
                link(V.tensor_scalar(z, lam, -1.0, None, ALU.mult))
                link(V.tensor_tensor(s1, z, lam, ALU.max))
                V.tensor_scalar(z, s1, -1.0, None, ALU.mult).then_inc(S["coef_ready"], 1)
                dve.wait_ge(S["lru_steps"], L + 1)
                link(V.tensor_scalar(s1, ex, 2.0, None, ALU.add))
                link(V.reciprocal(s2, s1))
                link(V.tensor_tensor(s1, ex, s2, ALU.mult))
                link(V.tensor_tensor(s2, s1, s1, ALU.mult))
                link(V.tensor_scalar(pl, s2, 1.0 / 15, None, ALU.mult))
                for k in (13, 11, 9, 7, 5, 3):
                    link(V.scalar_tensor_tensor(pl, pl, 1.0 / k, s2, ALU.add, ALU.mult))
                link(V.scalar_tensor_tensor(pl, pl, 1.0, s1, ALU.add, ALU.mult))
                link(V.tensor_scalar(s1, lam, -1.0, 0.0, ALU.mult, ALU.max))
                link(V.scalar_tensor_tensor(s1, pl, 2.0, s1, ALU.mult, ALU.add))
                link(V.tensor_scalar(c1, s1, -4.0, None, ALU.mult))
                V.tensor_scalar(sm[:, 22:26], vec[:, V_BA:V_BA + 4], 0.5, None, ALU.mult) \
                    .then_inc(S["coef_ready"], 1)
                dve.wait_ge(S["coef_ready"], 2 * (L + 1))

                xc, R, I, C, H = lru
                seqs = lambda v: v[:, SEQ:].rearrange("p (b c) -> p b c", c=NQ + 1)

                def conv(t):
                    after(dve, L, ("z", Z_X + t, 1))
                    after(dve, L, ("z", Z_X + t, 0))
                    xq = xext[:, t, XE:].rearrange("p (b c) -> p b c", c=SEXT)
                    if t == 1:
                        for k in range(3):
                            take(dve, L, ("gate", 0, k))
                        V.memset(seqs(xc)[:, :, 0], 0.0)
                    w = lambda k: vec[:, V_CW + 2 * k + t:V_CW + 2 * k + t + 1]
                    V.tensor_scalar(xc[:, 0:SEQ], xext[:, t, 0:SEQ], w(0), vec[:, V_CB + t:V_CB + t + 1],
                                    ALU.mult, ALU.add)
                    link(V.tensor_scalar(seqs(xc)[:, :, 1:], xq[:, :, 0:NQ], w(0), vec[:, V_CB + t:V_CB + t + 1],
                                         ALU.mult, ALU.add))
                    for k in range(1, 4):
                        V.scalar_tensor_tensor(xc[:, 0:SEQ], xext[:, t, k:k + SEQ], w(k), xc[:, 0:SEQ],
                                               ALU.mult, ALU.add)
                        ins = V.scalar_tensor_tensor(seqs(xc)[:, :, 1:], xq[:, :, k:k + NQ], w(k),
                                                     seqs(xc)[:, :, 1:], ALU.mult, ALU.add)
                        if k < 3:
                            link(ins)
                        else:
                            ins.then_inc(S["conv_ready"], 1)

                def log_decay(t):
                    dve.wait_ge(S["conv_ready"], 2 * L + t + 1)
                    for k in range(3):
                        after(dve, L, ("gate", t, k))
                    V.tensor_scalar(R, R, 1.0, c1[:, t:t + 1], ALU.add, ALU.mult).then_inc(S["r_ready"], 1)
                    link(V.scalar_tensor_tensor(I, I, 1.0, xc, ALU.add, ALU.mult))

                def one_less(t):
                    dve.wait_ge(S["a_ready"], 8 * L + 4 * t + 1)
                    link(V.tensor_scalar(H, C, -1.0, 1.0, ALU.mult, ALU.add))
                    link(V.reciprocal(H, H))
                    V.scalar_tensor_tensor(C, C, -2.0, H, ALU.mult, ALU.mult).then_inc(S["r_ready"], 1)

                def scan(t):
                    dve.wait_ge(S["a_ready"], 8 * L + 4 * t + 2)
                    link(V.scalar_tensor_tensor(C, C, 0.5, I, ALU.mult, ALU.mult))
                    V.memset(seqs(R)[:, :, 0], 0.0)
                    V.tensor_copy(seqs(C)[:, :, 0], vec[:, V_SL + NB * t:V_SL + NB * (t + 1)]) \
                        .then_inc(S["gelu"], 1)
                    dve.wait_ge(S["gelu"], 4 * L + 2 * t + 1)
                    link(V.tensor_tensor_scan(H, R, C, 0.0, ALU.mult, ALU.add))
                    if L > 0 and t == 0:
                        dve.wait_ge(S["lru_out"], 16 * L)
                    V.tensor_copy(sm[:, 110 + 9 * t:111 + 9 * t], H[:, SEQ - 1:SEQ])
                    V.tensor_copy(sm[:, 111 + 9 * t:119 + 9 * t], seqs(H)[:, :, NQ]).then_inc(S["lru_saved"], 1)

                def gelu_out(t):
                    dve.wait_ge(S["a_ready"], 8 * L + 4 * t + 3)
                    after(dve, L, ("z", Z_Y + t, 1))
                    link(V.tensor_scalar(I[:, 0:T], I[:, 0:T], 0.044715, 1.0, ALU.mult, ALU.add))
                    V.tensor_tensor(I[:, 0:T], I[:, 0:T], yl[:, t, :], ALU.mult).then_inc(S["gelu"], 1)
                    dve.wait_ge(S["a_ready"], 8 * L + 4 * t + 4)
                    link(V.scalar_tensor_tensor(yl[:, t, :], I[:, 0:T], 1.0, yl[:, t, :], ALU.add, ALU.mult))
                    V.scalar_tensor_tensor(yl[:, t, 0:SEQ], yl[:, t, 0:SEQ], 0.5, H[:, 0:SEQ], ALU.mult, ALU.mult)
                    ys = yl[:, t, SEQ:T].rearrange("p (b q) -> p b q", q=NQ)
                    link(V.scalar_tensor_tensor(ys, ys, 0.5, seqs(H)[:, :, 1:], ALU.mult, ALU.mult))
                    if t == 0:
                        V.memset(seqs(R)[:, :, 0], 0.0)
                        link(V.memset(seqs(I)[:, :, 0], 0.0))


                nsq = 0
                for m in Z_ORDER:
                    for h, cols in enumerate(halves):
                        key = ("z", m, h)
                        if m in (Z_CQ, Z_CQ + 1, Z_CKV):
                            bk = take(dve, L, key)
                            nsq += 1
                            dve.wait_ge(S["sq_ready"], 6 * L + nsq)
                            give(V.tensor_copy(cq[:, m - Z_CQ, cols] if m < Z_CKV else ckvT[:, cols],
                                               bk[:, 0:HALF]), key)
                        elif m == Z_PE:
                            bk = take(dve, L, key)
                            if h > 0:
                                dve.wait_ge(S["kpe_ready"], 2 * L + h)
                            V.tensor_copy(gaT[64:80, cols], bk[64:80, 0:HALF])
                            link(V.tensor_copy(ropetmp[0:32, :], bk[32:64, 0:HALF]))
                            link(V.tensor_tensor(ropetmp[0:32, :], ropetmp[0:32, :], sin[0:32, cols], ALU.mult))
                            give(V.tensor_tensor(kpeT[0:32, cols], bk[0:32, 0:HALF], cos[0:32, cols], ALU.mult),
                                 key)
                            after(dve, L, key)
                            V.tensor_tensor(kpeT[0:32, cols], kpeT[0:32, cols], ropetmp[0:32, :], ALU.add) \
                                .then_inc(S["kpe_ready"], 1)
                        elif m in (Z_GQ, Z_GK):
                            bk = take(dve, L, key)
                            give(V.tensor_copy((gq if m == Z_GQ else gk)[:, cols], bk[:, 0:HALF]), key)
                        elif m >= Z_GO:
                            bk = take(dve, L, key)
                            dve.wait_ge(S["y_stored"], 16)
                            give(V.tensor_copy(gout[:, m - Z_GO, cols], bk[:, 0:HALF]), key)
                    if m == Z_X + 1:
                        dve.wait_ge(S["pads_ready"], L + 1)
                        conv(0)
                        for h, cols in enumerate(halves):
                            dve.wait_ge(S["lnexp"], 4 * L + h + 1)
                            for j in range(2):
                                after(dve, L, ("z", Z_CQ + j, h))
                                V.scalar_tensor_tensor(cq[:, j, cols], cq[:, j, cols], vec[:, V_QN + j:V_QN + j + 1],
                                                       rsq[:, 0, cols], ALU.mult, ALU.mult) \
                                    .then_inc(S["q_ready"], 1)
                        for h, cols in enumerate(halves):
                            dve.wait_ge(S["lnexp"], 4 * L + h + 3)
                            after(dve, L, ("z", Z_CKV, h))
                            V.scalar_tensor_tensor(ckvT[:, cols], ckvT[:, cols], vec[:, V_KN:V_KN + 1],
                                                   rsq[:, 1, cols], ALU.mult, ALU.mult).then_inc(S["ckv_ready"], 1)
                        log_decay(0)
                        conv(1)
                        one_less(0)
                        scan(0)
                    if m == Z_Y + 1:
                        gelu_out(0)
                        for g in range(2):
                            for h, cols in enumerate(halves):
                                rope_add(L, ("pe", g, h), ("rot", g, h), h, cols, qpe[:, g, cols], "qpe_ready")
                        log_decay(1)
                        for h, cols in enumerate(halves):
                            bk = take(dve, L, ("alpha", h))
                            give(V.tensor_scalar(la[:, cols], bk[:, 0:HALF], vec[:, V_GB:V_GB + 1], None, ALU.add),
                                 ("alpha", h))
                            after(dve, L, ("alpha", h))
                        V.scalar_tensor_tensor(gdiff[:, 0, :], la, -1.0, la, ALU.mult, ALU.max).then_inc(S["la_ready"], 1)
                        link(V.tensor_scalar(la, la, 0.0, None, ALU.min))
                        for hd in range(1, HEADS, 2):
                            for h in range(2):
                                absorbed_query(dve, V.tensor_copy, L, hd, h)
                            if hd == 3:
                                one_less(1)
                                scan(1)
                        bk = take(dve, L, ("qp",))
                        give(V.tensor_copy(qp[0:32, :, :].rearrange("p b (h q) -> p h b q", q=NQ),
                                           bk[0:32, :].rearrange("p (h b q) -> p h b q", h=HEADS, q=NQ)), ("qp",))
                        gelu_out(1)
                    if m == Z_GK:
                        dve.wait_ge(S["gexp"], 4 * L + 1)
                        link(V.scalar_tensor_tensor(la, gdiff[:, 0, :], -1.0, la, ALU.mult, ALU.add))
                        link(V.tensor_scalar(la, la, 1.0 / 16.0, None, ALU.mult))
                        V.tensor_tensor_scan(cum, cst[:, C_RST:C_RST + T], la, 0.0, ALU.mult, ALU.add) \
                            .then_inc(S["cum_ready"], 1)
                        dve.wait_ge(S["cum_ready"], L + 1)
                        dve.wait_ge(S["gexp"], 4 * L + 2)
                        for h in range(2):
                            after(dve, L, ("z", Z_GQ, h))
                            after(dve, L, ("z", Z_GK, h))
                        link(V.tensor_tensor(gw[:, 1, :], gq, gw[:, 0, :], ALU.mult))
                        for h in range(GH):
                            ins = V.tensor_scalar(qbd[:, h, :], gw[:, 1, :], cst[:, C_QM + h:C_QM + h + 1], None, ALU.mult)
                        ins.then_inc(S["qbd_ready"], 1)
                        dve.wait_ge(S["gexp"], 4 * L + 3)
                        V.tensor_tensor(kd, gk, gdiff[:, 0, :], ALU.mult).then_inc(S["kd_ready"], 1)
                bk = take(dve, L, ("ktok", 0))
                give(V.tensor_copy(ktok[:, 0:4, :], bk[:, :].rearrange("p (t c) -> p t c", t=4)), ("ktok", 0))
                bk = take(dve, L, ("ktok", 1))
                give(V.tensor_copy(ktok[:NS, 4, :], bk[:NS, 0:P]), ("ktok", 1))
                dve.wait_ge(S["gstate_in"], 16 * (L + 1))
                if L > 0:
                    dve.wait_ge(S["gla_out"], 32 * L)
                for t in range(TT):
                    bk = take(dve, L, ("delta", t))
                    for c in range(8):
                        n = 8 * t + c
                        src = st[:, n, :] if t < 4 else st[:, n + 1, :]
                        dst = st[:, n + 1, :] if t < 4 else gsout[:, c, :]
                        ins = V.scalar_tensor_tensor(dst, src, sm[:, 30 + n:31 + n],
                                                     bk[:, c * GDV:(c + 1) * GDV], ALU.mult, ALU.add)
                        if c < 7 and t < 4:
                            link(ins)
                    give(ins, ("delta", t))
                    after(dve, L, ("delta", t))
                for g in range(3):
                    bk, key = take(dve, L, ("inter", g)), ("inter", g)
                    n, at = (256, 256 * g) if g < 2 else (NS, SEQ)
                    give(V.tensor_copy(oacc[:, :, at:at + n], bk[:, 0:2 * n].rearrange("p (j n) -> p j n", j=2)), key)
                    after(dve, L, key)

                def chunked(v, n, at, k):
                    size, part = (CH, v[:, 0:SEQ]) if k == 0 else (NQ, v[:, SEQ:T])
                    return part.rearrange("p (c n) -> p c n", n=size)[:, :, at:at + n]

                def packed(v, n, k):
                    return (v[:, 0:NCH * n] if k == 0 else v[:, SEQ:SEQ + NB * n]) \
                        .rearrange("p (c n) -> p c n", n=n)

                def products(d):
                    if d >= 2:
                        take(dve, L, ("dp", d - 2, 1))
                        if d - 2 < NQ:
                            take(dve, L, ("ds", d - 2))
                    parts = [(0, CH - d)] + ([(1, NQ - d)] if d < NQ else [])
                    out = gw[:, d % 2, :]
                    if d == 0:
                        V.tensor_tensor(out, gq, gk, ALU.mult).then_inc(S["w_ready"], 1)
                        return
                    dve.wait_ge(S["exp_ready"], (CH - 1) * L + d)
                    for k, n in parts:
                        ins = V.tensor_tensor(packed(out, n, k), packed(gdiff[:, d % 2, :], n, k),
                                              chunked(gq, n, d, k), ALU.mult)
                    link(ins)
                    for k, n in parts:
                        ins = V.tensor_tensor(packed(out, n, k), packed(out, n, k), chunked(gk, n, 0, k), ALU.mult)
                    ins.then_inc(S["w_ready"], 1)

                def accumulate(d):
                    n = CH - d
                    for j in range(2):
                        bk = take(dve, L, ("dp", d, j))
                        give(V.tensor_tensor(packed(gtmp[:, j, :], n, 0), packed(bk, n, 0),
                                             chunked(gv[:, j, :], n, 0, 0), ALU.mult), ("dp", d, j))
                        after(dve, L, ("dp", d, j))
                        V.tensor_tensor(chunked(oacc[:, j, :], n, d, 0), chunked(oacc[:, j, :], n, d, 0),
                                        packed(gtmp[:, j, :], n, 0), ALU.add).then_inc(S["oacc_steps"], 1)
                    if d < NQ:
                        n = NQ - d
                        bk = take(dve, L, ("ds", d))
                        for j in range(2):
                            ins = V.tensor_tensor(packed(gtmp[:, j, :], n, 1),
                                                  bk[:, j * NS:j * NS + NB * n].rearrange("p (c n) -> p c n", n=n),
                                                  chunked(gv[:, j, :], n, 0, 1), ALU.mult)
                        give(ins, ("ds", d))
                        after(dve, L, ("ds", d))
                        for j in range(2):
                            ins = V.tensor_tensor(chunked(oacc[:, j, :], n, d, 1), chunked(oacc[:, j, :], n, d, 1),
                                                  packed(gtmp[:, j, :], n, 1), ALU.add)
                        ins.then_inc(S["oacc_steps"], 1)
                    acc[0] += 2 + (d < NQ)
                    dve.wait_ge(S["oacc_steps"], acc[0])

                for m in (0, 1):
                    after(dve, L, ("z", Z_GV + m, 0))
                    after(dve, L, ("z", Z_GV + m, 1))
                products(0)
                for s in range(ATT_STEPS):
                    if s < 4 * HEADS:
                        n, b2 = (s % 4 + 1) * P, s % 2
                        bk = take(dve, L, ("s", s // 4, s % 4))
                        link(V.tensor_reduce(sm[:, 70 + b2:71 + b2], bk[:, 0:n], AX_X, ALU.max))
                        V.tensor_scalar(sm[:, 72 + b2:73 + b2], sm[:, 70 + b2:71 + b2], -SCALE, None, ALU.mult) \
                            .then_inc(S["max_ready"], 1)
                    if 0 < s <= 4 * HEADS:
                        w = s - 1
                        n, b2 = (w % 4 + 1) * P, w % 2
                        after(dve, L, ("s", w // 4, w % 4))
                        link(V.reciprocal(sm[:, 76 + b2:77 + b2], sm[:, 74 + b2:75 + b2]))
                        V.tensor_scalar(prob[:, b2, 0:n], prob[:, b2, 0:n], sm[:, 76 + b2:77 + b2], None, ALU.mult) \
                            .then_inc(S["prob_ready"], 1)
                    if s + 1 < CH:
                        products(s + 1)
                    if 0 < s <= CH:
                        accumulate(s - 1)
                    if s == CH:
                        V.tensor_copy(sm[:, 201:202], sm[:, 190:191]).then_inc(S["oacc_ready"], 1)
                    if s == GN_STEP + 1:
                        for j in range(2):
                            for h, cols in enumerate(halves):
                                dve.wait_ge(S["gn_ready"], 4 * L + 2 * j + h + 1)
                                ins = V.scalar_tensor_tensor(oacc[:, j, cols], oacc[:, j, cols], vec[:, V_GN:V_GN + 1],
                                                             gdiff[:, j, cols], ALU.mult, ALU.mult)
                        link(ins)
                        dve.wait_ge(S["gexp"], 4 * L + 4)
                        link(V.scalar_tensor_tensor(gout, gw, 1.0, gout, ALU.add, ALU.mult))
                        V.scalar_tensor_tensor(outC, gout, 0.5, oacc, ALU.mult, ALU.mult).then_inc(S["out_c"], 1)

                for p in range(4):
                    for k, n in enumerate((512, 512, NS)):
                        bk = take(dve, L, ("ss", p, k))
                        ins = V.tensor_reduce(sm[:, 80 + k:81 + k], bk[:, 0:n], AX_X, ALU.max)
                    link(ins)
                    link(V.tensor_reduce(sm[:, 83:84], sm[:, 80:83], AX_X, ALU.max))
                    V.tensor_scalar(sm[:, 84:85], sm[:, 83:84], -SCALE, None, ALU.mult).then_inc(S["s_max"], 1)
                    for k in range(3):
                        after(dve, L, ("ss", p, k))
                    link(V.tensor_reduce(sm[:, 88:89], sm[:, 85:88], AX_X, ALU.add))
                    link(V.reciprocal(sm[:, 89:90], sm[:, 88:89]))
                    V.tensor_scalar(sprob, sprob, sm[:, 89:90], None, ALU.mult).then_inc(S["s_prob"], 1)
                dve.wait_ge(S["gla_out"], 32 * (L + 1))
                bk = take(dve, L, ("uvs",))
                give(V.tensor_copy(outB[:, :, SEQ:T], bk[:, 0:4 * NS].rearrange("p (j n) -> p j n", j=4)), ("uvs",))
                after(dve, L, ("uvs",))
                V.tensor_copy(sm[:, 202:203], sm[:, 190:191]).then_inc(S["out_b"], 1)

                for k, g in enumerate((0, 0, 1, 1, 1, 1, 2, 2)):
                    if k in (0, 2, 6):
                        dve.wait_ge(S["ors_ready"], 6 * L + 2 * g + 2)
                    V.scalar_tensor_tensor(merged[k], merged[k], vec[:, V_ON + k:V_ON + k + 1], ors[:, g, :],
                                           ALU.mult, ALU.mult).then_inc(S["merged"], 1)
                for n in range(2):
                    for t in range(TT):
                        bk, r, key = take(dve, L, ("wo", n, t)), rows_of(t), ("wo", n, t)
                        half = x[:r, t, 512 * n:512 * n + 512]
                        give(V.tensor_tensor(half, half, bk[:r, :], ALU.add), key)

                norm_rows(2 * L + 1)
                for t in range(TT):
                    bk, r = take(dve, L, ("hm", t, 1)), rows_of(t)
                    give(V.tensor_copy(hT[:, 4:8, t * P:t * P + r],
                                       bk[:, :].rearrange("p (k n) -> p k n", k=4)[:, :, 0:r]), ("hm", t, 1))

                link(V.memset(rf[:, 0:1200], 0.0))
                link(V.memset(r_g, -3.0e38))
                dve.wait_ge(S["router_in"], 32 * (L + 1))
                bk = take(dve, L, ("logits",))
                V.tensor_tensor(r_log[:, 0:4, :], bk[:, 0:144].rearrange("p (t n) -> p t n", t=4),
                                rbias[:, :].unsqueeze(1).to_broadcast([P, 4, 36]), ALU.add)
                give(V.tensor_tensor(r_log[:NS, 4, :], bk[:NS, 144:180], rbias[:NS, :], ALU.add), ("logits",))
                after(dve, L, ("logits",))
                link(V.tensor_copy(r_g[:, :, 0:GROUPS], r_log[:, :, 0:GROUPS]))
                for t in range(TT):
                    ins = V.max(r_g8[:, t, :], r_g[:, t, :])
                link(ins)
                for t in range(TT):
                    ins = V.max_index(r_gi[:, t, :], r_g8[:, t, :], r_g[:, t, :])
                link(ins)
                link(V.tensor_copy(r_gid, r_gi[:, :, 0]))
                link(V.tensor_tensor(r_gone, iota[:, 0:GROUPS].unsqueeze(1).to_broadcast([P, TT, GROUPS]),
                                     r_gid.unsqueeze(2).to_broadcast([P, TT, GROUPS]), ALU.is_equal))
                for g in range(GROUPS):
                    part = r_log[:, :, GROUPS + EPG * g:GROUPS + EPG * (g + 1)]
                    link(V.tensor_tensor(r_part, part, r_gone[:, :, g:g + 1].to_broadcast([P, TT, EPG]), ALU.mult))
                    link(V.tensor_tensor(r_e, r_e, r_part, ALU.add))
                for t in range(TT):
                    ins = V.max(r_e8[:, t, :], r_e[:, t, :])
                link(ins)
                for t in range(TT):
                    ins = V.max_index(r_ei[:, t, :], r_e8[:, t, :], r_e[:, t, :])
                link(ins)
                link(V.tensor_copy(r_eid, r_ei[:, :, 0:2]))
                link(V.scalar_tensor_tensor(r_eid, r_gid.unsqueeze(2).to_broadcast([P, TT, 2]), float(EPG), r_eid,
                                            ALU.mult, ALU.add))
                V.tensor_tensor(r_diff[:, :, 0:GROUPS], r_log[:, :, 0:GROUPS],
                                r_g8[:, :, 0:1].to_broadcast([P, TT, GROUPS]), ALU.subtract)
                V.tensor_tensor(r_diff[:, :, GROUPS], r_e8[:, :, 1], r_e8[:, :, 0], ALU.subtract) \
                    .then_inc(S["sel_exp"], 1)
                for k in range(2):
                    ins = V.tensor_tensor(r_sel[:, :, k, :], iota[:, 0:EXPERTS].unsqueeze(1).to_broadcast([P, TT, EXPERTS]),
                                          r_eid[:, :, k:k + 1].to_broadcast([P, TT, EXPERTS]), ALU.is_equal)
                link(ins)
                V.tensor_tensor(r_any, r_sel[:, :, 0, :], r_sel[:, :, 1, :], ALU.add).then_inc(S["sel_ready"], 1)
                dve.wait_ge(S["sel_exp_done"], L + 1)
                link(V.tensor_reduce(r_sum, r_diff[:, :, 0:GROUPS], AX_X, ALU.add))
                link(V.tensor_scalar(r_two, r_diff[:, :, GROUPS], 1.0, None, ALU.add))
                link(V.tensor_tensor(r_sum, r_sum, r_two, ALU.mult))
                link(V.reciprocal(sm[:, 100:105], r_sum))
                link(V.tensor_tensor(sm[:, 105:110], sm[:, 100:105], r_diff[:, :, GROUPS], ALU.mult))
                bk = take(dve, L, ("rank",))
                V.tensor_copy(r_rank[:, 0:4, :], bk[:, 0:128].rearrange("p (t e) -> p t e", t=4))
                V.tensor_copy(r_rank[:NS, 4, :], bk[:NS, 128:160])
                give(V.tensor_copy(r_cnt, bk[:, 160:192]), ("rank",))
                after(dve, L, ("rank",))
                link(V.tensor_scalar(r_nb, r_cnt, float(P), 1.0, ALU.is_gt, ALU.add))
                for k in (2, 3, 4):
                    link(V.scalar_tensor_tensor(r_nb, r_cnt, float(k * P), r_nb, ALU.is_gt, ALU.add))
                link(V.tensor_tensor_scan(r_tab[:, 34:66], ones[:, 0:EXPERTS], r_nb, 0.0, ALU.mult, ALU.add))
                V.tensor_copy(r_tab[:, 0:32], r_nb)
                link(V.tensor_scalar(r_tab[:, 66:99], r_tab[:, 33:66], sm[:, 190:191], None, ALU.add))
                link(V.tensor_copy(sm[:, 190:191], r_tab[:, 98:99]))
                if L > 0:
                    dve.wait_ge(S["combined"], TT * L)
                V.tensor_copy(blocks[0:1, 0:99], r_tab[0:1, 0:99]).then_inc(S["route_ready"], 1)
                link(V.tensor_scalar(r_hi, r_rank, float(P), None, ALU.is_ge))
                for k in (2, 3, 4):
                    link(V.scalar_tensor_tensor(r_hi, r_rank, float(k * P), r_hi, ALU.is_ge, ALU.add))
                link(V.scalar_tensor_tensor(r_rank, r_hi, -float(P), r_rank, ALU.mult, ALU.add))
                link(V.tensor_tensor(r_hi, r_hi, r_tab[:, 33:65].unsqueeze(1).to_broadcast([P, TT, EXPERTS]), ALU.add))
                for src, dst in ((r_hi, r_h2), (r_rank, r_l2)):
                    for k in range(2):
                        ins = V.tensor_tensor(r_prod[:, :, k, :], r_sel[:, :, k, :], src, ALU.mult)
                    link(ins)
                    link(V.tensor_reduce(dst, r_prod.rearrange("p t k e -> p (t k) e"), AX_X, ALU.add))
                V.scalar_tensor_tensor(pos[:, :], r_h2, float(P), r_l2, ALU.mult, ALU.add)
                for n in range(2 * TT):
                    V.tensor_scalar(r_lo1[:, n, :], iota, r_l2[:, n:n + 1], None, ALU.is_equal)
                    V.tensor_scalar(r_hi1[:, n, :], iota[:, 0:TABLE], r_h2[:, n:n + 1],
                                    cst[:, C_TOK + n // 2:C_TOK + n // 2 + 1], ALU.is_equal, ALU.mult) \
                        .then_inc(S["pos_ready"], 1)
                bk = take(dve, L, ("table",))
                give(V.tensor_copy(slots[:, :], bk[:, 0:TABLE]), ("table",))
                after(dve, L, ("table",))
                V.memset(sm[:, 203:204], 0.0).then_inc(S["table_ready"], 1)

                V.memset(sm[:, 204:205], 0.0).then_inc(S["y_vec"], 1)
                dve.wait_ge(S["route_ready"], L + 1)

                def rows_transposed(n):
                    dve.wait_ge(S["xg_used"], n)
                    V.tensor_copy(xT[:, 4:8, :], bank[1][:, :].rearrange("p (k n) -> p k n", k=4)) \
                        .then_inc(S["xt_vec"], 1)

                before = dve.value_load(blocks[0:1, 66:67], min_val=0, max_val=DEPTH * MAXBLK)
                rows_transposed(before + L + 1)
                with dve.Fori(0, EXPERTS) as e:
                    count = dve.value_load(blocks[0:1, bass.ds(e, 1)], min_val=1, max_val=TT)
                    ever = dve.value_load(blocks[0:1, bass.ds(e + 66, 1)], min_val=0, max_val=DEPTH * MAXBLK)
                    with dve.Fori(0, count) as c:
                        dve.wait_ge(S["silu_done"], ever + c + 1)
                        V.tensor_tensor(act2, act1, bank[2][:, DE:2 * DE], ALU.mult).then_inc(S["act_ready"], 1)
                        rows_transposed(ever + c + L + 2)
                        dve.wait_ge(S["down_done"], ever + c + 1)
                        dve.wait_ge(S["y_stored"], (ever + c + 1) * 16)
                        V.tensor_copy(ysb[:, 512:1024], bank[6][:, :]).then_inc(S["y_vec"], 1)
                for n in range(2 * TT):
                    t, k = n // 2, n % 2
                    r = rows_of(t)
                    dve.wait_ge(ygat_in[n % 4], 16 * (L * YUSES[n % 4] + n // 4 + 1))
                    if k == 1:
                        dve.wait_ge(S["ygat_used"], 2 * TT * L + n)
                    ins = V.scalar_tensor_tensor(x[:r, t, :], ygat[:r, n % 4, :], sm[:r, 100 + 5 * k + t:101 + 5 * k + t],
                                                 x[:r, t, :], ALU.mult, ALU.add)
                    ins.then_inc(S["ygat_used"], 1)
                    if k == 1:
                        dve.wait_ge(S["ygat_used"], 2 * TT * L + n + 1)
                        V.memset(sm[:, 205:206], 0.0).then_inc(S["combined"], 1)
            norm_rows(2 * DEPTH)

        @block.tensor
        def _(pe):
            mm, tr = nc.tensor.matmul, nc.tensor.transpose
            pe.wait_ge(S["const_in"], 16)
            pe.wait_ge(S["mask_cast"], 1)

            def transpose_rows(L, kind, n):
                for t in range(TT):
                    r = rows_of(t)
                    pe.wait_ge(S["xs_ready"], TT * n + t + 1)
                    for g in range(2):
                        bk = begin(pe, L, (kind, t, g))
                        for k in range(4):
                            ins = tr(bk[:, k * P:k * P + r], xs[:r, t % 2, (4 * g + k) * P:(4 * g + k + 1) * P],
                                     ident[:r, :r])
                        done(ins, (kind, t, g))

            for L in range(DEPTH):
                transpose_rows(L, "hn", 2 * L)
                for t in range(TT):
                    for g in range(2):
                        after(pe, L, ("hn", t, g))
                def gate_products(t):
                    xcs = lru[0][:, SEQ:].rearrange("p (b c) -> p b c", c=NQ + 1)[:, :, 1:]
                    pe.wait_ge(S["wlru_in"], 16 * (L + 1))
                    pe.wait_ge(S["conv_ready"], 2 * L + t + 1)
                    for k in range(2):
                        bk = begin(pe, L, ("gate", t, k))
                        done(mm(bk[:, :], wlru[:, (2 * k + t) * P:(2 * k + t + 1) * P], lru[0][:, 0:SEQ],
                                start=True, stop=True), ("gate", t, k))
                    bk = begin(pe, L, ("gate", t, 2))
                    for k in range(2):
                        ins = mm(bk[:, k * NS:(k + 1) * NS], wlru[:, (2 * k + t) * P:(2 * k + t + 1) * P], xcs,
                                 start=True, stop=True)
                    done(ins, ("gate", t, 2))

                for n, m in enumerate(Z_ORDER):
                    pe.wait_ge(win_in[n % 4], 16 * (L * WUSES[n % 4] + n // 4 + 1))
                    mrows = 80 if m == Z_PE else P
                    for h, cols in enumerate(halves):
                        bk = begin(pe, L, ("z", m, h))
                        for k in range(KT):
                            ins = mm(bk[:mrows, 0:HALF], win[:, n % 4, k, :mrows], hT[:, k, cols],
                                     start=k == 0, stop=k == KT - 1)
                        done(ins, ("z", m, h))
                    if m == Z_X + 1:
                        pe.wait_ge(S["sq_ready"], 6 * (L + 1))
                        for h, cols in enumerate(halves):
                            bk = begin(pe, L, ("qsum", h))
                            mm(bk[:, 0:HALF], ones, sq[:, 0, cols], start=True, stop=False)
                            done(mm(bk[:, 0:HALF], ones, sq[:, 1, cols], start=False, stop=True), ("qsum", h))
                        for h, cols in enumerate(halves):
                            bk = begin(pe, L, ("kvsum", h))
                            done(mm(bk[:, 0:HALF], ones, sq[:, 2, cols], start=True, stop=True), ("kvsum", h))
                        gate_products(0)
                    if m == Z_Y + 1:
                        pe.wait_ge(S["q_ready"], 4 * (L + 1))
                        pe.wait_ge(S["ckv_ready"], 2 * (L + 1))
                        pe.wait_ge(S["wq_in"], 16 * (L + 1))

                        def query(key, col, cols):
                            bk = begin(pe, L, key)
                            for k in range(2):
                                ins = mm(bk[:, 0:HALF], wq[:, k, col * P:(col + 1) * P], cq[:, k, cols],
                                         start=k == 0, stop=k == 1)
                            done(ins, key)

                        for j in range(4):
                            for h, cols in enumerate(halves):
                                query(("q", j, h), j, cols)
                        for g in range(2):
                            for h, cols in enumerate(halves):
                                query(("pe", g, h), 4 + g, cols)
                                query(("rot", g, h), 6 + g, cols)
                        gate_products(1)
                        pe.wait_ge(S["wa2_in"], 16 * (L + 1))
                        for h, cols in enumerate(halves):
                            bk = begin(pe, L, ("alpha", h))
                            done(mm(bk[:, 0:HALF], wa2[64:80, :], gaT[64:80, cols], start=True, stop=True), ("alpha", h))
                        pe.wait_ge(S["uk_in"], 16 * (L + 1))
                        for hd in range(HEADS):
                            rows = slice(64 * (hd % 2), 64 * (hd % 2) + 64)
                            for h, cols in enumerate(halves):
                                after(pe, L, ("q", hd // 2, h))
                                bk = begin(pe, L, ("qa", hd, h))
                                done(mm(bk[:, 0:HALF], ukT[rows, hd // 2, :], qn[rows, hd // 2, cols], start=True, stop=True),
                                     ("qa", hd, h))
                        bk = begin(pe, L, ("ctok", 0))
                        for t in range(4):
                            ins = tr(bk[:, t * P:(t + 1) * P], ckvT[:, t * P:(t + 1) * P], ident)
                        done(ins, ("ctok", 0))
                        bk = begin(pe, L, ("ctok", 1))
                        done(tr(bk[:NS, 0:P], ckvT[:, SEQ:T], ident), ("ctok", 1))
                        pe.wait_ge(S["qpe_ready"], 4 * (L + 1))
                        bk = begin(pe, L, ("qp",))
                        for hd in range(HEADS):
                            g = 32 * (hd % 4)
                            ins = mm(bk[0:32, hd * NS:(hd + 1) * NS], ident[:, g:g + 32], qpe[:, hd // 4, SEQ:T],
                                     start=True, stop=True)
                        done(ins, ("qp",))

                    if m == Z_GV + 1:
                        for n in range(3):
                            bk = begin(pe, L, ("vtok", n))
                            for i in range(2 if n < 2 else 1):
                                t = 2 * n + i
                                r = rows_of(t)
                                for j in range(2):
                                    after(pe, L, ("z", Z_GV + j, 1))
                                    ins = tr(bk[:r, i * 256 + j * P:i * 256 + (j + 1) * P], gv[:, j, t * P:t * P + r],
                                             ident)
                            done(ins, ("vtok", n))
                pe.wait_ge(S["kd_ready"], L + 1)
                bk = begin(pe, L, ("ktok", 0))
                for t in range(4):
                    ins = tr(bk[:, t * P:(t + 1) * P], kd[:, t * P:(t + 1) * P], ident)
                done(ins, ("ktok", 0))
                bk = begin(pe, L, ("ktok", 1))
                done(tr(bk[:NS, 0:P], kd[:, SEQ:T], ident), ("ktok", 1))
                after(pe, L, ("ktok", 0))
                after(pe, L, ("ktok", 1))
                for t in range(TT):
                    r = rows_of(t)
                    bk = begin(pe, L, ("delta", t))
                    for h in range(GH):
                        pe.wait_ge(S["gmsk_ready"], 4 * TT * L + 4 * t + h + 1)
                        ins = mm(bk[32 * h:32 * h + 32, :], ktok[:r, t, 32 * h:32 * h + 32], gmsk[:r, h % 2, :],
                                 start=True, stop=True)
                        if h < 3:
                            ins.then_inc(S["gmsk_used"], 1)
                    done(ins, ("delta", t))
                pe.wait_ge(S["qbd_ready"], L + 1)
                for g in range(3):
                    bk = begin(pe, L, ("inter", g))
                    n, cs = (16, range(16 * g, 16 * g + 16)) if g < 2 else (NQ, range(NCH, NCH + NB))
                    after(pe, L, ("delta", min(2 * g + 1, TT - 1)))
                    for i, c in enumerate(cs):
                        t0 = c * CH if g < 2 else SEQ + i * NQ
                        s = st[:, c, :] if g < 2 else st[:, c + 1, :]
                        width = 256 if g < 2 else NS
                        for hh in range(2):
                            out = bk[64 * hh:64 * hh + 64, 0:2 * width].rearrange("p (j n) -> p j n", j=2)
                            ins = mm(out[:, :, i * n:(i + 1) * n], s, qbd[:, hh:GH:2, t0:t0 + n],
                                     start=True, stop=True)
                    done(ins, ("inter", g))
                def offset_sums(d):
                    pe.wait_ge(S["w_ready"], CH * L + d + 1)
                    for j in range(2):
                        bk = begin(pe, L, ("dp", d, j))
                        n = NCH * (CH - d)
                        done(mm(bk[:, 0:n], cst[:, C_BM + j * P:C_BM + (j + 1) * P], gw[:, d % 2, 0:n],
                                start=True, stop=True), ("dp", d, j))
                    if d < NQ:
                        bk = begin(pe, L, ("ds", d))
                        n = NB * (NQ - d)
                        for j in range(2):
                            ins = mm(bk[:, j * NS:j * NS + n], cst[:, C_BM + j * P:C_BM + (j + 1) * P],
                                     gw[:, d % 2, SEQ:SEQ + n], start=True, stop=True)
                        done(ins, ("ds", d))

                def gla_norm_sums():
                    pe.wait_ge(S["gsq"], L + 1)
                    for j in range(2):
                        for h, cols in enumerate(halves):
                            bk = begin(pe, L, ("gnorm", j, h))
                            done(mm(bk[:, 0:HALF], blk64, gtmp[:, j, cols], start=True, stop=True), ("gnorm", j, h))


                pe.wait_ge(S["kperep"], L + 1)
                for hd in range(HEADS):
                    after(pe, L, ("qa", hd, 0))
                    after(pe, L, ("qa", hd, 1))
                after(pe, L, ("ctok", 0))
                after(pe, L, ("ctok", 1))
                after(pe, L, ("qp",))
                for s in range(ATT_STEPS):
                    for key in attention_order(s):
                        kind, hd = key[0], key[1]
                        bk = begin(pe, L, key)
                        if kind == "s":
                            i = key[2]
                            n, q, g = (i + 1) * P, slice(i * P, (i + 1) * P), slice(32 * (hd % 4), 32 * (hd % 4) + 32)
                            mm(bk[:, 0:n], qa[:, hd, q], ckvT[:, 0:n], start=True, stop=False)
                            mm(bk[:, 0:n], qpe[g, hd // 4, q], kpeT[g, 0:n], start=False, stop=False)
                            ins = mm(bk[:, i * P:n], idb, mask[:, M_CAUSAL:M_CAUSAL + P], start=False, stop=True)
                        elif kind == "pt":
                            i = key[2]
                            pe.wait_ge(S["prob_ready"], 4 * HEADS * L + 4 * hd + i + 1)
                            for j in range(i + 1):
                                ins = tr(bk[:, j * P:(j + 1) * P], prob[:, (4 * hd + i) % 2, j * P:(j + 1) * P], ident)
                        else:
                            for i in range(4):
                                after(pe, L, ("pt", hd, i))
                            for j in range(4):
                                ins = mm(bk[:, j * P:SEQ], ctok[:, j, :], pT[:, hd % 2, j, j * P:SEQ],
                                         start=j == 0, stop=j == 3, skip_group_check=True)
                        done(ins, key)
                    if s < CH:
                        offset_sums(s)
                    if s == GN_STEP:
                        gla_norm_sums()
                for p in range(4):
                    pe.wait_ge(page_in[p % 2], 16 * 2 * NPAGE * (2 * L + p // 2 + 1))
                    for k in range(3):
                        bk = begin(pe, L, ("ss", p, k))
                        for b2 in range(2):
                            b, out = 2 * p + b2, slice(64 * b2, 64 * b2 + 64)
                            n = 512 if k < 2 else NS
                            if k < 2:
                                four = pg[p % 2][:, b2, 4 * k:4 * k + 4, :]
                                c1, c2 = four[:, :, CKVT], four[0:32, :, KPET]
                            else:
                                c1, c2 = ckvT[:, SEQ:T], kpeT[0:32, SEQ:T]
                            mm(bk[out, 0:n], qas[:, b, :], c1, start=True, stop=False)
                            ins = mm(bk[out, 0:n], qp[0:32, b, :], c2, start=False, stop=k < 2)
                            if k == 2:
                                ins = mm(bk[out, 0:n], idb[:, 64 * b2:64 * b2 + 64],
                                         mask[:, M_SAMPLE + p * NS:M_SAMPLE + (p + 1) * NS], start=False, stop=True)
                        done(ins, ("ss", p, k))
                    pe.wait_ge(S["s_prob"], 4 * L + p + 1)
                    for k in range(3):
                        bk = begin(pe, L, ("sp", p, k))
                        if k < 2:
                            for j in range(4):
                                at = (4 * k + j) * P
                                ins = tr(bk[:, j * P:(j + 1) * P], sprob[:, at:at + P], ident)
                        else:
                            ins = tr(bk[:NS, 0:P], sprob[:, 1024:1088], ident)
                        done(ins, ("sp", p, k))
                    for k in range(3):
                        after(pe, L, ("sp", p, k))
                    bk = begin(pe, L, ("sv", p))
                    for b2 in range(2):
                        cols = slice(64 * b2, 64 * b2 + 64)
                        for j in range(NPAGE):
                            mm(bk[:, cols], pg[p % 2][:, b2, j, CKV], spT[:, j, cols], start=j == 0, stop=False)
                        ins = mm(bk[:, cols], ctok[:NS, 4, :], spT[:NS, 8, cols], start=False, stop=True)
                    done(ins, ("sv", p))
                pe.wait_ge(S["uv_in"], 16 * (L + 1))
                for jj in range(4):
                    bk = begin(pe, L, ("uv", jj))
                    for hh in range(2):
                        hd = 2 * jj + hh
                        after(pe, L, ("pv", hd))
                        ins = mm(bk[64 * hh:64 * hh + 64, :], uv[:, hd * VH:(hd + 1) * VH], qa[:, hd, :],
                                 start=True, stop=True)
                    done(ins, ("uv", jj))
                for p in range(4):
                    after(pe, L, ("sv", p))
                bk = begin(pe, L, ("uvs",))
                for hd in range(HEADS):
                    ins = mm(bk[64 * (hd % 2):64 * (hd % 2) + 64, NS * (hd // 2):NS * (hd // 2 + 1)],
                             uv[:, hd * VH:(hd + 1) * VH], qas[:, :, NQ * hd:NQ * (hd + 1)], start=True, stop=True)
                done(ins, ("uvs",))
                for g, (k0, k1) in enumerate(((0, 2), (2, 6), (6, 8))):
                    pe.wait_ge(S["osq_ready"], 8 * L + k1)
                    for h, cols in enumerate(halves):
                        bk = begin(pe, L, ("osum", g, h))
                        for k in range(k0, k1):
                            ins = mm(bk[:, 0:HALF], ones, osq[:, k, cols], start=k == k0, stop=k == k1 - 1)
                        done(ins, ("osum", g, h))
                pe.wait_ge(S["merged"], 8 * (L + 1))
                for n in range(2):
                    pe.wait_ge(wout_in[n], 16 * (L + 1))
                    for t in range(TT):
                        r = rows_of(t)
                        bk = begin(pe, L, ("wo", n, t))
                        for k in range(8):
                            ins = mm(bk[:r, :], merged[k][:, t * P:t * P + r], wout[n][:, k, :],
                                     start=k == 0, stop=k == 7)
                        done(ins, ("wo", n, t))

                transpose_rows(L, "hm", 2 * L + 1)
                pe.wait_ge(S["router_in"], 32 * (L + 1))
                bk = begin(pe, L, ("logits",))
                for t in range(TT):
                    r = rows_of(t)
                    after(pe, L, ("hm", t, 0))
                    after(pe, L, ("hm", t, 1))
                    for k in range(KT):
                        ins = mm(bk[:r, 36 * t:36 * t + 36], hT[:, k, t * P:t * P + r], wrt[:, 36 * k:36 * k + 36],
                                 start=k == 0, stop=k == KT - 1)
                done(ins, ("logits",))
                pe.wait_ge(S["sel_ready"], L + 1)
                bk = begin(pe, L, ("rank",))
                for t in range(TT):
                    r = rows_of(t)
                    for j in range(t):
                        mm(bk[:r, 32 * t:32 * t + 32], ones[:, 0:r], r_any[:, j, :], start=j == 0, stop=False)
                    mm(bk[:r, 32 * t:32 * t + 32], tri[:r, 0:r], r_any[:r, t, :], start=t == 0, stop=True)
                for j in range(TT):
                    r = rows_of(j)
                    ins = mm(bk[:, 160:192], ones[:r, :], r_any[:r, j, :], start=j == 0, stop=j == TT - 1)
                done(ins, ("rank",))
                bk = begin(pe, L, ("table",))
                for n in range(2 * TT):
                    r = rows_of(n // 2)
                    pe.wait_ge(S["pos_ready"], 2 * TT * L + n + 1)
                    ins = mm(bk[:, 0:TABLE], r_lo1[:r, n, :], r_hi1[:r, n, :], start=n == 0, stop=n == 2 * TT - 1)
                done(ins, ("table",))
                after(pe, L, ("table",))

                pe.wait_ge(S["route_ready"], L + 1)

                def rows_transpose(n):
                    pe.wait_ge(S["gathered"], n * 16)
                    for k in range(KT):
                        ins = tr(bank[k // 4][:, (k % 4) * P:(k % 4 + 1) * P], xg[:, k * P:(k + 1) * P], ident)
                    ins.then_inc(S["xg_used"], 1)

                before = pe.value_load(blocks[0:1, 66:67], min_val=0, max_val=DEPTH * MAXBLK)
                rows_transpose(before + L + 1)
                with pe.Fori(0, EXPERTS // RING) as g:
                    for s in range(RING):
                        count = pe.value_load(blocks[0:1, bass.ds(g * RING + s, 1)], min_val=1, max_val=TT)
                        ever = pe.value_load(blocks[0:1, bass.ds(g * RING + (66 + s), 1)], min_val=0,
                                             max_val=DEPTH * MAXBLK)
                        with pe.Fori(0, count) as c:
                            pe.wait_ge(wgu_in[s], (g + (EXPERTS // RING * L + 1)) * 32)
                            pe.wait_ge(S["xt_act"], ever + c + L + 1)
                            pe.wait_ge(S["xt_vec"], ever + c + L + 1)
                            for k in range(KT):
                                ins = mm(bank[2][:, :], xT[:, k, :], wgu[s][:, k, :], start=k == 0, stop=k == KT - 1)
                            ins.then_inc(S["gu_done"], 1)
                            rows_transpose(ever + c + L + 2)
                            pe.wait_ge(S["act_ready"], ever + c + 1)
                            for k in range(2):
                                ins = tr(bank[4][:, k * P:(k + 1) * P], act2[:, k * P:(k + 1) * P], ident)
                            ins.then_inc(S["at_done"], 1)
                            pe.wait_ge(S["actt_ready"], ever + c + 1)
                            pe.wait_ge(S["y_act"], ever + c + L + 1)
                            pe.wait_ge(S["y_vec"], ever + c + L + 1)
                            pe.wait_ge(wdn_in[s], (g + (EXPERTS // RING * L + 1)) * 16)
                            for n in range(2):
                                for k in range(2):
                                    ins = mm(bank[5 + n][:, :], actT[:, k, :], wdn[s][:, k, 512 * n:512 * n + 512],
                                             start=k == 0, stop=k == 1)
                            ins.then_inc(S["down_done"], 1)



_INS = ["x_prompt", "x_sample", "cst", "msk", "vecs", "norm1_g", "norm2_g", "final_norm_g", "win", "wq", "ukT", "w_uv",
        "wlru", "gla_wa2", "wrt", "rbias", "w_out", "w_gate", "w_up", "w_down",
        "cache", "page_table", "state_gla"]
_OUTS = {
    "y_prompt": (SEQ, D), "y_sample": (NS, D), "ckv": (DEPTH, P, T), "kpe": (DEPTH, ROPE, T),
    "conv": (DEPTH, P, 2, 27), "lru": (DEPTH, P, 2, 9), "gla_p": (DEPTH, P, GDV), "gla_s": (DEPTH, P, NB, GDV),
}


def lay_out(i):
    f = {k: np.asarray(v) for k, v in i.items()}
    cst, msk = constants()
    d = {k: f[k] for k in ("norm1_g", "norm2_g", "final_norm_g", "w_uv", "gla_wa2", "w_out", "w_gate", "w_up",
                           "w_down")}
    d["w_uv"] = d["w_uv"].reshape(DEPTH, P, HEADS * VH)
    d["x_prompt"] = f["x_prompt"].reshape(SEQ, D)
    d["x_sample"] = f["x_sample"].reshape(NS, D)
    d["cst"], d["msk"] = cst, msk

    def cols(v):
        return np.moveaxis(v.reshape(DEPTH, -1, P), 1, 2)

    d["vecs"] = np.concatenate([
        cols(f["conv_w"]), cols(f["conv_b"]), cols(f["lru_ba"]), cols(f["lru_bi"]), cols(f["lru_lambda"]),
        cols(f["q_norm_g"]), cols(f["kv_norm_g"]), cols(f["gla_ba"]),
        cols(np.tile(f["gla_norm_g"], (1, 2))), cols(f["out_norm_g"]),
        cols(f["state_conv"].reshape(DEPTH, NB, 3, 2, P).transpose(0, 3, 1, 2, 4)),
        cols(f["state_lru"].reshape(DEPTH, NB, 2, P).transpose(0, 2, 1, 3)),
    ], axis=2)
    w = f["w_in"]
    pad = np.zeros((DEPTH, D, P - 2 * ROPE - 16), np.float32)
    kpe = w[..., K_PE:K_PE + ROPE]
    w = np.concatenate([
        w[..., X_LRU:C_Q + 256], w[..., C_KV:C_KV + P],
        kpe, kpe[..., 16:], kpe[..., :16], w[..., G_A:G_A + 16], pad,
        w[..., G_Q:G_V + 256], w[..., G_O:G_O + 256]], axis=2)
    d["win"] = w.reshape(DEPTH, KT, P, ZT, P).transpose(0, 3, 2, 1, 4).reshape(DEPTH, ZT, P, KT * P)
    q = f["w_uq"].reshape(DEPTH, 2, P, HEADS, NOPE + ROPE)
    pe = q[..., NOPE:]
    rot = np.concatenate([pe[..., 16:], pe[..., :16]], axis=-1)
    d["wq"] = np.concatenate([v.reshape(DEPTH, 2, P, -1) for v in (q[..., :NOPE], pe, rot)], axis=3) \
        .transpose(0, 2, 1, 3).reshape(DEPTH, P, 2048)
    d["ukT"] = f["w_uk"].transpose(0, 2, 3, 1).reshape(DEPTH, 4, P, P).transpose(0, 2, 1, 3).reshape(DEPTH, P, 512)
    bd = np.zeros((DEPTH, P, 2, 2, P), np.float32)
    for g, name in enumerate(("lru_wa", "lru_wi")):
        for n in range(4):
            r = slice(64 * (n % 2), 64 * (n % 2) + 64)
            bd[:, r, g, n // 2, r] = f[name][:, n]
    d["wlru"] = bd.reshape(DEPTH, P, 512)
    wr = np.concatenate([f["router_wg"], f["router_we"]], axis=2)
    d["wrt"] = wr.reshape(DEPTH, KT, P, 36).transpose(0, 2, 1, 3).reshape(DEPTH, P, KT * 36)
    d["rbias"] = np.concatenate([f["router_bg"], f["router_be"]], axis=1)
    cache = np.zeros(f["cache_ckv"].shape[:3] + (3 * P,), np.float32)
    cache[..., 0:P] = f["cache_ckv"]
    cache[..., P:2 * P] = f["cache_ckv"].transpose(0, 1, 3, 2)
    cache[:, :, 0:ROPE, 2 * P:] = f["cache_kpe"].transpose(0, 1, 3, 2)
    d["cache"] = cache
    d["page_table"] = f["page_table"].reshape(1, NB * NPAGE)
    d["state_gla"] = f["state_gla"].transpose(0, 2, 3, 1, 4).reshape(DEPTH, P, NB, GDV)
    return {k: np.ascontiguousarray(d[k]) for k in _INS}


def hand_back(r):
    y, ckv, kpe = r["y_prompt"].reshape(1, SEQ, D), r["ckv"].transpose(0, 2, 1), r["kpe"].transpose(0, 2, 1)
    conv = r["conv"].transpose(0, 3, 2, 1).reshape(DEPTH, 27, 256)
    lru = r["lru"].transpose(0, 3, 2, 1).reshape(DEPTH, 9, 256)
    return (
        y, r["y_sample"].reshape(NB, NQ, D),
        ckv[:, None, :SEQ], kpe[:, None, :SEQ],
        ckv[:, SEQ:].reshape(DEPTH, NB, NQ, P), kpe[:, SEQ:].reshape(DEPTH, NB, NQ, ROPE),
        conv[:, None, :3], conv[:, 3:].reshape(DEPTH, NB, 3, 256),
        lru[:, None, 0], lru[:, 1:],
        r["gla_p"].reshape(DEPTH, 1, GH, GDK, GDV),
        r["gla_s"].reshape(DEPTH, GH, GDK, NB, GDV).transpose(0, 3, 1, 2, 4),
    )


def kernel(**inputs):
    import concourse.bacc as bacc
    from concourse.bass_utils import run_bass_kernel_spmd

    nc = bacc.Bacc("TRN2", target_bir_lowering=False, num_devices=1)
    arrays = lay_out(inputs)
    a = {n: nc.dram_tensor(f"in_{n}", v.shape, mybir.dt.from_np(v.dtype), kind="ExternalInput").ap()
         for n, v in arrays.items()}
    o = {n: nc.dram_tensor(f"out_{n}", s, F32, kind="ExternalOutput").ap() for n, s in _OUTS.items()}
    hybrid_step(nc, a, o)
    r = run_bass_kernel_spmd(nc, [{f"in_{n}": v for n, v in arrays.items()}], core_ids=[0])
    return hand_back({n: r.results[0][f"out_{n}"] for n in _OUTS})
```

```python
from contextlib import ExitStack

import numpy as np

import concourse.bass as bass
from concourse import mybir

F32 = mybir.dt.float32
BF16 = mybir.dt.bfloat16
I32 = mybir.dt.int32
U32 = mybir.dt.uint32
ALU = mybir.AluOpType
ACT = mybir.ActivationFunctionType
AX_X = mybir.AxisListType.X

P = 128
DEPTH, D, SEQ, NB, NQ = 2, 1024, 512, 8, 8
NS = NB * NQ
T = SEQ + NS
TT = 5
KT = D // P
HALF = T // 2
PAGE, NPAGE = 128, 8
HEADS, NOPE, ROPE, VH = 8, 64, 32, 64
GH, GDK, GDV, CH = 4, 32, 64, 16
NCH = SEQ // CH
EXPERTS, GROUPS, EPG, DE = 32, 4, 8, 256
EPS = 1e-6
SCALE = float(NOPE + ROPE) ** -0.5
NEG = -1e30
RING = 4
MAXBLK = EXPERTS + 8
TABLE = MAXBLK + TT + 1
XE = 3 + SEQ
SEXT = NQ + 3
HE = SEQ + NB * (NQ + 1)

_o = np.cumsum([0, 256, 256, 256, 128, 32, 128, 128, 256, 16, 256])
X_LRU, Y_LRU, C_Q, C_KV, K_PE, G_Q, G_K, G_V, G_A, G_O = (int(v) for v in _o[:10])
ZT = 14
Z_X, Z_Y, Z_CQ, Z_CKV, Z_PE, Z_GQ, Z_GK, Z_GV, Z_GO = 0, 2, 4, 6, 7, 8, 9, 10, 12
Z_ORDER = [4, 5, 6, 7, 0, 1, 2, 3, 8, 9, 10, 11, 12, 13]
ATT_STEPS = HEADS * 4 + 3
DP_STEPS = [TT + 1 + d + d // 12 for d in range(CH)]
SAMPLE_STEP = 27
SAMPLE_ORDER = (("scores", 1), ("scores", 2), ("values", 1), ("values", 2), ("scores", 3), ("values", 3))
GN_STEP = DP_STEPS[-1] + 2


def rows_of(t):
    return P if t < TT - 1 else NS


C_ID, C_TRI, C_ONE, C_BLK, C_BM = 0, 128, 256, 384, 512
C_COS, C_SIN, C_IOTA, C_CM, C_QM, C_TOK, C_RST = 768, 1344, 1920, 2048, 2064, 2068, 2073
C_END = 2073 + T
M_CAUSAL, M_SAMPLE, M_ID = 0, 128, 384
M_END = 512
V_CW, V_CB, V_BA, V_BI, V_LAM, V_QN, V_KN, V_GB, V_GN, V_ON, V_SC, V_SL = (
    0, 8, 10, 12, 14, 16, 18, 19, 20, 21, 29, 77)
V_END = 93


def constants():
    c = np.zeros((P, C_END), np.float32)
    i = np.arange(P)
    c[:, C_ID:C_ID + P] = np.eye(P)
    c[:, C_TRI:C_TRI + P] = i[:, None] < i[None, :]
    c[:, C_ONE:C_ONE + P] = 1.0
    c[:, C_BLK:C_BLK + P] = (i[:, None] // GDV) == (i[None, :] // GDV)
    for j in range(2):
        head = 2 * j + i // GDV
        c[:, C_BM + j * P:C_BM + (j + 1) * P] = (i[:, None] // GDK == head[None, :]) * GDK ** -0.5
    pos = np.concatenate([np.arange(SEQ), np.tile(PAGE * NPAGE + np.arange(NQ), NB)]).astype(np.float32)
    half = ROPE // 2
    inv = (np.float32(10000.0) ** (-np.arange(half, dtype=np.float32) / half)).astype(np.float32)
    ang = pos[None, :] * inv[i % half][:, None]
    sign = np.where(i % ROPE < half, -1.0, 1.0)[:, None]
    c[:, C_COS:C_COS + T] = np.cos(ang)
    c[:, C_SIN:C_SIN + T] = np.sin(ang) * sign
    c[:, C_IOTA:C_IOTA + P] = i[None, :]
    c[:, C_CM:C_CM + 8] = i[:, None] // CH == np.arange(8)[None, :]
    c[:, C_CM + 8:C_CM + 16] = i[:, None] // NQ == np.arange(8)[None, :]
    c[:, C_QM:C_QM + GH] = (i[:, None] // GDK == np.arange(GH)[None, :]) * GDK ** -0.5
    c[:, C_TOK:C_TOK + TT] = i[:, None] + P * np.arange(TT)[None, :]
    c[:, C_RST:C_RST + T] = 1.0
    c[:, C_RST:C_RST + SEQ:CH] = 0.0
    c[:, C_RST + SEQ:C_RST + T:NQ] = 0.0
    m = np.zeros((P, M_END), np.float32)
    m[:, M_CAUSAL:M_CAUSAL + P] = np.where(i[None, :] <= i[:, None], 0.0, NEG)
    b2, q = i // 64, i % NQ
    for p in range(4):
        kb, kk = np.arange(NS) // NQ, np.arange(NS) % NQ
        ok = (kb[None, :] == (2 * p + b2)[:, None]) & (kk[None, :] <= q[:, None])
        m[:, M_SAMPLE + p * NS:M_SAMPLE + (p + 1) * NS] = np.where(ok, 0.0, NEG)
    m[:, M_ID:M_ID + P] = np.eye(P)
    return c, m


def attention_order(s):
    ahead, n = 2, HEADS * 4
    if s < n:
        yield ("s", s // 4, s % 4)
    if ahead <= s < n + ahead:
        yield ("pt", (s - ahead) // 4, (s - ahead) % 4)
    if s > ahead and (s - ahead) % 4 == 0:
        yield ("pv", (s - ahead) // 4 - 1)


def psum_plan():
    keys = [("hn", t, g) for t in range(TT) for g in range(2)]
    for m in Z_ORDER:
        keys += [("z", m, h) for h in range(2)]
        if m == Z_X + 1:
            keys += [("qsum", 0), ("qsum", 1), ("kvsum", 0), ("kvsum", 1)]
            keys += [("gate", 0, k) for k in range(3)]
        if m == Z_Y + 1:
            keys += [("q", j, h) for j in range(4) for h in range(2)]
            keys += [(kind, g, h) for g in range(2) for h in range(2) for kind in ("pe", "rot")]
            keys += [("gate", 1, k) for k in range(3)]
            keys += [("alpha", h) for h in range(2)]
            keys += [("qa", hd, h) for hd in range(HEADS) for h in range(2)]
            keys += [("ctok", 0), ("ctok", 1), ("qp",)]
        if m == Z_GV + 1:
            keys += [("vtok", n) for n in range(3)]
    keys += [("ktok", n) for n in range(2)]
    for s in range(ATT_STEPS):
        keys += list(attention_order(s))
        if s < TT:
            keys += [("delta", s)]
        if s == TT:
            keys += [("inter", g) for g in range(3)]
        if s == SAMPLE_STEP:
            keys += [("ss", 0, k) for k in range(3)]
        if s == SAMPLE_STEP + 3:
            keys += [("sp", 0, k) for k in range(3)] + [("sv", 0)]
        if s in DP_STEPS:
            d = DP_STEPS.index(s)
            keys += [("dp", d, 0), ("dp", d, 1)]
            if d < NQ:
                keys += [("ds", d)]
        if s == GN_STEP:
            keys += [("gnorm", j, h) for j in range(2) for h in range(2)]
    for kind, p in SAMPLE_ORDER:
        keys += [("ss", p, k) for k in range(3)] if kind == "scores" else [("sp", p, k) for k in range(3)] + [("sv", p)]
    keys += [("uv", jj) for jj in range(4)] + [("uvs",)]
    keys += [("osum", k, h) for k in range(3) for h in range(2)]
    keys += [("wo", n, t) for n in range(2) for t in range(TT)]
    keys += [("hm", t, g) for t in range(2) for g in range(2)] + [("logits",)]
    keys += [("hm", t, g) for t in range(2, TT) for g in range(2)]
    keys += [("rank",), ("table",)]
    return keys


def hybrid_step(nc, a, o):
    plan = psum_plan()
    place = {k: (n % 8, n // 8) for n, k in enumerate(plan)}
    assert len(place) == len(plan)
    uses = [sum(1 for b, _ in place.values() if b == k) for k in range(8)]

    with ExitStack() as ctx:
        def sb(name, shape, dt=F32):
            return ctx.enter_context(nc.sbuf_tensor(name, shape, dt))

        def sem(name):
            return ctx.enter_context(nc.semaphore(name))

        cst = sb("cst", [P, C_END])
        mask = sb("mask", [P, M_END], BF16)
        x = sb("x", [P, TT, D])
        vec = sb("vec", [P, V_END])
        sm = sb("sm", [P, 220])
        wlru = sb("wlru", [P, 4 * P])
        wa2 = sb("wa2", [P, P])
        wrt = sb("wrt", [P, KT * 36])
        rbias = sb("rbias", [P, 36])
        ra = sb("ra", [P, 4608])
        rb = sb("rb", [P, 4096])
        re = sb("re", [P, 15616])
        rf = sb("rf", [P, 5280])
        rg = sb("rg", [P, 12288])
        pages = sb("pages", [1, NB * NPAGE], I32)
        blocks = sb("blocks", [1, 128], I32)
        slots = sb("slots", [P, TABLE], U32)
        slot_now = sb("slot_now", [P, 1], U32)
        pos = sb("pos", [P, 2 * TT], U32)

        bank = [ctx.enter_context(nc.psum_tensor(f"bank{b}", [P, 512], F32)) for b in range(8)]

        ident, tri, ones, blk64 = (cst[:, k:k + P] for k in (C_ID, C_TRI, C_ONE, C_BLK))
        cos, sin = cst[:, C_COS:C_COS + T], cst[:, C_SIN:C_SIN + T]
        iota = cst[:, C_IOTA:C_IOTA + P]
        idb = mask[:, M_ID:M_ID + P]

        def cut(region, at, *dims):
            n = int(np.prod(dims))
            v = region[:, at:at + n]
            if len(dims) == 1:
                return v
            names = "abcd"[:len(dims)]
            return v.rearrange(f"p ({' '.join(names)}) -> p {' '.join(names)}",
                               **{k: d for k, d in zip(names, dims)})

        hT = cut(ra, 0, KT, T)
        pT = cut(ra, 0, 2, 4, 512)
        xg = cut(ra, 0, D)
        ysb = cut(ra, 1024, D)
        win = cut(rb, 0, 4, KT, P)
        wout = [cut(rb, 0, KT, 512), cut(ra, 0, KT, 512)]
        xT = cut(rb, 0, KT, P)
        act1 = cut(rb, 1024, DE)
        act2 = cut(rb, 1280, DE)
        actT = cut(rb, 1536, 2, P)
        cq = cut(re, 0, 2, T)
        wq = cut(re, 1152, 2, 1024)
        gw = cut(re, 0, 2, T)
        gdiff = cut(re, 1152, 2, T)
        la = cut(re, 2304, T)
        ckvT = cut(re, 3200, T)
        kpeT = cut(re, 3776, T)
        qn = cut(re, 4352, 4, T)
        gmsk = [cut(re, 4352, 512), cut(re, 4864, 512), cut(rg, 5760, 512), cut(rg, 6272, 512)]
        ktok = cut(re, 5376, TT, P)
        gsout = cut(re, 6016, NB, GDV)
        outB = cut(re, 4352, 4, T)
        qpe = cut(re, 6656, 2, T)
        qa = cut(re, 7808, HEADS, SEQ)
        qas = cut(re, 7808 + HEADS * SEQ, NB, 64)
        sq = cut(re, 7808, 3, T)
        rsq = cut(re, 9536, 2, T)
        ctok = cut(re, 12416, TT, P)
        qp = cut(re, 13056, NB, 64)
        ukT = cut(re, 13568, 4, P)
        uv = cut(re, 14080, HEADS * VH)
        prob = cut(re, 14592, 2, 512)
        xs = cut(re, 12416, 2, D)
        gain = cut(re, 14464, D)
        xext = cut(rf, 0, 2, XE + NB * SEXT)
        yl = cut(rf, 1206, 2, T)
        outA = yl
        lru = [cut(rf, 2358 + k * HE, HE) for k in range(5)]
        gtmp = cut(rf, 2358, 2, T)
        ygat = cut(re, 0, 2 * TT, D)
        gq, gk, gv = cut(rg, 0, T), cut(rg, 576, T), cut(rg, 1152, 2, T)
        cum = cut(rg, 2304, T)
        qbd = cut(rg, 2880, GH, T)
        kd = cut(rg, 5184, T)
        oacc = cut(rg, 2880, 2, T)
        vtok = cut(rg, 6912, TT, 256)
        st = cut(rg, 8192, NCH + 1 + NB, GDV)
        gout = cut(rf, 0, 2, T)
        outC = gtmp
        pg = [cut(rg, 6144 * k, 2, NPAGE, 3 * P) for k in (1, 0)]
        CKV, CKVT, KPET = slice(0, P), slice(P, 2 * P), slice(2 * P, 3 * P)
        sprob = cut(re, 4352, 1088)
        spT = cut(re, 5440, 9, P)
        osq = cut(rg, 0, 8, T)
        ors = cut(rg, 4608, 3, T)
        slot_at = [(rg, 0), (rg, 6144), (re, 0), (re, 6144)]
        wgu = [cut(r, at, KT, 512) for r, at in slot_at]
        wdn = [cut(r, at + 4096, 2, D) for r, at in slot_at]

        h_rows = nc.dram_tensor("h_rows", (T, D), F32).ap()
        y_rows = nc.dram_tensor("y_rows", (TABLE * P, D), F32).ap()

        full = [sem(f"bank{b}_full") for b in range(8)]
        read = [sem(f"bank{b}_read") for b in range(8)]
        names = """const_in mask_in mask_cast vec_in gain_in wq_in uk_in uv_in wlru_in wa2_in gstate_in router_in
            ctail_out lru_out ckv_out kpe_out gla_out xs_ready ssq_ready q_ready ckv_ready kpe_ready sq_ready
            pads_ready conv_ready lru_steps r_ready a_ready coef_ready la_ready cum_ready kd_ready qbd_ready
            gmsk_ready gmsk_used diff_ready exp_ready w_ready gn_ready out_c max_ready prob_ready s_max s_prob
            merged osq_ready ors_ready route_ready sel_ready gathered xg_used xt_act xt_vec gu_done silu_done
            act_ready at_done actt_ready down_done y_act y_vec y_stored combined ygat_used pos_ready
            vector_steps scalar_steps final_ready table_ready slot_copied lru_saved lnexp tailsaved kperep
            qpe_ready gelu gexp oacc_ready oacc_steps gsq out_b sel_exp sel_exp_done zeros_ready held gate_done""".split()
        S = {n: sem(n) for n in names}
        win_in = [sem(f"win{k}_in") for k in range(4)]
        page_in = [sem(f"page{k}_in") for k in range(2)]
        wout_in = [sem(f"wout{k}_in") for k in range(2)]
        wgu_in = [sem(f"wgu{k}_in") for k in range(RING)]
        wdn_in = [sem(f"wdn{k}_in") for k in range(RING)]

        block = ctx.enter_context(nc.Block())

        def begin(pe, L, key):
            b, n = place[key]
            if L * uses[b] + n > 0:
                pe.wait_ge(read[b], L * uses[b] + n)
            return bank[b]

        def done(ins, key):
            ins.then_inc(full[place[key][0]], 1)

        def take(eng, L, key):
            b, n = place[key]
            eng.wait_ge(full[b], L * uses[b] + n + 1)
            return bank[b]

        def give(ins, key):
            ins.then_inc(read[place[key][0]], 1)

        def after(eng, L, key):
            b, n = place[key]
            eng.wait_ge(read[b], L * uses[b] + n + 1)

        def steps(eng, name):
            count = [0]

            def link(ins):
                count[0] += 1
                ins.then_inc(S[name], 1)
                eng.wait_ge(S[name], count[0])
            return link

        halves = [slice(0, HALF), slice(HALF, T)]

        gaT = cut(re, 14592, T)
        ropetmp = cut(re, 14592 + T, HALF)
        eps_col = sm[:, 210:211]
        merged = [outA[:, 0, :], outA[:, 1, :]] + [outB[:, k, :] for k in range(4)] + [outC[:, 0, :], outC[:, 1, :]]
        x_in = [sem(f"x{t}_in") for t in range(TT)]
        rows_out = [sem(f"rows_out{k}") for k in range(2)]
        y_out = [sem(f"y_out{k}") for k in range(2)]
        ygat_in = [sem(f"ygat_in{k}") for k in range(2 * TT)]
        WUSES = [sum(1 for n in range(ZT) if n % 4 == k) for k in range(4)]
        xs2 = [xs[:, 0, :], xs[:, 1, :], cut(rf, 0, D), cut(rf, 3510, D), cut(rf, 1206, D)]
        acc = [0]
        r_log = cut(rb, 0, TT, 36)
        r_g, r_g8, r_e, r_e8, r_part = (cut(rb, 180 + 40 * k, TT, 8) for k in range(5))
        r_gi, r_ei = (cut(rb, 380 + 40 * k, TT, 8).bitcast(U32) for k in range(2))
        r_gid, r_sum, r_two = (cut(rb, 460 + 5 * k, TT) for k in range(3))
        r_eid = cut(rb, 475, TT, 2)
        r_gone = cut(rb, 485, TT, GROUPS)
        r_diff = cut(rb, 505, TT, GROUPS + 1)
        r_any, r_rank, r_hi = (cut(rb, 530 + 160 * k, TT, EXPERTS) for k in range(3))
        r_h2, r_l2 = (cut(rb, 1010 + 10 * k, 2 * TT) for k in range(2))
        r_nb = cut(rb, 1062, EXPERTS)
        r_tot = cut(rb, 3590, TT, EXPERTS)
        r_tab = cut(rb, 1094, 99)
        r_sel, r_prod = (cut(rb, 1200 + 320 * k, TT, 2, EXPERTS) for k in range(2))
        r_lo1 = cut(rb, 1840, 2 * TT, P)
        r_hi1 = cut(rb, 3120, 2 * TT, TABLE)

        def xs_free(eng, n, t):
            if n < 2 * DEPTH and n % 2 == 0 and t >= 2:
                take(eng, n // 2, ("hn", t - 2, 1))
            if n % 2 == 1 and n > 1:
                eng.wait_ge(rows_out[t % 2], 16 * (n // 2) * (3 if t % 2 == 0 else 2))
            if n == 2 * DEPTH and t >= 2:
                eng.wait_ge(y_out[t % 2], 16 * (t // 2))

        def normed(n, t):
            return xs2[t] if n % 2 == 1 else xs[:, t % 2, :]

        def x_done(eng, n, t):
            if n % 2 == 1:
                after(eng, n // 2, ("wo", 0, t))
                after(eng, n // 2, ("wo", 1, t))
            elif n > 0:
                eng.wait_ge(S["combined"], TT * (n // 2 - 1) + t + 1)

        def absorbed_query(eng, copy, L, hd, h):
            bk, key = take(eng, L, ("qa", hd, h)), ("qa", hd, h)
            if h == 0:
                give(copy(qa[:, hd, 0:HALF], bk[:, 0:HALF]), key)
            else:
                copy(qa[:, hd, HALF:SEQ], bk[:, 0:SEQ - HALF])
                give(copy(qas[:, :, NQ * hd:NQ * (hd + 1)],
                          bk[:, SEQ - HALF:HALF].rearrange("p (b q) -> p b q", q=NQ)), key)

        @block.sync
        def _(sp):
            for t in range(TT):
                src = a["x_prompt"][t * P:(t + 1) * P, :] if t < 4 else a["x_sample"]
                sp.dma_start(x[:rows_of(t), t, :], src).then_inc(x_in[t], 16)
                if t == 0:
                    sp.dma_start(gain, a["norm1_g"][0:1, :].to_broadcast([P, D])).then_inc(S["gain_in"], 16)
                if t == 1:
                    sp.dma_start(cst[:, :], a["cst"]).then_inc(S["const_in"], 16)
                    sp.dma_start(rf[:, 0:M_END], a["msk"]).then_inc(S["mask_in"], 16)
            sp.dma_start(pages[:, :], a["page_table"]).then_inc(S["mask_in"], 16)

            def load_gain(n, row):
                if n > 0:
                    sp.wait_ge(S["xs_ready"], TT * n)
                sp.dma_start(gain, row.to_broadcast([P, D])).then_inc(S["gain_in"], 16)

            for L in range(DEPTH):
                if L > 0:
                    sp.wait_ge(S["combined"], TT * (L - 1) + 1)
                    load_gain(2 * L, a["norm1_g"][L:L + 1, :])
                sp.dma_start(vec[:, :], a["vecs"][L]).then_inc(S["vec_in"], 16)
                for n, m in enumerate(Z_ORDER):
                    if n >= 4:
                        take(sp, L, ("z", Z_ORDER[n - 4], 1))
                    sp.dma_start(cut(rb, (n % 4) * 1024, 1024), a["win"][L, m]).then_inc(win_in[n % 4], 16)
                    if n == 4:
                        sp.dma_start(cut(re, 13568, 512), a["ukT"][L]).then_inc(S["uk_in"], 16)
                        sp.dma_start(uv, a["w_uv"][L]).then_inc(S["uv_in"], 16)
                    if n == 3:
                        if L > 0:
                            sp.wait_ge(S["combined"], TT * L)
                        sp.dma_start(cut(re, 1152, 2048), a["wq"][L]).then_inc(S["wq_in"], 16)
                        sp.dma_start(wlru[:, :], a["wlru"][L]).then_inc(S["wlru_in"], 16)
                        sp.dma_start(wa2[64:80, :], a["gla_wa2"][L]).then_inc(S["wa2_in"], 16)
                        sp.dma_start(st[:, NCH + 1:NCH + 1 + NB, :], a["state_gla"][L]).then_inc(S["gstate_in"], 16)
                        sp.dma_start(wrt[:, :], a["wrt"][L]).then_inc(S["router_in"], 16)
                        sp.dma_start(rbias[:, :], a["rbias"][L:L + 1, :].to_broadcast([P, 36])) \
                            .then_inc(S["router_in"], 16)
                take(sp, L, ("z", Z_ORDER[-1], 1))
                wo_rows = a["w_out"][L].rearrange("(k p) n -> p k n", p=P)
                sp.dma_start(wout[0], wo_rows[:, :, 0:512]).then_inc(wout_in[0], 16)
                take(sp, L, ("inter", 2))
                sp.wait_ge(S["gla_out"], 32 * (L + 1))
                if L == 0:
                    sp.wait_ge(S["y_stored"], 16)
                for p in range(4):
                    page = [sp.value_load(pages[0:1, col:col + 1], min_val=0, max_val=a["cache"].shape[1] - 1)
                            for col in range(2 * p * NPAGE, 2 * (p + 1) * NPAGE)]
                    if p == 1:
                        sp.wait_ge(S["out_c"], L + 1)
                    if p > 1:
                        take(sp, L, ("sv", p - 2))
                    for n in range(2 * NPAGE):
                        sp.dma_start(pg[p % 2][:, n // NPAGE, n % NPAGE, :],
                                     a["cache"][L, bass.ds(page[n], 1)].rearrange("a p n -> (a p) n")) \
                            .then_inc(page_in[p % 2], 16)
                    if p == 3:
                        take(sp, L, ("pv", HEADS - 1))
                        sp.dma_start(wout[1], wo_rows[:, :, 512:1024]).then_inc(wout_in[1], 16)
                take(sp, L, ("uvs",))
                load_gain(2 * L + 1, a["norm2_g"][L:L + 1, :])

                def load_expert(e, s):
                    for half, w in enumerate((a["w_gate"], a["w_up"])):
                        sp.dma_start(wgu[s][:, :, half * DE:(half + 1) * DE],
                                     w[L, e].rearrange("(k p) f -> p k f", p=P)
                                     if isinstance(e, int) else
                                     w[L, bass.ds(e, 1)].rearrange("a (k p) f -> p (a k) f", p=P)) \
                            .then_inc(wgu_in[s], 16)
                    sp.dma_start(wdn[s], a["w_down"][L, e].rearrange("(k p) d -> p k d", p=P)
                                 if isinstance(e, int) else
                                 a["w_down"][L, bass.ds(e, 1)].rearrange("a (k p) d -> p (a k) d", p=P)) \
                        .then_inc(wdn_in[s], 16)

                sp.wait_ge(S["merged"], 8 * (L + 1))
                load_expert(0, 0)
                take(sp, L, ("wo", 1, TT - 1))
                for s in range(1, RING):
                    load_expert(s, s)
                sp.wait_ge(S["route_ready"], L + 1)
                with sp.Fori(1, EXPERTS // RING) as g:
                    for s in range(RING):
                        over = sp.value_load(blocks[0:1, bass.ds(g * RING + (66 + s - RING + 1), 1)],
                                             min_val=1, max_val=DEPTH * MAXBLK)
                        sp.wait_ge(S["down_done"], over)
                        load_expert(g * RING + s, s)
            load_gain(2 * DEPTH, a["final_norm_g"].rearrange("(a d) -> a d", a=1))
            for t in range(TT):
                r = rows_of(t)
                sp.wait_ge(S["xs_ready"], TT * 2 * DEPTH + t + 1)
                dst = o["y_prompt"][t * P:(t + 1) * P, :] if t < 4 else o["y_sample"]
                sp.dma_start(dst, xs[:r, t % 2, :]).then_inc(y_out[t % 2], 16)
            sp.wait_ge(y_out[0], 48)
            sp.wait_ge(y_out[1], 32)
            for n in ("ckv_out", "kpe_out", "ctail_out", "lru_out"):
                sp.wait_ge(S[n], 16 * DEPTH)
            sp.wait_ge(S["gla_out"], 32 * DEPTH)

        @block.gpsimd
        def _(pool):
            pool.wait_ge(S["mask_in"], 32)
            nc.gpsimd.tensor_copy(mask[:, :], rf[:, 0:M_END]).then_inc(S["mask_cast"], 1)
            pool.wait_ge(S["mask_cast"], 1)
            nc.gpsimd.memset(rg[:, 11136:11136 + D], 0.0).then_inc(S["zeros_ready"], 1)
            for L in range(DEPTH):
                if L > 0:
                    pool.wait_ge(S["combined"], TT * L)
                pool.wait_ge(S["vec_in"], 16 * (L + 1))
                nc.gpsimd.memset(xext[:, :, 0:3], 0.0)
                for t in range(2):
                    nc.gpsimd.tensor_copy(
                        xext[:, t, XE:].rearrange("p (b c) -> p b c", c=SEXT)[:, :, 0:3],
                        vec[:, V_SC + 24 * t:V_SC + 24 * t + 24].rearrange("p (b k) -> p b k", k=3))
                nc.gpsimd.memset(st[:, 0, :], 0.0)
                for k in (0, 1, 2):
                    last = nc.gpsimd.memset(lru[k][:, SEQ::NQ + 1], 0.0)
                last.then_inc(S["pads_ready"], 1)
                tail = sm[:, 130:184].rearrange("p (t c) -> p t c", t=2)
                if L > 0:
                    pool.wait_ge(S["ctail_out"], 16 * L)
                for t in range(2):
                    after(pool, L, ("z", Z_X + t, 0))
                    after(pool, L, ("z", Z_X + t, 1))
                    nc.gpsimd.tensor_copy(tail[:, t, 0:3], xext[:, t, XE - 3:XE])
                    last = nc.gpsimd.tensor_copy(
                        tail[:, t, 3:27].rearrange("p (b k) -> p b k", k=3),
                        xext[:, t, XE:].rearrange("p (b c) -> p b c", c=SEXT)[:, :, NQ:SEXT])
                last.then_inc(S["tailsaved"], 1)
                pool.wait_ge(S["tailsaved"], L + 1)
                pool.dma_start(o["conv"][L].rearrange("p t c -> p (t c)"), sm[:, 130:184]) \
                    .then_inc(S["ctail_out"], 16)
                pool.wait_ge(S["ckv_ready"], 2 * (L + 1))
                pool.dma_start(o["ckv"][L], ckvT).then_inc(S["ckv_out"], 16)
                pool.wait_ge(S["kpe_ready"], 2 * (L + 1))
                pool.dma_start(o["kpe"][L], kpeT[0:ROPE, :]).then_inc(S["kpe_out"], 16)
                pool.wait_ge(S["lru_saved"], 2 * (L + 1))
                pool.dma_start(o["lru"][L].rearrange("p t c -> p (t c)"), sm[:, 110:128]) \
                    .then_inc(S["lru_out"], 16)

                cumP = cum[:, 0:SEQ].rearrange("p (c n) -> p c n", n=CH)
                cumS = cum[:, SEQ:T].rearrange("p (c n) -> p c n", n=NQ)
                pool.wait_ge(S["cum_ready"], L + 1)
                nc.gpsimd.tensor_tensor(gdiff[:, 0, 0:SEQ].rearrange("p (c n) -> p c n", n=CH),
                                        cumP[:, :, CH - 1:CH].to_broadcast([P, NCH, CH]), cumP, ALU.subtract)
                nc.gpsimd.tensor_tensor(gdiff[:, 0, SEQ:T].rearrange("p (c n) -> p c n", n=NQ),
                                        cumS[:, :, NQ - 1:NQ].to_broadcast([P, NB, NQ]), cumS, ALU.subtract) \
                    .then_inc(S["diff_ready"], 1)
                for n in range(4 * TT):
                    t, h = n // 4, n % 4
                    r, cm = rows_of(t), C_CM + (8 if t == TT - 1 else 0)
                    if h == 0 and t % 2 == 0:
                        after(pool, L, ("vtok", t // 2))
                    if n >= 4:
                        was = n - 4
                        if was % 4 == 3:
                            take(pool, L, ("delta", was // 4))
                        else:
                            pool.wait_ge(S["gmsk_used"], 3 * TT * L + 3 * (was // 4) + was % 4 + 1)
                    nc.gpsimd.tensor_tensor(
                        gmsk[n % 4][:r, :].rearrange("p (c e) -> p c e", c=8),
                        vtok[:r, t, h * GDV:(h + 1) * GDV].unsqueeze(1).to_broadcast([r, 8, GDV]),
                        cst[:r, cm:cm + 8].unsqueeze(2).to_broadcast([r, 8, GDV]), ALU.mult) \
                        .then_inc(S["gmsk_ready"], 1)
                after(pool, L, ("delta", TT - 1))
                pool.dma_start(o["gla_p"][L], st[:, NCH, :]).then_inc(S["gla_out"], 16)
                pool.dma_start(o["gla_s"][L], gsout).then_inc(S["gla_out"], 16)
                for d in range(1, CH):
                    if d >= 3:
                        pool.wait_ge(S["w_ready"], CH * L + d - 1)
                    else:
                        pool.wait_ge(S["kd_ready"], L + 1)
                    n = CH - d
                    last = nc.gpsimd.tensor_tensor(
                        gdiff[:, d % 2, 0:NCH * n].rearrange("p (c n) -> p c n", n=n),
                        cumP[:, :, d:CH], cumP[:, :, 0:n], ALU.subtract)
                    if d < NQ:
                        n = NQ - d
                        last = nc.gpsimd.tensor_tensor(
                            gdiff[:, d % 2, SEQ:SEQ + NB * n].rearrange("p (c n) -> p c n", n=n),
                            cumS[:, :, d:NQ], cumS[:, :, 0:n], ALU.subtract)
                    last.then_inc(S["diff_ready"], 1)

                for t in range(TT):
                    r = rows_of(t)
                    pool.wait_ge(S["xs_ready"], TT * (2 * L + 1) + t + 1)
                    pool.dma_start(h_rows[t * P:t * P + r, :], xs2[t][:r, :]).then_inc(rows_out[t % 2], 16)
                pool.wait_ge(rows_out[0], 48 * (L + 1))
                pool.wait_ge(rows_out[1], 32 * (L + 1))

                def hold():
                    nc.gpsimd.tensor_tensor(sm[0:1, 211:212], cst[0:1, 0:1], cst[0:1, 0:1], ALU.mult) \
                        .then_inc(S["held"], 1)

                def gather(block):
                    nc.gpsimd.tensor_copy(slot_now[:, :], slots[:, block]).then_inc(S["slot_copied"], 1)

                def gather_rows(n):
                    pool.wait_ge(S["slot_copied"], n)
                    hold()
                    nc.gpsimd.indirect_dma_start(
                        xg, None, h_rows, bass.IndirectOffsetOnAxis(ap=slot_now[:, 0:1], axis=0)) \
                        .then_inc(S["gathered"], 16)

                pool.wait_ge(S["table_ready"], L + 1)
                gather(slice(0, 1))
                before = pool.value_load(blocks[0:1, 66:67], min_val=0, max_val=DEPTH * MAXBLK)
                if L > 0:
                    pool.wait_ge(S["held"], before + 2 * L)
                gather_rows(before + L + 1)
                with pool.Fori(0, EXPERTS) as e:
                    count = pool.value_load(blocks[0:1, bass.ds(e, 1)], min_val=1, max_val=TT)
                    first = pool.value_load(blocks[0:1, bass.ds(e + 33, 1)], min_val=0, max_val=MAXBLK)
                    ever = pool.value_load(blocks[0:1, bass.ds(e + 66, 1)], min_val=0, max_val=DEPTH * MAXBLK)
                    with pool.Fori(0, count) as c:
                        pool.wait_ge(S["xg_used"], ever + c + L + 1)
                        pool.wait_ge(S["gathered"], (ever + c + L + 1) * 16)
                        pool.wait_ge(S["held"], ever + c + 2 * L + 1)
                        gather(bass.ds(first + c + 1, 1))
                        gather_rows(ever + c + L + 2)
                total = pool.value_load(blocks[0:1, 98:99], min_val=1, max_val=DEPTH * MAXBLK)
                pool.wait_ge(S["gathered"], (total + L + 1) * 16)
                pool.wait_ge(S["held"], total + 2 * L + 1)
                pool.wait_ge(S["y_stored"], (total + 1) * 16)
                hold()
                for n in range(2 * TT):
                    r = rows_of(n // 2)
                    nc.gpsimd.indirect_dma_start(
                        ygat[:r, n, :], None, y_rows,
                        bass.IndirectOffsetOnAxis(ap=pos[:r, n:n + 1], axis=0)).then_inc(ygat_in[n], 16)

        @block.scalar
        def _(act):
            link = steps(act, "scalar_steps")
            copy, fn = nc.scalar.copy, nc.scalar.activation

            def half_out(L, kind, t):
                bk, r = take(act, L, (kind, t, 0)), rows_of(t)
                give(copy(hT[:, 0:4, t * P:t * P + r],
                          bk[:, :].rearrange("p (k n) -> p k n", k=4)[:, :, 0:r]), (kind, t, 0))

            def norm_sums(n):
                junk = cut(rb, 0, D) if n % 2 == 1 else cut(rg, 0, D)
                for t in range(TT):
                    r = rows_of(t)
                    if n == 0:
                        act.wait_ge(x_in[t], 16)
                    x_done(act, n, t)
                    link(fn(junk[:r, :], x[:r, t, :], ACT.Square, accum_out=sm[:r, t:t + 1]))
                    fn(sm[:r, 5 + t:6 + t], sm[:r, t:t + 1], ACT.Sqrt, scale=1.0 / D, bias=eps_col[:r]) \
                        .then_inc(S["ssq_ready"], 1)
                    if n % 2 == 0 and n < 2 * DEPTH and t >= 2:
                        half_out(n // 2, "hn", t - 2)

            def rstds(L, *what):
                for key, dst, n, signal in what:
                    bk = take(act, L, key)
                    give(fn(dst, bk[:, 0:HALF], ACT.Ln, scale=1.0 / n, bias=eps_col), key)
                for key, dst, n, signal in what:
                    after(act, L, key)
                    fn(dst, dst, ACT.Exp, scale=-0.5).then_inc(S[signal], 1)

            xc, R, I, C, H = lru

            def gates(L, t):
                for k, dst in ((0, R), (1, I)):
                    bk = take(act, L, ("gate", t, k))
                    give(fn(dst[:, 0:SEQ], bk[:, :], ACT.Tanh, scale=0.5,
                            bias=sm[:, 22 + 2 * k + t:23 + 2 * k + t]), ("gate", t, k))
                bk = take(act, L, ("gate", t, 2))
                for k, dst in ((0, R), (1, I)):
                    last = fn(dst[:, SEQ:].rearrange("p (b c) -> p b c", c=NQ + 1)[:, :, 1:],
                              bk[:, k * NS:(k + 1) * NS].rearrange("p (b q) -> p b q", q=NQ), ACT.Tanh,
                              scale=0.5, bias=sm[:, 22 + 2 * k + t:23 + 2 * k + t])
                give(last, ("gate", t, 2))

            def decay(L, t):
                act.wait_ge(S["r_ready"], 4 * L + 2 * t + 1)
                link(fn(C, R, ACT.Tanh))
                fn(R, R, ACT.Exp).then_inc(S["a_ready"], 1)

            def input_scale(L, t):
                act.wait_ge(S["r_ready"], 4 * L + 2 * t + 2)
                fn(C, C, ACT.Sqrt).then_inc(S["a_ready"], 1)

            def gelu(L, t):
                act.wait_ge(S["gelu"], 4 * L + 2 * t + 1)
                fn(I[:, 0:T], yl[:, t, :], ACT.Square).then_inc(S["a_ready"], 1)
                act.wait_ge(S["gelu"], 4 * L + 2 * t + 2)
                fn(I[:, 0:T], I[:, 0:T], ACT.Tanh, scale=0.7978845608028654).then_inc(S["a_ready"], 1)

            act.wait_ge(S["final_ready"], 1)
            for L in range(DEPTH):
                norm_sums(2 * L)
                for t in range(TT - 2, TT):
                    half_out(L, "hn", t)

                act.wait_ge(S["coef_ready"], 2 * L + 1)
                fn(sm[:, 12:14], sm[:, 10:12], ACT.Exp).then_inc(S["lru_steps"], 1)
                act.wait_ge(S["pads_ready"], L + 1)
                for m in Z_ORDER:
                    for h, cols in enumerate(halves):
                        if m in (Z_CQ, Z_CQ + 1, Z_CKV):
                            bk = take(act, L, ("z", m, h))
                            fn(sq[:, m - Z_CQ, cols], bk[:, 0:HALF], ACT.Square).then_inc(S["sq_ready"], 1)
                        elif m < Z_Y:
                            bk, key = take(act, L, ("z", m, h)), ("z", m, h)
                            if h == 0:
                                give(copy(xext[:, m, 3:3 + HALF], bk[:, 0:HALF]), key)
                            else:
                                copy(xext[:, m, 3 + HALF:XE], bk[:, 0:SEQ - HALF])
                                give(copy(xext[:, m, XE:].rearrange("p (b c) -> p b c", c=SEXT)[:, :, 3:],
                                          bk[:, SEQ - HALF:HALF].rearrange("p (b q) -> p b q", q=NQ)), key)
                        elif m < Z_CQ:
                            bk = take(act, L, ("z", m, h))
                            give(copy(yl[:, m - Z_Y, cols], bk[:, 0:HALF]), ("z", m, h))
                        elif m in (Z_GV, Z_GV + 1):
                            bk = take(act, L, ("z", m, h))
                            give(copy(gv[:, m - Z_GV, cols], bk[:, 0:HALF]), ("z", m, h))
                    if m == Z_X + 1:
                        rstds(L, *[(("qsum", h), rsq[:, 0, cols], 256, "lnexp") for h, cols in enumerate(halves)],
                              *[(("kvsum", h), rsq[:, 1, cols], P, "lnexp") for h, cols in enumerate(halves)])
                        act.wait_ge(S["kpe_ready"], 2 * (L + 1))
                        for g in range(1, 4):
                            last = copy(kpeT[32 * g:32 * g + 32, :], kpeT[0:32, :])
                        last.then_inc(S["kperep"], 1)
                        act.wait_ge(S["coef_ready"], 2 * L + 2)
                        gates(L, 0)
                        decay(L, 0)
                    if m == Z_Y:
                        input_scale(L, 0)
                    if m == Z_Y + 1:
                        gelu(L, 0)
                        for j in range(4):
                            for h, cols in enumerate(halves):
                                bk = take(act, L, ("q", j, h))
                                give(copy(qn[:, j, cols], bk[:, 0:HALF]), ("q", j, h))
                        gates(L, 1)
                        decay(L, 1)
                        for hd in (0, 2):
                            for h in range(2):
                                absorbed_query(act, copy, L, hd, h)
                        input_scale(L, 1)
                        for hd in (4, 6):
                            for h in range(2):
                                absorbed_query(act, copy, L, hd, h)
                        bk = take(act, L, ("ctok", 0))
                        give(copy(ctok[:, 0:4, :], bk[:, :].rearrange("p (t r) -> p t r", t=4)), ("ctok", 0))
                        bk = take(act, L, ("ctok", 1))
                        give(copy(ctok[:NS, 4, :], bk[:NS, 0:P]), ("ctok", 1))
                        gelu(L, 1)
                    if m == Z_GK and L == 0:
                        act.wait_ge(S["zeros_ready"], 1)
                        act.dma_start(y_rows[EXPERTS * P:, :].rearrange("(b p) d -> p b d", p=P),
                                      rg[:, 11136:11136 + D].unsqueeze(1).to_broadcast([P, TABLE - EXPERTS, D])) \
                            .then_inc(S["y_stored"], 16)
                    if m == Z_GK:
                        act.wait_ge(S["la_ready"], L + 1)
                        link(fn(gdiff[:, 0, :], gdiff[:, 0, :], ACT.Exp, scale=-1.0))
                        fn(gdiff[:, 0, :], gdiff[:, 0, :], ACT.Ln, bias=1.0).then_inc(S["gexp"], 1)
                    if m == Z_GV + 1:
                        for n in range(3):
                            bk = take(act, L, ("vtok", n))
                            if n < 2:
                                give(copy(vtok[:, 2 * n:2 * n + 2, :], bk[:, :].rearrange("p (t c) -> p t c", t=2)),
                                     ("vtok", n))
                            else:
                                give(copy(vtok[:NS, 4, :], bk[:NS, 0:256]), ("vtok", n))
                act.wait_ge(S["cum_ready"], L + 1)
                fn(gw[:, 0, :], cum, ACT.Exp)
                fn(sm[:, 30:62], cum[:, CH - 1:SEQ:CH], ACT.Exp)
                fn(sm[:, 62:70], cum[:, SEQ + NQ - 1:T:NQ], ACT.Exp).then_inc(S["gexp"], 1)
                act.wait_ge(S["diff_ready"], CH * L + 1)
                fn(gdiff[:, 0, :], gdiff[:, 0, :], ACT.Exp).then_inc(S["gexp"], 1)

                def decays(d):
                    act.wait_ge(S["diff_ready"], CH * L + d + 1)
                    n = NCH * (CH - d)
                    last = fn(gdiff[:, d % 2, 0:n], gdiff[:, d % 2, 0:n], ACT.Exp)
                    if d < NQ:
                        n = NB * (NQ - d)
                        last = fn(gdiff[:, d % 2, SEQ:SEQ + n], gdiff[:, d % 2, SEQ:SEQ + n], ACT.Exp)
                    last.then_inc(S["exp_ready"], 1)

                def sample_exp(p):
                    act.wait_ge(S["s_max"], 4 * L + p + 1)
                    for k, (at, n) in enumerate(((0, 512), (512, 512), (1024, NS))):
                        bk = take(act, L, ("ss", p, k))
                        give(fn(sprob[:, at:at + n], bk[:, 0:n], ACT.Exp, scale=SCALE, bias=sm[:, 84:85],
                                accum_out=sm[:, 85 + k:86 + k]), ("ss", p, k))

                def probabilities_out(p):
                    for k in range(3):
                        bk = take(act, L, ("sp", p, k))
                        if k < 2:
                            give(copy(spT[:, 4 * k:4 * k + 4, :], bk[:, :].rearrange("p (j q) -> p j q", j=4)),
                                 ("sp", p, k))
                        else:
                            give(copy(spT[:NS, 8, :], bk[:NS, 0:P]), ("sp", p, k))

                def sample_out(p):
                    bk = take(act, L, ("sv", p))
                    give(copy(qas[:, 2 * p:2 * p + 2, :], bk[:, 0:P].rearrange("p (b c) -> p b c", b=2)), ("sv", p))

                for s in range(ATT_STEPS):
                    w = s - 2
                    for d in range(1, CH):
                        if s == DP_STEPS[d] - 2:
                            decays(d)
                    if s == GN_STEP:
                        act.wait_ge(S["oacc_ready"], L + 1)
                        fn(gtmp, oacc, ACT.Square).then_inc(S["gsq"], 1)
                        fn(gw, gout, ACT.Tanh, scale=0.5).then_inc(S["gexp"], 1)
                    if s == GN_STEP + 1:
                        rstds(L, *[(("gnorm", j, h), gdiff[:, j, cols], GDV, "gn_ready")
                                   for j in range(2) for h, cols in enumerate(halves)])
                    if 0 <= w < 4 * HEADS:
                        hd, i = w // 4, w % 4
                        key = ("pt", hd, i)
                        bk = take(act, L, key)
                        give(copy(pT[:, hd % 2, 0:i + 1, i * P:(i + 1) * P],
                                  bk[:, 0:(i + 1) * P].rearrange("p (k q) -> p k q", q=P)), key)
                    if s < 4 * HEADS:
                        n, key = (s % 4 + 1) * P, ("s", s // 4, s % 4)
                        bk = take(act, L, key)
                        act.wait_ge(S["max_ready"], 4 * HEADS * L + s + 1)
                        give(fn(prob[:, s % 2, 0:n], bk[:, 0:n], ACT.Exp, scale=SCALE,
                                bias=sm[:, 72 + s % 2:73 + s % 2], accum_out=sm[:, 74 + s % 2:75 + s % 2]), key)
                    if s >= 6 and (s - 2) % 4 == 0:
                        hd = (s - 2) // 4 - 1
                        bk = take(act, L, ("pv", hd))
                        give(copy(qa[:, hd, :], bk[:, :]), ("pv", hd))
                    if s == SAMPLE_STEP + 1:
                        act.wait_ge(S["gla_out"], 32 * (L + 1))
                        sample_exp(0)
                    if s == SAMPLE_STEP + 3:
                        probabilities_out(0)
                    if s == SAMPLE_STEP + 4:
                        sample_out(0)
                for p in range(1, 4):
                    if p != 2:
                        sample_exp(p)
                    probabilities_out(p)
                    if p == 1:
                        sample_exp(2)
                    sample_out(p)
                for jj in range(4):
                    bk = take(act, L, ("uv", jj))
                    give(copy(outB[:, jj, 0:SEQ], bk[:, :]), ("uv", jj))

                act.wait_ge(S["out_b"], L + 1)
                after(act, L, ("uv", 3))
                for k in range(8):
                    fn(osq[:, k, :], merged[k], ACT.Square).then_inc(S["osq_ready"], 1)
                rstds(L, *[(("osum", k, h), ors[:, k, cols], n, "ors_ready")
                           for k, n in enumerate((256, 512, 256)) for h, cols in enumerate(halves)])

                norm_sums(2 * L + 1)
                for t in range(TT):
                    half_out(L, "hm", t)
                act.wait_ge(S["sel_exp"], L + 1)
                fn(r_diff, r_diff, ACT.Exp).then_inc(S["sel_exp_done"], 1)

                act.wait_ge(S["route_ready"], L + 1)
                copy(sm[:, 200:201], sm[:, 190:191]).then_inc(S["y_act"], 1)

                def rows_transposed(n):
                    act.wait_ge(S["xg_used"], n)
                    copy(xT[:, 0:4, :], bank[0][:, :].rearrange("p (k n) -> p k n", k=4)).then_inc(S["xt_act"], 1)

                before = act.value_load(blocks[0:1, 66:67], min_val=0, max_val=DEPTH * MAXBLK)
                rows_transposed(before + L + 1)
                with act.Fori(0, EXPERTS) as e:
                    count = act.value_load(blocks[0:1, bass.ds(e, 1)], min_val=1, max_val=TT)
                    first = act.value_load(blocks[0:1, bass.ds(e + 33, 1)], min_val=0, max_val=MAXBLK)
                    ever = act.value_load(blocks[0:1, bass.ds(e + 66, 1)], min_val=0, max_val=DEPTH * MAXBLK)
                    with act.Fori(0, count) as c:
                        act.wait_ge(S["gate_done"], ever + c + 1)
                        fn(act1, bank[2][:, 0:DE], ACT.Silu).then_inc(S["silu_done"], 1)
                        act.wait_ge(S["at_done"], ever + c + 1)
                        copy(actT, bank[4][:, 0:DE].rearrange("p (k n) -> p k n", k=2)).then_inc(S["actt_ready"], 1)
                        rows_transposed(ever + c + L + 2)
                        act.wait_ge(S["down_done"], ever + c + 1)
                        act.wait_ge(S["y_stored"], (ever + c + 1) * 16)
                        copy(ysb[:, 0:512], bank[5][:, :]).then_inc(S["y_act"], 1)
                        act.wait_ge(S["y_act"], ever + c + L + 2)
                        act.wait_ge(S["y_vec"], ever + c + L + 2)
                        act.dma_start(y_rows[bass.ds((first + c) * P, P), :], ysb).then_inc(S["y_stored"], 16)
            norm_sums(2 * DEPTH)

        @block.vector
        def _(dve):
            V = nc.vector
            link = steps(dve, "vector_steps")

            def norm_rows(n, tiles):
                dve.wait_ge(S["gain_in"], 16 * (n + 1))
                for t in tiles:
                    r = rows_of(t)
                    xs_free(dve, n, t)
                    dve.wait_ge(S["ssq_ready"], TT * n + t + 1)
                    link(V.reciprocal(sm[:r, 5 + t:6 + t], sm[:r, 5 + t:6 + t]))
                    V.scalar_tensor_tensor(normed(n, t)[:r, :], x[:r, t, :], sm[:r, 5 + t:6 + t], gain[:r, :],
                                           ALU.mult, ALU.mult).then_inc(S["xs_ready"], 1)

            def rope_add(L, kind_pe, kind_rot, h, cols, dst, signal):
                bk = take(dve, L, kind_pe)
                if kind_pe[1:] != (0, 0):
                    dve.wait_ge(S[signal], 4 * L + 2 * kind_pe[1] + h)
                give(V.tensor_tensor(dst, bk[:, 0:HALF], cos[:, cols], ALU.mult), kind_pe)
                bk = take(dve, L, kind_rot)
                give(V.tensor_tensor(ropetmp, bk[:, 0:HALF], sin[:, cols], ALU.mult), kind_rot)
                after(dve, L, kind_pe)
                after(dve, L, kind_rot)
                V.tensor_tensor(dst, dst, ropetmp, ALU.add).then_inc(S[signal], 1)

            link(V.memset(sm[:, :], 0.0))
            V.memset(eps_col, EPS).then_inc(S["final_ready"], 1)
            dve.wait_ge(S["final_ready"], 1)
            dve.wait_ge(S["const_in"], 16)
            for L in range(DEPTH):
                if L == 0:
                    norm_rows(0, range(TT))
                for t in range(TT):
                    bk, r = take(dve, L, ("hn", t, 1)), rows_of(t)
                    give(V.tensor_copy(hT[:, 4:8, t * P:t * P + r],
                                       bk[:, :].rearrange("p (k n) -> p k n", k=4)[:, :, 0:r]), ("hn", t, 1))
                dve.wait_ge(S["vec_in"], 16 * (L + 1))
                lam = vec[:, V_LAM:V_LAM + 2]
                z, ex, s1, s2, pl, c1 = (sm[:, 10 + 2 * k:12 + 2 * k] for k in range(6))
                link(V.tensor_scalar(z, lam, -1.0, None, ALU.mult))
                link(V.tensor_tensor(s1, z, lam, ALU.max))
                V.tensor_scalar(z, s1, -1.0, None, ALU.mult).then_inc(S["coef_ready"], 1)
                dve.wait_ge(S["lru_steps"], L + 1)
                link(V.tensor_scalar(s1, ex, 2.0, None, ALU.add))
                link(V.reciprocal(s2, s1))
                link(V.tensor_tensor(s1, ex, s2, ALU.mult))
                link(V.tensor_tensor(s2, s1, s1, ALU.mult))
                link(V.tensor_scalar(pl, s2, 1.0 / 15, None, ALU.mult))
                for k in (13, 11, 9, 7, 5, 3):
                    link(V.scalar_tensor_tensor(pl, pl, 1.0 / k, s2, ALU.add, ALU.mult))
                link(V.scalar_tensor_tensor(pl, pl, 1.0, s1, ALU.add, ALU.mult))
                link(V.tensor_scalar(s1, lam, -1.0, 0.0, ALU.mult, ALU.max))
                link(V.scalar_tensor_tensor(s1, pl, 2.0, s1, ALU.mult, ALU.add))
                link(V.tensor_scalar(c1, s1, -4.0, None, ALU.mult))
                V.tensor_scalar(sm[:, 22:26], vec[:, V_BA:V_BA + 4], 0.5, None, ALU.mult) \
                    .then_inc(S["coef_ready"], 1)
                dve.wait_ge(S["coef_ready"], 2 * (L + 1))

                xc, R, I, C, H = lru
                seqs = lambda v: v[:, SEQ:].rearrange("p (b c) -> p b c", c=NQ + 1)

                def conv(t):
                    after(dve, L, ("z", Z_X + t, 1))
                    after(dve, L, ("z", Z_X + t, 0))
                    xq = xext[:, t, XE:].rearrange("p (b c) -> p b c", c=SEXT)
                    if t == 1:
                        for k in range(3):
                            take(dve, L, ("gate", 0, k))
                        V.memset(seqs(xc)[:, :, 0], 0.0)
                    w = lambda k: vec[:, V_CW + 2 * k + t:V_CW + 2 * k + t + 1]
                    V.tensor_scalar(xc[:, 0:SEQ], xext[:, t, 0:SEQ], w(0), vec[:, V_CB + t:V_CB + t + 1],
                                    ALU.mult, ALU.add)
                    link(V.tensor_scalar(seqs(xc)[:, :, 1:], xq[:, :, 0:NQ], w(0), vec[:, V_CB + t:V_CB + t + 1],
                                         ALU.mult, ALU.add))
                    for k in range(1, 4):
                        V.scalar_tensor_tensor(xc[:, 0:SEQ], xext[:, t, k:k + SEQ], w(k), xc[:, 0:SEQ],
                                               ALU.mult, ALU.add)
                        ins = V.scalar_tensor_tensor(seqs(xc)[:, :, 1:], xq[:, :, k:k + NQ], w(k),
                                                     seqs(xc)[:, :, 1:], ALU.mult, ALU.add)
                        if k < 3:
                            link(ins)
                        else:
                            ins.then_inc(S["conv_ready"], 1)

                def log_decay(t):
                    dve.wait_ge(S["conv_ready"], 2 * L + t + 1)
                    for k in range(3):
                        after(dve, L, ("gate", t, k))
                    V.tensor_scalar(R, R, 1.0, c1[:, t:t + 1], ALU.add, ALU.mult).then_inc(S["r_ready"], 1)
                    link(V.scalar_tensor_tensor(I, I, 1.0, xc, ALU.add, ALU.mult))

                def one_less(t):
                    dve.wait_ge(S["a_ready"], 8 * L + 4 * t + 1)
                    link(V.tensor_scalar(H, C, -1.0, 1.0, ALU.mult, ALU.add))
                    link(V.reciprocal(H, H))
                    V.scalar_tensor_tensor(C, C, -2.0, H, ALU.mult, ALU.mult).then_inc(S["r_ready"], 1)

                def scan(t):
                    dve.wait_ge(S["a_ready"], 8 * L + 4 * t + 2)
                    link(V.scalar_tensor_tensor(C, C, 0.5, I, ALU.mult, ALU.mult))
                    V.memset(seqs(R)[:, :, 0], 0.0)
                    V.tensor_copy(seqs(C)[:, :, 0], vec[:, V_SL + NB * t:V_SL + NB * (t + 1)]) \
                        .then_inc(S["gelu"], 1)
                    dve.wait_ge(S["gelu"], 4 * L + 2 * t + 1)
                    link(V.tensor_tensor_scan(H, R, C, 0.0, ALU.mult, ALU.add))
                    if L > 0 and t == 0:
                        dve.wait_ge(S["lru_out"], 16 * L)
                    V.tensor_copy(sm[:, 110 + 9 * t:111 + 9 * t], H[:, SEQ - 1:SEQ])
                    V.tensor_copy(sm[:, 111 + 9 * t:119 + 9 * t], seqs(H)[:, :, NQ]).then_inc(S["lru_saved"], 1)

                def gelu_out(t):
                    dve.wait_ge(S["a_ready"], 8 * L + 4 * t + 3)
                    after(dve, L, ("z", Z_Y + t, 1))
                    link(V.tensor_scalar(I[:, 0:T], I[:, 0:T], 0.044715, 1.0, ALU.mult, ALU.add))
                    V.tensor_tensor(I[:, 0:T], I[:, 0:T], yl[:, t, :], ALU.mult).then_inc(S["gelu"], 1)
                    dve.wait_ge(S["a_ready"], 8 * L + 4 * t + 4)
                    link(V.scalar_tensor_tensor(yl[:, t, :], I[:, 0:T], 1.0, yl[:, t, :], ALU.add, ALU.mult))
                    V.scalar_tensor_tensor(yl[:, t, 0:SEQ], yl[:, t, 0:SEQ], 0.5, H[:, 0:SEQ], ALU.mult, ALU.mult)
                    ys = yl[:, t, SEQ:T].rearrange("p (b q) -> p b q", q=NQ)
                    link(V.scalar_tensor_tensor(ys, ys, 0.5, seqs(H)[:, :, 1:], ALU.mult, ALU.mult))
                    if t == 0:
                        V.memset(seqs(R)[:, :, 0], 0.0)
                        link(V.memset(seqs(I)[:, :, 0], 0.0))


                nsq = 0
                for m in Z_ORDER:
                    for h, cols in enumerate(halves):
                        key = ("z", m, h)
                        if m in (Z_CQ, Z_CQ + 1, Z_CKV):
                            bk = take(dve, L, key)
                            nsq += 1
                            dve.wait_ge(S["sq_ready"], 6 * L + nsq)
                            give(V.tensor_copy(cq[:, m - Z_CQ, cols] if m < Z_CKV else ckvT[:, cols],
                                               bk[:, 0:HALF]), key)
                        elif m == Z_PE:
                            bk = take(dve, L, key)
                            if h > 0:
                                dve.wait_ge(S["kpe_ready"], 2 * L + h)
                            V.tensor_copy(gaT[64:80, cols], bk[64:80, 0:HALF])
                            link(V.tensor_copy(ropetmp[0:32, :], bk[32:64, 0:HALF]))
                            link(V.tensor_tensor(ropetmp[0:32, :], ropetmp[0:32, :], sin[0:32, cols], ALU.mult))
                            give(V.tensor_tensor(kpeT[0:32, cols], bk[0:32, 0:HALF], cos[0:32, cols], ALU.mult),
                                 key)
                            after(dve, L, key)
                            V.tensor_tensor(kpeT[0:32, cols], kpeT[0:32, cols], ropetmp[0:32, :], ALU.add) \
                                .then_inc(S["kpe_ready"], 1)
                        elif m in (Z_GQ, Z_GK):
                            bk = take(dve, L, key)
                            give(V.tensor_copy((gq if m == Z_GQ else gk)[:, cols], bk[:, 0:HALF]), key)
                        elif m >= Z_GO:
                            bk = take(dve, L, key)
                            dve.wait_ge(S["tailsaved"], L + 1)
                            give(V.tensor_copy(gout[:, m - Z_GO, cols], bk[:, 0:HALF]), key)
                    if m == Z_X + 1:
                        dve.wait_ge(S["pads_ready"], L + 1)
                        conv(0)
                        for h, cols in enumerate(halves):
                            dve.wait_ge(S["lnexp"], 4 * L + h + 1)
                            for j in range(2):
                                after(dve, L, ("z", Z_CQ + j, h))
                                V.scalar_tensor_tensor(cq[:, j, cols], cq[:, j, cols], vec[:, V_QN + j:V_QN + j + 1],
                                                       rsq[:, 0, cols], ALU.mult, ALU.mult) \
                                    .then_inc(S["q_ready"], 1)
                        for h, cols in enumerate(halves):
                            dve.wait_ge(S["lnexp"], 4 * L + h + 3)
                            after(dve, L, ("z", Z_CKV, h))
                            V.scalar_tensor_tensor(ckvT[:, cols], ckvT[:, cols], vec[:, V_KN:V_KN + 1],
                                                   rsq[:, 1, cols], ALU.mult, ALU.mult).then_inc(S["ckv_ready"], 1)
                        log_decay(0)
                        conv(1)
                        one_less(0)
                        scan(0)
                    if m == Z_Y + 1:
                        gelu_out(0)
                        for g in range(2):
                            for h, cols in enumerate(halves):
                                rope_add(L, ("pe", g, h), ("rot", g, h), h, cols, qpe[:, g, cols], "qpe_ready")
                        log_decay(1)
                        for h, cols in enumerate(halves):
                            bk = take(dve, L, ("alpha", h))
                            give(V.tensor_scalar(la[:, cols], bk[:, 0:HALF], vec[:, V_GB:V_GB + 1], None, ALU.add),
                                 ("alpha", h))
                            after(dve, L, ("alpha", h))
                        V.scalar_tensor_tensor(gdiff[:, 0, :], la, -1.0, la, ALU.mult, ALU.max).then_inc(S["la_ready"], 1)
                        link(V.tensor_scalar(la, la, 0.0, None, ALU.min))
                        for hd in range(1, HEADS, 2):
                            for h in range(2):
                                absorbed_query(dve, V.tensor_copy, L, hd, h)
                            if hd == 3:
                                one_less(1)
                                scan(1)
                        bk = take(dve, L, ("qp",))
                        give(V.tensor_copy(qp[0:32, :, :].rearrange("p b (h q) -> p h b q", q=NQ),
                                           bk[0:32, :].rearrange("p (h b q) -> p h b q", h=HEADS, q=NQ)), ("qp",))
                        gelu_out(1)
                    if m == Z_GK:
                        dve.wait_ge(S["gexp"], 4 * L + 1)
                        link(V.scalar_tensor_tensor(la, gdiff[:, 0, :], -1.0, la, ALU.mult, ALU.add))
                        link(V.tensor_scalar(la, la, 1.0 / 16.0, None, ALU.mult))
                        V.tensor_tensor_scan(cum, cst[:, C_RST:C_RST + T], la, 0.0, ALU.mult, ALU.add) \
                            .then_inc(S["cum_ready"], 1)
                        dve.wait_ge(S["cum_ready"], L + 1)
                        dve.wait_ge(S["gexp"], 4 * L + 2)
                        for h in range(2):
                            after(dve, L, ("z", Z_GQ, h))
                            after(dve, L, ("z", Z_GK, h))
                        link(V.tensor_tensor(gw[:, 1, :], gq, gw[:, 0, :], ALU.mult))
                        for h in range(GH):
                            ins = V.tensor_scalar(qbd[:, h, :], gw[:, 1, :], cst[:, C_QM + h:C_QM + h + 1], None, ALU.mult)
                        ins.then_inc(S["qbd_ready"], 1)
                        dve.wait_ge(S["gexp"], 4 * L + 3)
                        V.tensor_tensor(kd, gk, gdiff[:, 0, :], ALU.mult).then_inc(S["kd_ready"], 1)
                bk = take(dve, L, ("ktok", 0))
                give(V.tensor_copy(ktok[:, 0:4, :], bk[:, :].rearrange("p (t c) -> p t c", t=4)), ("ktok", 0))
                bk = take(dve, L, ("ktok", 1))
                give(V.tensor_copy(ktok[:NS, 4, :], bk[:NS, 0:P]), ("ktok", 1))
                dve.wait_ge(S["gstate_in"], 16 * (L + 1))
                if L > 0:
                    dve.wait_ge(S["gla_out"], 32 * L)

                def states(t):
                    bk = take(dve, L, ("delta", t))
                    if t < TT - 1:
                        for c in range(8):
                            n = 8 * t + c
                            ins = V.scalar_tensor_tensor(st[:, n + 1, :], st[:, n, :], sm[:, 30 + n:31 + n],
                                                         bk[:, c * GDV:(c + 1) * GDV], ALU.mult, ALU.add)
                            if c < 7:
                                link(ins)
                    else:
                        link(V.tensor_tensor(gsout, st[:, NCH + 1:, :],
                                             sm[:, 62:70].unsqueeze(2).to_broadcast([P, NB, GDV]), ALU.mult))
                        ins = V.tensor_tensor(gsout, gsout, bk[:, :].rearrange("p (c e) -> p c e", c=NB), ALU.add)
                    give(ins, ("delta", t))
                    after(dve, L, ("delta", t))

                def inter_out(g):
                    bk, key = take(dve, L, ("inter", g)), ("inter", g)
                    n, at = (256, 256 * g) if g < 2 else (NS, SEQ)
                    give(V.tensor_copy(oacc[:, :, at:at + n], bk[:, 0:2 * n].rearrange("p (j n) -> p j n", j=2)), key)
                    after(dve, L, key)

                def chunked(v, n, at, k):
                    size, part = (CH, v[:, 0:SEQ]) if k == 0 else (NQ, v[:, SEQ:T])
                    return part.rearrange("p (c n) -> p c n", n=size)[:, :, at:at + n]

                def packed(v, n, k):
                    return (v[:, 0:NCH * n] if k == 0 else v[:, SEQ:SEQ + NB * n]) \
                        .rearrange("p (c n) -> p c n", n=n)

                def products(d):
                    if d >= 2:
                        take(dve, L, ("dp", d - 2, 1))
                        if d - 2 < NQ:
                            take(dve, L, ("ds", d - 2))
                    parts = [(0, CH - d)] + ([(1, NQ - d)] if d < NQ else [])
                    out = gw[:, d % 2, :]
                    if d == 0:
                        V.tensor_tensor(out, gq, gk, ALU.mult).then_inc(S["w_ready"], 1)
                        return
                    dve.wait_ge(S["exp_ready"], (CH - 1) * L + d)
                    for k, n in parts:
                        ins = V.tensor_tensor(packed(out, n, k), packed(gdiff[:, d % 2, :], n, k),
                                              chunked(gq, n, d, k), ALU.mult)
                    link(ins)
                    for k, n in parts:
                        ins = V.tensor_tensor(packed(out, n, k), packed(out, n, k), chunked(gk, n, 0, k), ALU.mult)
                    ins.then_inc(S["w_ready"], 1)

                def accumulate(d):
                    n = CH - d
                    for j in range(2):
                        bk = take(dve, L, ("dp", d, j))
                        give(V.tensor_tensor(packed(gtmp[:, j, :], n, 0), packed(bk, n, 0),
                                             chunked(gv[:, j, :], n, 0, 0), ALU.mult), ("dp", d, j))
                        after(dve, L, ("dp", d, j))
                        V.tensor_tensor(chunked(oacc[:, j, :], n, d, 0), chunked(oacc[:, j, :], n, d, 0),
                                        packed(gtmp[:, j, :], n, 0), ALU.add).then_inc(S["oacc_steps"], 1)
                    if d < NQ:
                        n = NQ - d
                        bk = take(dve, L, ("ds", d))
                        for j in range(2):
                            ins = V.tensor_tensor(packed(gtmp[:, j, :], n, 1),
                                                  bk[:, j * NS:j * NS + NB * n].rearrange("p (c n) -> p c n", n=n),
                                                  chunked(gv[:, j, :], n, 0, 1), ALU.mult)
                        give(ins, ("ds", d))
                        after(dve, L, ("ds", d))
                        for j in range(2):
                            ins = V.tensor_tensor(chunked(oacc[:, j, :], n, d, 1), chunked(oacc[:, j, :], n, d, 1),
                                                  packed(gtmp[:, j, :], n, 1), ALU.add)
                        ins.then_inc(S["oacc_steps"], 1)
                    acc[0] += 2 + (d < NQ)
                    dve.wait_ge(S["oacc_steps"], acc[0])

                for m in (0, 1):
                    after(dve, L, ("z", Z_GV + m, 0))
                    after(dve, L, ("z", Z_GV + m, 1))
                def sample_max(p):
                    for k, n in enumerate((512, 512, NS)):
                        bk = take(dve, L, ("ss", p, k))
                        ins = V.tensor_reduce(sm[:, 80 + k:81 + k], bk[:, 0:n], AX_X, ALU.max)
                    link(ins)
                    link(V.tensor_reduce(sm[:, 83:84], sm[:, 80:83], AX_X, ALU.max))
                    V.tensor_scalar(sm[:, 84:85], sm[:, 83:84], -SCALE, None, ALU.mult).then_inc(S["s_max"], 1)

                def sample_divide(p):
                    for k in range(3):
                        after(dve, L, ("ss", p, k))
                    link(V.tensor_reduce(sm[:, 88:89], sm[:, 85:88], AX_X, ALU.add))
                    link(V.reciprocal(sm[:, 89:90], sm[:, 88:89]))
                    V.tensor_scalar(sprob, sprob, sm[:, 89:90], None, ALU.mult).then_inc(S["s_prob"], 1)

                products(0)
                for s in range(ATT_STEPS):
                    if s < 4 * HEADS:
                        n, b2 = (s % 4 + 1) * P, s % 2
                        bk = take(dve, L, ("s", s // 4, s % 4))
                        link(V.tensor_reduce(sm[:, 70 + b2:71 + b2], bk[:, 0:n], AX_X, ALU.max))
                        V.tensor_scalar(sm[:, 72 + b2:73 + b2], sm[:, 70 + b2:71 + b2], -SCALE, None, ALU.mult) \
                            .then_inc(S["max_ready"], 1)
                    if 0 < s <= 4 * HEADS:
                        w = s - 1
                        n, b2 = (w % 4 + 1) * P, w % 2
                        after(dve, L, ("s", w // 4, w % 4))
                        link(V.reciprocal(sm[:, 76 + b2:77 + b2], sm[:, 74 + b2:75 + b2]))
                        V.tensor_scalar(prob[:, b2, 0:n], prob[:, b2, 0:n], sm[:, 76 + b2:77 + b2], None, ALU.mult) \
                            .then_inc(S["prob_ready"], 1)
                    if s < TT:
                        states(s)
                    if s + 1 in DP_STEPS[1:]:
                        products(DP_STEPS.index(s + 1))
                    if s == DP_STEPS[0]:
                        take(dve, L, ("inter", 2))
                        for g in range(3):
                            inter_out(g)
                    if s - 1 in DP_STEPS:
                        accumulate(DP_STEPS.index(s - 1))
                    if s == SAMPLE_STEP:
                        sample_max(0)
                    if s == SAMPLE_STEP + 1:
                        sample_divide(0)
                    if s == DP_STEPS[-1] + 1:
                        V.tensor_copy(sm[:, 201:202], sm[:, 190:191]).then_inc(S["oacc_ready"], 1)
                    if s == GN_STEP + 1:
                        for j in range(2):
                            for h, cols in enumerate(halves):
                                dve.wait_ge(S["gn_ready"], 4 * L + 2 * j + h + 1)
                                ins = V.scalar_tensor_tensor(oacc[:, j, cols], oacc[:, j, cols], vec[:, V_GN:V_GN + 1],
                                                             gdiff[:, j, cols], ALU.mult, ALU.mult)
                        link(ins)
                        dve.wait_ge(S["gexp"], 4 * L + 4)
                        link(V.scalar_tensor_tensor(gout, gw, 1.0, gout, ALU.add, ALU.mult))
                        V.scalar_tensor_tensor(outC, gout, 0.5, oacc, ALU.mult, ALU.mult).then_inc(S["out_c"], 1)

                for p in range(1, 4):
                    sample_max(p)
                    sample_divide(p)
                dve.wait_ge(S["gla_out"], 32 * (L + 1))
                bk = take(dve, L, ("uvs",))
                give(V.tensor_copy(outB[:, :, SEQ:T], bk[:, 0:4 * NS].rearrange("p (j n) -> p j n", j=4)), ("uvs",))
                after(dve, L, ("uvs",))
                V.tensor_copy(sm[:, 202:203], sm[:, 190:191]).then_inc(S["out_b"], 1)

                for k, g in enumerate((0, 0, 1, 1, 1, 1, 2, 2)):
                    if k in (0, 2, 6):
                        dve.wait_ge(S["ors_ready"], 6 * L + 2 * g + 2)
                    V.scalar_tensor_tensor(merged[k], merged[k], vec[:, V_ON + k:V_ON + k + 1], ors[:, g, :],
                                           ALU.mult, ALU.mult).then_inc(S["merged"], 1)
                for n in range(2):
                    for t in range(TT):
                        bk, r, key = take(dve, L, ("wo", n, t)), rows_of(t), ("wo", n, t)
                        half = x[:r, t, 512 * n:512 * n + 512]
                        give(V.tensor_tensor(half, half, bk[:r, :], ALU.add), key)
                        if n == 1 and t > 0:
                            norm_rows(2 * L + 1, (t - 1,))
                norm_rows(2 * L + 1, (TT - 1,))
                for t in range(TT):
                    bk, r = take(dve, L, ("hm", t, 1)), rows_of(t)
                    give(V.tensor_copy(hT[:, 4:8, t * P:t * P + r],
                                       bk[:, :].rearrange("p (k n) -> p k n", k=4)[:, :, 0:r]), ("hm", t, 1))

                link(V.memset(rb[:, 0:1200], 0.0))
                link(V.memset(r_g, -3.0e38))
                dve.wait_ge(S["router_in"], 32 * (L + 1))
                bk = take(dve, L, ("logits",))
                V.tensor_tensor(r_log[:, 0:4, :], bk[:, 0:144].rearrange("p (t n) -> p t n", t=4),
                                rbias[:, :].unsqueeze(1).to_broadcast([P, 4, 36]), ALU.add)
                give(V.tensor_tensor(r_log[:NS, 4, :], bk[:NS, 144:180], rbias[:NS, :], ALU.add), ("logits",))
                after(dve, L, ("logits",))
                link(V.tensor_copy(r_g[:, :, 0:GROUPS], r_log[:, :, 0:GROUPS]))
                for t in range(TT):
                    ins = V.max(r_g8[:, t, :], r_g[:, t, :])
                link(ins)
                for t in range(TT):
                    ins = V.max_index(r_gi[:, t, :], r_g8[:, t, :], r_g[:, t, :])
                link(ins)
                link(V.tensor_copy(r_gid, r_gi[:, :, 0]))
                link(V.tensor_tensor(r_gone, iota[:, 0:GROUPS].unsqueeze(1).to_broadcast([P, TT, GROUPS]),
                                     r_gid.unsqueeze(2).to_broadcast([P, TT, GROUPS]), ALU.is_equal))
                for g in range(GROUPS):
                    part = r_log[:, :, GROUPS + EPG * g:GROUPS + EPG * (g + 1)]
                    link(V.tensor_tensor(r_part, part, r_gone[:, :, g:g + 1].to_broadcast([P, TT, EPG]), ALU.mult))
                    link(V.tensor_tensor(r_e, r_e, r_part, ALU.add))
                for t in range(TT):
                    ins = V.max(r_e8[:, t, :], r_e[:, t, :])
                link(ins)
                for t in range(TT):
                    ins = V.max_index(r_ei[:, t, :], r_e8[:, t, :], r_e[:, t, :])
                link(ins)
                link(V.tensor_copy(r_eid, r_ei[:, :, 0:2]))
                link(V.scalar_tensor_tensor(r_eid, r_gid.unsqueeze(2).to_broadcast([P, TT, 2]), float(EPG), r_eid,
                                            ALU.mult, ALU.add))
                V.tensor_tensor(r_diff[:, :, 0:GROUPS], r_log[:, :, 0:GROUPS],
                                r_g8[:, :, 0:1].to_broadcast([P, TT, GROUPS]), ALU.subtract)
                V.tensor_tensor(r_diff[:, :, GROUPS], r_e8[:, :, 1], r_e8[:, :, 0], ALU.subtract) \
                    .then_inc(S["sel_exp"], 1)
                for k in range(2):
                    ins = V.tensor_tensor(r_sel[:, :, k, :], iota[:, 0:EXPERTS].unsqueeze(1).to_broadcast([P, TT, EXPERTS]),
                                          r_eid[:, :, k:k + 1].to_broadcast([P, TT, EXPERTS]), ALU.is_equal)
                link(ins)
                V.tensor_tensor(r_any, r_sel[:, :, 0, :], r_sel[:, :, 1, :], ALU.add).then_inc(S["sel_ready"], 1)
                bk = take(dve, L, ("rank",))
                V.tensor_copy(r_rank, bk[:, 0:160].rearrange("p (t e) -> p t e", t=TT))
                give(V.tensor_copy(r_tot, bk[:, 160:320].rearrange("p (t e) -> p t e", t=TT)), ("rank",))
                after(dve, L, ("rank",))
                for t in range(1, TT):
                    link(V.tensor_tensor(r_tot[:, t, :], r_tot[:, t, :], r_tot[:, t - 1, :], ALU.add))
                V.tensor_tensor(r_rank[:, 1:TT, :], r_rank[:, 1:TT, :], r_tot[:, 0:TT - 1, :], ALU.add)
                r_cnt = r_tot[:, TT - 1, :]
                link(V.tensor_scalar(r_nb, r_cnt, float(P), 1.0, ALU.is_gt, ALU.add))
                for k in (2, 3, 4):
                    link(V.scalar_tensor_tensor(r_nb, r_cnt, float(k * P), r_nb, ALU.is_gt, ALU.add))
                link(V.tensor_tensor_scan(r_tab[:, 34:66], ones[:, 0:EXPERTS], r_nb, 0.0, ALU.mult, ALU.add))
                V.tensor_copy(r_tab[:, 0:32], r_nb)
                link(V.tensor_scalar(r_tab[:, 66:99], r_tab[:, 33:66], sm[:, 190:191], None, ALU.add))
                link(V.tensor_copy(sm[:, 190:191], r_tab[:, 98:99]))
                if L > 0:
                    dve.wait_ge(S["combined"], TT * L)
                V.tensor_copy(blocks[0:1, 0:99], r_tab[0:1, 0:99]).then_inc(S["route_ready"], 1)
                link(V.tensor_scalar(r_hi, r_rank, float(P), None, ALU.is_ge))
                for k in (2, 3, 4):
                    link(V.scalar_tensor_tensor(r_hi, r_rank, float(k * P), r_hi, ALU.is_ge, ALU.add))
                link(V.scalar_tensor_tensor(r_rank, r_hi, -float(P), r_rank, ALU.mult, ALU.add))
                link(V.tensor_tensor(r_hi, r_hi, r_tab[:, 33:65].unsqueeze(1).to_broadcast([P, TT, EXPERTS]), ALU.add))
                for src, dst in ((r_hi, r_h2), (r_rank, r_l2)):
                    for k in range(2):
                        ins = V.tensor_tensor(r_prod[:, :, k, :], r_sel[:, :, k, :], src, ALU.mult)
                    link(ins)
                    link(V.tensor_reduce(dst, r_prod.rearrange("p t k e -> p (t k) e"), AX_X, ALU.add))
                V.scalar_tensor_tensor(pos[:, :], r_h2, float(P), r_l2, ALU.mult, ALU.add)
                for n in range(2 * TT):
                    V.tensor_scalar(r_lo1[:, n, :], iota, r_l2[:, n:n + 1], None, ALU.is_equal)
                    V.tensor_scalar(r_hi1[:, n, :], iota[:, 0:TABLE], r_h2[:, n:n + 1],
                                    cst[:, C_TOK + n // 2:C_TOK + n // 2 + 1], ALU.is_equal, ALU.mult) \
                        .then_inc(S["pos_ready"], 1)
                dve.wait_ge(S["sel_exp_done"], L + 1)
                link(V.tensor_reduce(r_sum, r_diff[:, :, 0:GROUPS], AX_X, ALU.add))
                link(V.tensor_scalar(r_two, r_diff[:, :, GROUPS], 1.0, None, ALU.add))
                link(V.tensor_tensor(r_sum, r_sum, r_two, ALU.mult))
                link(V.reciprocal(sm[:, 100:105], r_sum))
                link(V.tensor_tensor(sm[:, 105:110], sm[:, 100:105], r_diff[:, :, GROUPS], ALU.mult))
                bk = take(dve, L, ("table",))
                give(V.tensor_copy(slots[:, :], bk[:, 0:TABLE]), ("table",))
                after(dve, L, ("table",))
                V.memset(sm[:, 203:204], 0.0).then_inc(S["table_ready"], 1)

                V.memset(sm[:, 204:205], 0.0).then_inc(S["y_vec"], 1)
                dve.wait_ge(S["route_ready"], L + 1)

                def rows_transposed(n):
                    dve.wait_ge(S["xg_used"], n)
                    V.tensor_copy(xT[:, 4:8, :], bank[1][:, :].rearrange("p (k n) -> p k n", k=4)) \
                        .then_inc(S["xt_vec"], 1)

                before = dve.value_load(blocks[0:1, 66:67], min_val=0, max_val=DEPTH * MAXBLK)
                rows_transposed(before + L + 1)
                with dve.Fori(0, EXPERTS) as e:
                    count = dve.value_load(blocks[0:1, bass.ds(e, 1)], min_val=1, max_val=TT)
                    ever = dve.value_load(blocks[0:1, bass.ds(e + 66, 1)], min_val=0, max_val=DEPTH * MAXBLK)
                    with dve.Fori(0, count) as c:
                        dve.wait_ge(S["silu_done"], ever + c + 1)
                        dve.wait_ge(S["gu_done"], ever + c + 1)
                        V.tensor_tensor(act2, act1, bank[3][:, 0:DE], ALU.mult).then_inc(S["act_ready"], 1)
                        rows_transposed(ever + c + L + 2)
                        dve.wait_ge(S["down_done"], ever + c + 1)
                        dve.wait_ge(S["y_stored"], (ever + c + 1) * 16)
                        V.tensor_copy(ysb[:, 512:1024], bank[6][:, :]).then_inc(S["y_vec"], 1)
                for n in range(2 * TT):
                    t, k = n // 2, n % 2
                    r = rows_of(t)
                    dve.wait_ge(ygat_in[n], 16 * (L + 1))
                    if k == 1:
                        dve.wait_ge(S["ygat_used"], 2 * TT * L + n)
                    ins = V.scalar_tensor_tensor(x[:r, t, :], ygat[:r, n, :], sm[:r, 100 + 5 * k + t:101 + 5 * k + t],
                                                 x[:r, t, :], ALU.mult, ALU.add)
                    ins.then_inc(S["ygat_used"], 1)
                    if k == 1:
                        dve.wait_ge(S["ygat_used"], 2 * TT * L + n + 1)
                        V.memset(sm[:, 205:206], 0.0).then_inc(S["combined"], 1)
                        if t > 0:
                            norm_rows(2 * L + 2, (t - 1,))
                norm_rows(2 * L + 2, (TT - 1,))

        @block.tensor
        def _(pe):
            mm, tr = nc.tensor.matmul, nc.tensor.transpose
            pe.wait_ge(S["const_in"], 16)
            pe.wait_ge(S["mask_cast"], 1)

            def transpose_rows(L, kind, n, tiles):
                for t in tiles:
                    r = rows_of(t)
                    pe.wait_ge(S["xs_ready"], TT * n + t + 1)
                    for g in range(2):
                        bk = begin(pe, L, (kind, t, g))
                        for k in range(4):
                            ins = tr(bk[:, k * P:k * P + r], normed(n, t)[:r, (4 * g + k) * P:(4 * g + k + 1) * P],
                                     ident[:r, :r])
                        done(ins, (kind, t, g))

            for L in range(DEPTH):
                transpose_rows(L, "hn", 2 * L, range(TT))
                for t in range(TT):
                    for g in range(2):
                        after(pe, L, ("hn", t, g))
                def gate_products(t):
                    xcs = lru[0][:, SEQ:].rearrange("p (b c) -> p b c", c=NQ + 1)[:, :, 1:]
                    pe.wait_ge(S["wlru_in"], 16 * (L + 1))
                    pe.wait_ge(S["conv_ready"], 2 * L + t + 1)
                    for k in range(2):
                        bk = begin(pe, L, ("gate", t, k))
                        done(mm(bk[:, :], wlru[:, (2 * k + t) * P:(2 * k + t + 1) * P], lru[0][:, 0:SEQ],
                                start=True, stop=True), ("gate", t, k))
                    bk = begin(pe, L, ("gate", t, 2))
                    for k in range(2):
                        ins = mm(bk[:, k * NS:(k + 1) * NS], wlru[:, (2 * k + t) * P:(2 * k + t + 1) * P], xcs,
                                 start=True, stop=True)
                    done(ins, ("gate", t, 2))

                for n, m in enumerate(Z_ORDER):
                    pe.wait_ge(win_in[n % 4], 16 * (L * WUSES[n % 4] + n // 4 + 1))
                    mrows = 80 if m == Z_PE else P
                    for h, cols in enumerate(halves):
                        bk = begin(pe, L, ("z", m, h))
                        for k in range(KT):
                            ins = mm(bk[:mrows, 0:HALF], win[:, n % 4, k, :mrows], hT[:, k, cols],
                                     start=k == 0, stop=k == KT - 1)
                        done(ins, ("z", m, h))
                    if m == Z_X + 1:
                        pe.wait_ge(S["sq_ready"], 6 * (L + 1))
                        for h, cols in enumerate(halves):
                            bk = begin(pe, L, ("qsum", h))
                            mm(bk[:, 0:HALF], ones, sq[:, 0, cols], start=True, stop=False)
                            done(mm(bk[:, 0:HALF], ones, sq[:, 1, cols], start=False, stop=True), ("qsum", h))
                        for h, cols in enumerate(halves):
                            bk = begin(pe, L, ("kvsum", h))
                            done(mm(bk[:, 0:HALF], ones, sq[:, 2, cols], start=True, stop=True), ("kvsum", h))
                        gate_products(0)
                    if m == Z_Y + 1:
                        pe.wait_ge(S["q_ready"], 4 * (L + 1))
                        pe.wait_ge(S["ckv_ready"], 2 * (L + 1))
                        pe.wait_ge(S["wq_in"], 16 * (L + 1))

                        def query(key, col, cols):
                            bk = begin(pe, L, key)
                            for k in range(2):
                                ins = mm(bk[:, 0:HALF], wq[:, k, col * P:(col + 1) * P], cq[:, k, cols],
                                         start=k == 0, stop=k == 1)
                            done(ins, key)

                        for j in range(4):
                            for h, cols in enumerate(halves):
                                query(("q", j, h), j, cols)
                        for g in range(2):
                            for h, cols in enumerate(halves):
                                query(("pe", g, h), 4 + g, cols)
                                query(("rot", g, h), 6 + g, cols)
                        gate_products(1)
                        pe.wait_ge(S["wa2_in"], 16 * (L + 1))
                        for h, cols in enumerate(halves):
                            bk = begin(pe, L, ("alpha", h))
                            done(mm(bk[:, 0:HALF], wa2[64:80, :], gaT[64:80, cols], start=True, stop=True), ("alpha", h))
                        pe.wait_ge(S["uk_in"], 16 * (L + 1))
                        for hd in range(HEADS):
                            rows = slice(64 * (hd % 2), 64 * (hd % 2) + 64)
                            for h, cols in enumerate(halves):
                                after(pe, L, ("q", hd // 2, h))
                                bk = begin(pe, L, ("qa", hd, h))
                                done(mm(bk[:, 0:HALF], ukT[rows, hd // 2, :], qn[rows, hd // 2, cols], start=True, stop=True),
                                     ("qa", hd, h))
                        bk = begin(pe, L, ("ctok", 0))
                        for t in range(4):
                            ins = tr(bk[:, t * P:(t + 1) * P], ckvT[:, t * P:(t + 1) * P], ident)
                        done(ins, ("ctok", 0))
                        bk = begin(pe, L, ("ctok", 1))
                        done(tr(bk[:NS, 0:P], ckvT[:, SEQ:T], ident), ("ctok", 1))
                        pe.wait_ge(S["qpe_ready"], 4 * (L + 1))
                        bk = begin(pe, L, ("qp",))
                        for hd in range(HEADS):
                            g = 32 * (hd % 4)
                            ins = mm(bk[0:32, hd * NS:(hd + 1) * NS], ident[:, g:g + 32], qpe[:, hd // 4, SEQ:T],
                                     start=True, stop=True)
                        done(ins, ("qp",))

                    if m == Z_GV + 1:
                        for n in range(3):
                            bk = begin(pe, L, ("vtok", n))
                            for i in range(2 if n < 2 else 1):
                                t = 2 * n + i
                                r = rows_of(t)
                                for j in range(2):
                                    after(pe, L, ("z", Z_GV + j, 1))
                                    ins = tr(bk[:r, i * 256 + j * P:i * 256 + (j + 1) * P], gv[:, j, t * P:t * P + r],
                                             ident)
                            done(ins, ("vtok", n))
                pe.wait_ge(S["kd_ready"], L + 1)
                bk = begin(pe, L, ("ktok", 0))
                for t in range(4):
                    ins = tr(bk[:, t * P:(t + 1) * P], kd[:, t * P:(t + 1) * P], ident)
                done(ins, ("ktok", 0))
                bk = begin(pe, L, ("ktok", 1))
                done(tr(bk[:NS, 0:P], kd[:, SEQ:T], ident), ("ktok", 1))
                after(pe, L, ("ktok", 0))
                after(pe, L, ("ktok", 1))

                def state_products(t):
                    r = rows_of(t)
                    bk = begin(pe, L, ("delta", t))
                    for h in range(GH):
                        pe.wait_ge(S["gmsk_ready"], 4 * TT * L + 4 * t + h + 1)
                        ins = mm(bk[32 * h:32 * h + 32, :], ktok[:r, t, 32 * h:32 * h + 32], gmsk[h][:r, :],
                                 start=True, stop=True)
                        if h < 3:
                            ins.then_inc(S["gmsk_used"], 1)
                    done(ins, ("delta", t))

                def between_chunks(g):
                    pe.wait_ge(S["qbd_ready"], L + 1)
                    bk = begin(pe, L, ("inter", g))
                    n, cs = (16, range(16 * g, 16 * g + 16)) if g < 2 else (NQ, range(NCH, NCH + NB))
                    after(pe, L, ("delta", min(2 * g + 1, TT - 1)))
                    for i, c in enumerate(cs):
                        t0 = c * CH if g < 2 else SEQ + i * NQ
                        s = st[:, c, :] if g < 2 else st[:, c + 1, :]
                        width = 256 if g < 2 else NS
                        for hh in range(2):
                            out = bk[64 * hh:64 * hh + 64, 0:2 * width].rearrange("p (j n) -> p j n", j=2)
                            ins = mm(out[:, :, i * n:(i + 1) * n], s, qbd[:, hh:GH:2, t0:t0 + n],
                                     start=True, stop=True)
                    done(ins, ("inter", g))
                def offset_sums(d):
                    pe.wait_ge(S["w_ready"], CH * L + d + 1)
                    for j in range(2):
                        bk = begin(pe, L, ("dp", d, j))
                        n = NCH * (CH - d)
                        done(mm(bk[:, 0:n], cst[:, C_BM + j * P:C_BM + (j + 1) * P], gw[:, d % 2, 0:n],
                                start=True, stop=True), ("dp", d, j))
                    if d < NQ:
                        bk = begin(pe, L, ("ds", d))
                        n = NB * (NQ - d)
                        for j in range(2):
                            ins = mm(bk[:, j * NS:j * NS + n], cst[:, C_BM + j * P:C_BM + (j + 1) * P],
                                     gw[:, d % 2, SEQ:SEQ + n], start=True, stop=True)
                        done(ins, ("ds", d))

                def gla_norm_sums():
                    pe.wait_ge(S["gsq"], L + 1)
                    for j in range(2):
                        for h, cols in enumerate(halves):
                            bk = begin(pe, L, ("gnorm", j, h))
                            done(mm(bk[:, 0:HALF], blk64, gtmp[:, j, cols], start=True, stop=True), ("gnorm", j, h))


                def sample_scores(p):
                    pe.wait_ge(page_in[p % 2], 16 * 2 * NPAGE * (2 * L + p // 2 + 1))
                    for k in range(3):
                        bk = begin(pe, L, ("ss", p, k))
                        for b2 in range(2):
                            b, out = 2 * p + b2, slice(64 * b2, 64 * b2 + 64)
                            n = 512 if k < 2 else NS
                            if k < 2:
                                four = pg[p % 2][:, b2, 4 * k:4 * k + 4, :]
                                c1, c2 = four[:, :, CKVT], four[0:32, :, KPET]
                            else:
                                c1, c2 = ckvT[:, SEQ:T], kpeT[0:32, SEQ:T]
                            mm(bk[out, 0:n], qas[:, b, :], c1, start=True, stop=False)
                            ins = mm(bk[out, 0:n], qp[0:32, b, :], c2, start=False, stop=k < 2)
                            if k == 2:
                                ins = mm(bk[out, 0:n], idb[:, 64 * b2:64 * b2 + 64],
                                         mask[:, M_SAMPLE + p * NS:M_SAMPLE + (p + 1) * NS], start=False, stop=True)
                        done(ins, ("ss", p, k))

                def sample_values(p):
                    pe.wait_ge(S["s_prob"], 4 * L + p + 1)
                    for k in range(3):
                        bk = begin(pe, L, ("sp", p, k))
                        if k < 2:
                            for j in range(4):
                                at = (4 * k + j) * P
                                ins = tr(bk[:, j * P:(j + 1) * P], sprob[:, at:at + P], ident)
                        else:
                            ins = tr(bk[:NS, 0:P], sprob[:, 1024:1088], ident)
                        done(ins, ("sp", p, k))
                    for k in range(3):
                        after(pe, L, ("sp", p, k))
                    bk = begin(pe, L, ("sv", p))
                    for b2 in range(2):
                        cols = slice(64 * b2, 64 * b2 + 64)
                        for j in range(NPAGE):
                            mm(bk[:, cols], pg[p % 2][:, b2, j, CKV], spT[:, j, cols], start=j == 0, stop=False)
                        ins = mm(bk[:, cols], ctok[:NS, 4, :], spT[:NS, 8, cols], start=False, stop=True)
                    done(ins, ("sv", p))

                pe.wait_ge(S["kperep"], L + 1)
                for hd in range(HEADS):
                    after(pe, L, ("qa", hd, 0))
                    after(pe, L, ("qa", hd, 1))
                after(pe, L, ("ctok", 0))
                after(pe, L, ("ctok", 1))
                after(pe, L, ("qp",))
                for s in range(ATT_STEPS):
                    for key in attention_order(s):
                        kind, hd = key[0], key[1]
                        bk = begin(pe, L, key)
                        if kind == "s":
                            i = key[2]
                            n, q, g = (i + 1) * P, slice(i * P, (i + 1) * P), slice(32 * (hd % 4), 32 * (hd % 4) + 32)
                            mm(bk[:, 0:n], qa[:, hd, q], ckvT[:, 0:n], start=True, stop=False)
                            mm(bk[:, 0:n], qpe[g, hd // 4, q], kpeT[g, 0:n], start=False, stop=False)
                            ins = mm(bk[:, i * P:n], idb, mask[:, M_CAUSAL:M_CAUSAL + P], start=False, stop=True)
                        elif kind == "pt":
                            i = key[2]
                            pe.wait_ge(S["prob_ready"], 4 * HEADS * L + 4 * hd + i + 1)
                            for j in range(i + 1):
                                ins = tr(bk[:, j * P:(j + 1) * P], prob[:, (4 * hd + i) % 2, j * P:(j + 1) * P], ident)
                        else:
                            for i in range(4):
                                after(pe, L, ("pt", hd, i))
                            for j in range(4):
                                ins = mm(bk[:, j * P:SEQ], ctok[:, j, :], pT[:, hd % 2, j, j * P:SEQ],
                                         start=j == 0, stop=j == 3, skip_group_check=True)
                        done(ins, key)
                    if s < TT:
                        state_products(s)
                    if s == TT:
                        for g in range(3):
                            between_chunks(g)
                    if s == SAMPLE_STEP:
                        sample_scores(0)
                    if s == SAMPLE_STEP + 3:
                        sample_values(0)
                    if s in DP_STEPS:
                        offset_sums(DP_STEPS.index(s))
                    if s == GN_STEP:
                        gla_norm_sums()
                for kind, p in SAMPLE_ORDER:
                    (sample_scores if kind == "scores" else sample_values)(p)
                pe.wait_ge(S["uv_in"], 16 * (L + 1))
                for jj in range(4):
                    bk = begin(pe, L, ("uv", jj))
                    for hh in range(2):
                        hd = 2 * jj + hh
                        after(pe, L, ("pv", hd))
                        ins = mm(bk[64 * hh:64 * hh + 64, :], uv[:, hd * VH:(hd + 1) * VH], qa[:, hd, :],
                                 start=True, stop=True)
                    done(ins, ("uv", jj))
                for p in range(4):
                    after(pe, L, ("sv", p))
                bk = begin(pe, L, ("uvs",))
                for hd in range(HEADS):
                    ins = mm(bk[64 * (hd % 2):64 * (hd % 2) + 64, NS * (hd // 2):NS * (hd // 2 + 1)],
                             uv[:, hd * VH:(hd + 1) * VH], qas[:, :, NQ * hd:NQ * (hd + 1)], start=True, stop=True)
                done(ins, ("uvs",))
                for g, (k0, k1) in enumerate(((0, 2), (2, 6), (6, 8))):
                    pe.wait_ge(S["osq_ready"], 8 * L + k1)
                    for h, cols in enumerate(halves):
                        bk = begin(pe, L, ("osum", g, h))
                        for k in range(k0, k1):
                            ins = mm(bk[:, 0:HALF], ones, osq[:, k, cols], start=k == k0, stop=k == k1 - 1)
                        done(ins, ("osum", g, h))
                for n in range(2):
                    pe.wait_ge(wout_in[n], 16 * (L + 1))
                    for t in range(TT):
                        r = rows_of(t)
                        bk = begin(pe, L, ("wo", n, t))
                        for k in range(8):
                            if n == 0 and t == 0:
                                pe.wait_ge(S["merged"], 8 * L + k + 1)
                            ins = mm(bk[:r, :], merged[k][:, t * P:t * P + r], wout[n][:, k, :],
                                     start=k == 0, stop=k == 7)
                        done(ins, ("wo", n, t))

                transpose_rows(L, "hm", 2 * L + 1, (0, 1))
                pe.wait_ge(S["router_in"], 32 * (L + 1))
                logits = begin(pe, L, ("logits",))
                for t in range(TT):
                    r = rows_of(t)
                    after(pe, L, ("hm", t, 0))
                    after(pe, L, ("hm", t, 1))
                    for k in range(KT):
                        ins = mm(logits[:r, 36 * t:36 * t + 36], hT[:, k, t * P:t * P + r], wrt[:, 36 * k:36 * k + 36],
                                 start=k == 0, stop=k == KT - 1)
                    if t + 2 < TT:
                        transpose_rows(L, "hm", 2 * L + 1, (t + 2,))
                done(ins, ("logits",))
                pe.wait_ge(S["sel_ready"], L + 1)
                bk = begin(pe, L, ("rank",))
                for at, weights in ((0, tri), (TT * EXPERTS, ones)):
                    mm(bk[:, at:at + 128], weights, r_any[:, 0:4, :], start=True, stop=True)
                    ins = mm(bk[:, at + 128:at + 160], weights[:NS, :], r_any[:NS, 4, :], start=True, stop=True)
                done(ins, ("rank",))
                bk = begin(pe, L, ("table",))
                for n in range(2 * TT):
                    r = rows_of(n // 2)
                    pe.wait_ge(S["pos_ready"], 2 * TT * L + n + 1)
                    ins = mm(bk[:, 0:TABLE], r_lo1[:r, n, :], r_hi1[:r, n, :], start=n == 0, stop=n == 2 * TT - 1)
                done(ins, ("table",))
                after(pe, L, ("table",))

                pe.wait_ge(S["route_ready"], L + 1)

                def rows_transpose(n, half):
                    if half == 0:
                        pe.wait_ge(S["gathered"], n * 16)
                    for k in range(4):
                        at = (4 * half + k) * P
                        ins = tr(bank[half][:, k * P:(k + 1) * P], xg[:, at:at + P], ident)
                    if half == 1:
                        ins.then_inc(S["xg_used"], 1)

                before = pe.value_load(blocks[0:1, 66:67], min_val=0, max_val=DEPTH * MAXBLK)
                rows_transpose(before + L + 1, 0)
                rows_transpose(before + L + 1, 1)
                with pe.Fori(0, EXPERTS // RING) as g:
                    for s in range(RING):
                        count = pe.value_load(blocks[0:1, bass.ds(g * RING + s, 1)], min_val=1, max_val=TT)
                        ever = pe.value_load(blocks[0:1, bass.ds(g * RING + (66 + s), 1)], min_val=0,
                                             max_val=DEPTH * MAXBLK)
                        with pe.Fori(0, count) as c:
                            pe.wait_ge(wgu_in[s], (g + (EXPERTS // RING * L + 1)) * 32)
                            pe.wait_ge(S["xt_act"], ever + c + L + 1)
                            pe.wait_ge(S["xt_vec"], ever + c + L + 1)
                            for half, signal in ((0, "gate_done"), (1, "gu_done")):
                                for k in range(KT):
                                    ins = mm(bank[2 + half][:, 0:DE], xT[:, k, :],
                                             wgu[s][:, k, half * DE:(half + 1) * DE], start=k == 0, stop=k == KT - 1)
                                ins.then_inc(S[signal], 1)
                            rows_transpose(ever + c + L + 2, 0)
                            pe.wait_ge(S["act_ready"], ever + c + 1)
                            for k in range(2):
                                ins = tr(bank[4][:, k * P:(k + 1) * P], act2[:, k * P:(k + 1) * P], ident)
                            ins.then_inc(S["at_done"], 1)
                            rows_transpose(ever + c + L + 2, 1)
                            pe.wait_ge(S["actt_ready"], ever + c + 1)
                            pe.wait_ge(S["y_act"], ever + c + L + 1)
                            pe.wait_ge(S["y_vec"], ever + c + L + 1)
                            pe.wait_ge(wdn_in[s], (g + (EXPERTS // RING * L + 1)) * 16)
                            for n in range(2):
                                for k in range(2):
                                    ins = mm(bank[5 + n][:, :], actT[:, k, :], wdn[s][:, k, 512 * n:512 * n + 512],
                                             start=k == 0, stop=k == 1)
                            ins.then_inc(S["down_done"], 1)



_INS = ["x_prompt", "x_sample", "cst", "msk", "vecs", "norm1_g", "norm2_g", "final_norm_g", "win", "wq", "ukT", "w_uv",
        "wlru", "gla_wa2", "wrt", "rbias", "w_out", "w_gate", "w_up", "w_down",
        "cache", "page_table", "state_gla"]
_OUTS = {
    "y_prompt": (SEQ, D), "y_sample": (NS, D), "ckv": (DEPTH, P, T), "kpe": (DEPTH, ROPE, T),
    "conv": (DEPTH, P, 2, 27), "lru": (DEPTH, P, 2, 9), "gla_p": (DEPTH, P, GDV), "gla_s": (DEPTH, P, NB, GDV),
}


def lay_out(i):
    f = {k: np.asarray(v) for k, v in i.items()}
    cst, msk = constants()
    d = {k: f[k] for k in ("norm1_g", "norm2_g", "final_norm_g", "w_uv", "gla_wa2", "w_out", "w_gate", "w_up",
                           "w_down")}
    d["w_uv"] = d["w_uv"].reshape(DEPTH, P, HEADS * VH)
    d["x_prompt"] = f["x_prompt"].reshape(SEQ, D)
    d["x_sample"] = f["x_sample"].reshape(NS, D)
    d["cst"], d["msk"] = cst, msk

    def cols(v):
        return np.moveaxis(v.reshape(DEPTH, -1, P), 1, 2)

    d["vecs"] = np.concatenate([
        cols(f["conv_w"]), cols(f["conv_b"]), cols(f["lru_ba"]), cols(f["lru_bi"]), cols(f["lru_lambda"]),
        cols(f["q_norm_g"]), cols(f["kv_norm_g"]), cols(f["gla_ba"]),
        cols(np.tile(f["gla_norm_g"], (1, 2))), cols(f["out_norm_g"]),
        cols(f["state_conv"].reshape(DEPTH, NB, 3, 2, P).transpose(0, 3, 1, 2, 4)),
        cols(f["state_lru"].reshape(DEPTH, NB, 2, P).transpose(0, 2, 1, 3)),
    ], axis=2)
    w = f["w_in"]
    pad = np.zeros((DEPTH, D, P - 2 * ROPE - 16), np.float32)
    kpe = w[..., K_PE:K_PE + ROPE]
    w = np.concatenate([
        w[..., X_LRU:C_Q + 256], w[..., C_KV:C_KV + P],
        kpe, kpe[..., 16:], kpe[..., :16], w[..., G_A:G_A + 16], pad,
        w[..., G_Q:G_V + 256], w[..., G_O:G_O + 256]], axis=2)
    d["win"] = w.reshape(DEPTH, KT, P, ZT, P).transpose(0, 3, 2, 1, 4).reshape(DEPTH, ZT, P, KT * P)
    q = f["w_uq"].reshape(DEPTH, 2, P, HEADS, NOPE + ROPE)
    pe = q[..., NOPE:]
    rot = np.concatenate([pe[..., 16:], pe[..., :16]], axis=-1)
    d["wq"] = np.concatenate([v.reshape(DEPTH, 2, P, -1) for v in (q[..., :NOPE], pe, rot)], axis=3) \
        .transpose(0, 2, 1, 3).reshape(DEPTH, P, 2048)
    d["ukT"] = f["w_uk"].transpose(0, 2, 3, 1).reshape(DEPTH, 4, P, P).transpose(0, 2, 1, 3).reshape(DEPTH, P, 512)
    bd = np.zeros((DEPTH, P, 2, 2, P), np.float32)
    for g, name in enumerate(("lru_wa", "lru_wi")):
        for n in range(4):
            r = slice(64 * (n % 2), 64 * (n % 2) + 64)
            bd[:, r, g, n // 2, r] = f[name][:, n]
    d["wlru"] = bd.reshape(DEPTH, P, 512)
    wr = np.concatenate([f["router_wg"], f["router_we"]], axis=2)
    d["wrt"] = wr.reshape(DEPTH, KT, P, 36).transpose(0, 2, 1, 3).reshape(DEPTH, P, KT * 36)
    d["rbias"] = np.concatenate([f["router_bg"], f["router_be"]], axis=1)
    cache = np.zeros(f["cache_ckv"].shape[:3] + (3 * P,), np.float32)
    cache[..., 0:P] = f["cache_ckv"]
    cache[..., P:2 * P] = f["cache_ckv"].transpose(0, 1, 3, 2)
    cache[:, :, 0:ROPE, 2 * P:] = f["cache_kpe"].transpose(0, 1, 3, 2)
    d["cache"] = cache
    d["page_table"] = f["page_table"].reshape(1, NB * NPAGE)
    d["state_gla"] = f["state_gla"].transpose(0, 2, 3, 1, 4).reshape(DEPTH, P, NB, GDV)
    return {k: np.ascontiguousarray(d[k]) for k in _INS}


def hand_back(r):
    y, ckv, kpe = r["y_prompt"].reshape(1, SEQ, D), r["ckv"].transpose(0, 2, 1), r["kpe"].transpose(0, 2, 1)
    conv = r["conv"].transpose(0, 3, 2, 1).reshape(DEPTH, 27, 256)
    lru = r["lru"].transpose(0, 3, 2, 1).reshape(DEPTH, 9, 256)
    return (
        y, r["y_sample"].reshape(NB, NQ, D),
        ckv[:, None, :SEQ], kpe[:, None, :SEQ],
        ckv[:, SEQ:].reshape(DEPTH, NB, NQ, P), kpe[:, SEQ:].reshape(DEPTH, NB, NQ, ROPE),
        conv[:, None, :3], conv[:, 3:].reshape(DEPTH, NB, 3, 256),
        lru[:, None, 0], lru[:, 1:],
        r["gla_p"].reshape(DEPTH, 1, GH, GDK, GDV),
        r["gla_s"].reshape(DEPTH, GH, GDK, NB, GDV).transpose(0, 3, 1, 2, 4),
    )


def kernel(**inputs):
    import concourse.bacc as bacc
    from concourse.bass_utils import run_bass_kernel_spmd

    nc = bacc.Bacc("TRN2", target_bir_lowering=False, num_devices=1)
    arrays = lay_out(inputs)
    a = {n: nc.dram_tensor(f"in_{n}", v.shape, mybir.dt.from_np(v.dtype), kind="ExternalInput").ap()
         for n, v in arrays.items()}
    o = {n: nc.dram_tensor(f"out_{n}", s, F32, kind="ExternalOutput").ap() for n, s in _OUTS.items()}
    hybrid_step(nc, a, o)
    r = run_bass_kernel_spmd(nc, [{f"in_{n}": v for n, v in arrays.items()}], core_ids=[0])
    return hand_back({n: r.results[0][f"out_{n}"] for n in _OUTS})
```
